# Optimizing a Trainium2 kernel written in Bass

```python
import jax, jax.numpy as jnp
from jax import lax
import numpy as np

D_MODEL = 1024
BATCH = 1
SEQ = 256
DEPTH = 1

GRID_W = 64
CTX_LEN = 256
N_HEADS = 8
N_KV_HEADS = 2
HEAD_DIM = 128
ROPE_THETA = 10000.0
Q_BLOCK = 128
CONV_DIM = 512
CONV_WIDTH = 31
FFN_DIM = 2816
FFN_CONV_WIDTH = 3
EPS = 1e-6
Q_DIM = N_HEADS * HEAD_DIM
KV_DIM = N_KV_HEADS * HEAD_DIM
IN_DIM = Q_DIM + 2 * KV_DIM + 2 * CONV_DIM + 2 * D_MODEL
SPLITS = (Q_DIM, Q_DIM + KV_DIM, Q_DIM + 2 * KV_DIM, Q_DIM + 2 * KV_DIM + 2 * CONV_DIM)


def rms_norm(x, g):
    xf = x.astype(jnp.float32)
    y = xf * lax.rsqrt(jnp.mean(xf * xf, axis=-1, keepdims=True) + EPS)
    return (y * g.astype(jnp.float32)).astype(x.dtype)

def layer_norm(x, g, b):
    xf = x.astype(jnp.float32)
    mu = jnp.mean(xf, axis=-1, keepdims=True)
    var = jnp.mean(jnp.square(xf - mu), axis=-1, keepdims=True)
    y = (xf - mu) * lax.rsqrt(var + EPS)
    return (y * g.astype(jnp.float32) + b.astype(jnp.float32)).astype(x.dtype)

def depthwise_conv(x, w, b):
    C = x.shape[-1]
    y = lax.conv_general_dilated(x, w[:, None, :], window_strides=(1,), padding='SAME',
                                 dimension_numbers=('NWC', 'WIO', 'NWC'), feature_group_count=C)
    return y + b

def modulation(cvec, w_mod, b_mod):
    m = jax.nn.silu(cvec) @ w_mod + b_mod
    return jnp.split(m[:, None, :], 6, axis=-1)

def modulate(h, shift, scale):
    return h * (1.0 + scale) + shift

def axial_rope(rows):
    half = HEAD_DIM // 2
    inv_freq = ROPE_THETA ** (-jnp.arange(0, half, 2, dtype=jnp.float32) / half)
    r = jnp.repeat(jnp.arange(rows, dtype=jnp.float32), GRID_W)
    col = jnp.tile(jnp.arange(GRID_W, dtype=jnp.float32), rows)
    ang = jnp.concatenate([r[:, None] * inv_freq, col[:, None] * inv_freq], axis=-1)
    return jnp.cos(ang), jnp.sin(ang)

def apply_rope(x, cos, sin):
    xf = x.astype(jnp.float32).reshape(x.shape[:-1] + (HEAD_DIM // 2, 2))
    x0, x1 = xf[..., 0], xf[..., 1]
    c = cos[None, :, None, :]
    s = sin[None, :, None, :]
    out = jnp.stack([x0 * c - x1 * s, x0 * s + x1 * c], axis=-1)
    return out.reshape(x.shape).astype(x.dtype)

def head_rms(t, n_heads, g):
    B, L, _ = t.shape
    return rms_norm(t.reshape(B, L, n_heads, HEAD_DIM), g)

def project(h, w_in, q_g, k_g):
    p = h @ w_in
    q, k, v, u, g = jnp.split(p, SPLITS, axis=-1)
    B, L, _ = h.shape
    q = head_rms(q, N_HEADS, q_g)
    k = head_rms(k, N_KV_HEADS, k_g)
    v = v.reshape(B, L, N_KV_HEADS, HEAD_DIM)
    return q, k, v, u, g

def context_kv(hc, w_in, k_g):
    p = hc @ w_in[:, Q_DIM:Q_DIM + 2 * KV_DIM]
    k, v = jnp.split(p, 2, axis=-1)
    B, L, _ = hc.shape
    return head_rms(k, N_KV_HEADS, k_g), v.reshape(B, L, N_KV_HEADS, HEAD_DIM)

def block_attention(q, k, v):
    B, Lq, H, d = q.shape
    G = H // N_KV_HEADS
    nblk = Lq // Q_BLOCK
    qb = q.reshape(B, nblk, Q_BLOCK, N_KV_HEADS, G, d).transpose(1, 0, 2, 3, 4, 5)
    scale = HEAD_DIM ** -0.5

    def one_block(qblk):
        s = jnp.einsum('bqkgd,bskd->bkgqs', qblk, k, preferred_element_type=jnp.float32) * scale
        p = jax.nn.softmax(s, axis=-1)
        return jnp.einsum('bkgqs,bskd->bqkgd', p.astype(v.dtype), v)

    o = lax.map(one_block, qb)
    return o.transpose(1, 0, 2, 3, 4, 5).reshape(B, Lq, H * d)

def conformer_conv(u, dw_w, dw_b, ln_g, ln_b, w_conv_out):
    a, b = jnp.split(u, 2, axis=-1)
    h = a * jax.nn.sigmoid(b)
    h = depthwise_conv(h, dw_w, dw_b)
    h = jax.nn.silu(layer_norm(h, ln_g, ln_b))
    return h @ w_conv_out

def merge_branches(attn, u, g, w_attn_out, dw_w, dw_b, ln_g, ln_b, w_conv_out, w_out):
    y_a = attn @ w_attn_out
    y_b = conformer_conv(u, dw_w, dw_b, ln_g, ln_b, w_conv_out)
    g_a, g_b = jnp.split(g, 2, axis=-1)
    return (jax.nn.sigmoid(g_a) * y_a + jax.nn.sigmoid(g_b) * y_b) @ w_out

def conv_glu_ffn(h, w_up, dw_w, dw_b, w_down):
    up = h @ w_up
    a, b = jnp.split(up, 2, axis=-1)
    a = depthwise_conv(a, dw_w, dw_b)
    return (jax.nn.gelu(a, approximate=True) * b) @ w_down

def first_inputs(seed: int = 0) -> dict:
    key = jax.random.key(seed)
    ks = jax.random.split(key, 24)

    def nrm(k, shape, scale):
        return jax.random.normal(k, shape, jnp.float32) * scale

    return {
        'x': nrm(ks[0], (BATCH, SEQ, D_MODEL), 1.0),
        'c': nrm(ks[1], (BATCH, D_MODEL), 1.0),
        'ctx': nrm(ks[2], (BATCH, CTX_LEN, D_MODEL), 1.0),
        'c_ctx': nrm(ks[3], (D_MODEL,), 1.0),
        'w_mod': nrm(ks[4], (DEPTH, D_MODEL, 6 * D_MODEL), 0.5 * D_MODEL ** -0.5),
        'b_mod': nrm(ks[5], (DEPTH, 6 * D_MODEL), 0.02),
        'norm1_g': 1.0 + nrm(ks[6], (DEPTH, D_MODEL), 0.02),
        'w_in': nrm(ks[7], (DEPTH, D_MODEL, IN_DIM), D_MODEL ** -0.5),
        'q_norm_g': 1.0 + nrm(ks[8], (DEPTH, HEAD_DIM), 0.02),
        'k_norm_g': 1.0 + nrm(ks[9], (DEPTH, HEAD_DIM), 0.02),
        'w_attn_out': nrm(ks[10], (DEPTH, Q_DIM, D_MODEL), Q_DIM ** -0.5),
        'conv_dw_w': nrm(ks[11], (DEPTH, CONV_WIDTH, CONV_DIM), CONV_WIDTH ** -0.5),
        'conv_dw_b': nrm(ks[12], (DEPTH, CONV_DIM), 0.02),
        'conv_ln_g': 1.0 + nrm(ks[13], (DEPTH, CONV_DIM), 0.02),
        'conv_ln_b': nrm(ks[14], (DEPTH, CONV_DIM), 0.02),
        'w_conv_out': nrm(ks[15], (DEPTH, CONV_DIM, D_MODEL), CONV_DIM ** -0.5),
        'w_out': nrm(ks[16], (DEPTH, D_MODEL, D_MODEL), D_MODEL ** -0.5),
        'norm2_g': 1.0 + nrm(ks[17], (DEPTH, D_MODEL), 0.02),
        'w_up': nrm(ks[18], (DEPTH, D_MODEL, 2 * FFN_DIM), D_MODEL ** -0.5),
        'ffn_dw_w': nrm(ks[19], (DEPTH, FFN_CONV_WIDTH, FFN_DIM), FFN_CONV_WIDTH ** -0.5),
        'ffn_dw_b': nrm(ks[20], (DEPTH, FFN_DIM), 0.02),
        'w_down': nrm(ks[21], (DEPTH, FFN_DIM, D_MODEL), FFN_DIM ** -0.5),
        'final_g': 1.0 + nrm(ks[22], (D_MODEL,), 0.02),
    }

def first_block(x, c, ctx, c_ctx, w_mod, b_mod, norm1_g, w_in, q_norm_g, k_norm_g, w_attn_out,
              conv_dw_w, conv_dw_b, conv_ln_g, conv_ln_b, w_conv_out, w_out, norm2_g,
              w_up, ffn_dw_w, ffn_dw_b, w_down, final_g):
    B, L, _ = x.shape
    rows = L // GRID_W
    cos, sin = axial_rope(rows)
    for i in range(DEPTH):
        sh1, sc1, g1, sh2, sc2, g2 = modulation(c, w_mod[i], b_mod[i])
        csh1, csc1, cg1, csh2, csc2, cg2 = modulation(c_ctx[None], w_mod[i], b_mod[i])

        hx = modulate(rms_norm(x, norm1_g[i]), sh1, sc1)
        hc = modulate(rms_norm(ctx, norm1_g[i]), csh1, csc1)
        qx, kx, vx, ux, gx = project(hx, w_in[i], q_norm_g[i], k_norm_g[i])
        qx = apply_rope(qx, cos, sin)
        kx = apply_rope(kx, cos, sin)
        last = i == DEPTH - 1
        if last:
            kc, vc = context_kv(hc, w_in[i], k_norm_g[i])
        else:
            qc, kc, vc, uc, gc = project(hc, w_in[i], q_norm_g[i], k_norm_g[i])
        attn_x = block_attention(qx, jnp.concatenate([kc, kx], axis=1), jnp.concatenate([vc, vx], axis=1))
        mix_x = merge_branches(attn_x, ux, gx, w_attn_out[i], conv_dw_w[i], conv_dw_b[i],
                               conv_ln_g[i], conv_ln_b[i], w_conv_out[i], w_out[i])
        x = x + g1 * mix_x
        hx2 = modulate(rms_norm(x, norm2_g[i]), sh2, sc2)
        x = x + g2 * conv_glu_ffn(hx2, w_up[i], ffn_dw_w[i], ffn_dw_b[i], w_down[i])

        if not last:
            attn_c = block_attention(qc, kc, vc)
            mix_c = merge_branches(attn_c, uc, gc, w_attn_out[i], conv_dw_w[i], conv_dw_b[i],
                                   conv_ln_g[i], conv_ln_b[i], w_conv_out[i], w_out[i])
            ctx = ctx + cg1 * mix_c
            hc2 = modulate(rms_norm(ctx, norm2_g[i]), csh2, csc2)
            ctx = ctx + cg2 * conv_glu_ffn(hc2, w_up[i], ffn_dw_w[i], ffn_dw_b[i], w_down[i])
    return rms_norm(x, final_g)


CHUNK = 64
HEAD_DIM_2 = 64
H_SB = 8
H_CH = 8
W_SB = H_SB * HEAD_DIM_2
W_CH = H_CH * HEAD_DIM_2
MIX_WIDTH = W_SB + W_CH
LOOKBACK = 8
BAND = (LOOKBACK + 1) * CHUNK
REL_CLIP = 128
D_FF = 2816
PLE_DIM = 256
NEG_INF = -1e30


def rms_norm_2(x, g):
    xf = x.astype(jnp.float32)
    y = xf * lax.rsqrt(jnp.mean(xf * xf, axis=-1, keepdims=True) + EPS)
    return (y * g.astype(jnp.float32)).astype(x.dtype)

def swiglu(x, w_gate, w_up, w_down):
    return (jax.nn.silu(x @ w_gate) * (x @ w_up)) @ w_down

def split_heads(t, n_heads):
    b, s, _ = t.shape
    return t.reshape(b, s, n_heads, HEAD_DIM_2).transpose(0, 2, 1, 3)

def merge_heads(t):
    b, h, s, d = t.shape
    return t.transpose(0, 2, 1, 3).reshape(b, s, h * d)

def stick_breaking_attention(q, k, v):
    b, h, s, d = q.shape
    nq = s // Q_BLOCK
    scale = d ** -0.5
    q_blocks = q.reshape(b, h, nq, Q_BLOCK, d).transpose(2, 0, 1, 3, 4)
    starts = jnp.arange(nq, dtype=jnp.int32) * Q_BLOCK
    key_pos = jnp.arange(s, dtype=jnp.int32)

    def one_block(args):
        q_blk, start = args
        z = jnp.einsum('bhqd,bhkd->bhqk', q_blk, k,
                       preferred_element_type=jnp.float32) * scale
        q_pos = start + jnp.arange(Q_BLOCK, dtype=jnp.int32)
        before = key_pos[None, :] < q_pos[:, None]
        log_fail = jnp.where(before, jax.nn.log_sigmoid(-z), 0.0)
        later = lax.cumsum(log_fail, axis=3, reverse=True) - log_fail
        log_a = jax.nn.log_sigmoid(z) + later
        a = jnp.where(before, jnp.exp(jnp.where(before, log_a, 0.0)), 0.0)
        return jnp.einsum('bhqk,bhkd->bhqd', a.astype(v.dtype), v)

    out = lax.map(one_block, (q_blocks, starts))
    return out.transpose(1, 2, 0, 3, 4).reshape(b, h, s, d)

def rel_bias_index():
    i = np.arange(CHUNK)[:, None]
    j = np.arange(BAND)[None, :]
    dist = i + LOOKBACK * CHUNK - j
    return jnp.asarray(np.clip(dist, -REL_CLIP, REL_CLIP) + REL_CLIP, dtype=jnp.int32)

def chunk_band_attention(q, k, v, rel_bias):
    b, h, s, d = q.shape
    nc = s // CHUNK
    scale = d ** -0.5
    qc = q.reshape(b, h, nc, CHUNK, d)

    def band(t):
        tc = t.reshape(b, h, nc, CHUNK, d)
        tp = jnp.pad(tc, ((0, 0), (0, 0), (LOOKBACK, 0), (0, 0), (0, 0)))
        return jnp.concatenate([tp[:, :, w:w + nc] for w in range(LOOKBACK + 1)], axis=3)

    kb, vb = band(k), band(v)
    bias = rel_bias.astype(jnp.float32)[:, rel_bias_index()]
    z = jnp.einsum('bhnqd,bhnkd->bhnqk', qc, kb,
                   preferred_element_type=jnp.float32) * scale + bias[None, :, None]
    slot_chunk = jnp.arange(BAND, dtype=jnp.int32) // CHUNK
    chunk_id = jnp.arange(nc, dtype=jnp.int32)
    valid = (chunk_id[:, None] + slot_chunk[None, :] - LOOKBACK) >= 0
    z = jnp.where(valid[None, None, :, None, :], z, NEG_INF)
    prob = jax.nn.softmax(z, axis=-1)
    o = jnp.einsum('bhnqk,bhnkd->bhnqd', prob.astype(vb.dtype), vb)
    return o.reshape(b, h, s, d)

def second_inputs(seed: int = 0) -> dict:
    key = jax.random.key(seed)
    ks = jax.random.split(key, 24)
    f32 = jnp.float32

    def w(k, shape, fan_in):
        return jax.random.normal(k, shape, f32) * (fan_in ** -0.5)

    def gain(k, n):
        return 1.0 + 0.05 * jax.random.normal(k, (DEPTH, n), f32)

    return {
        "x": jax.random.normal(ks[0], (BATCH, SEQ, D_MODEL), f32),
        "p": jax.random.normal(ks[1], (DEPTH, BATCH, SEQ, PLE_DIM), f32),
        "g_ffn1_pre": gain(ks[2], D_MODEL),
        "g_ffn1_post": gain(ks[3], D_MODEL),
        "w_ffn1_gate": w(ks[4], (DEPTH, D_MODEL, D_FF), D_MODEL),
        "w_ffn1_up": w(ks[5], (DEPTH, D_MODEL, D_FF), D_MODEL),
        "w_ffn1_down": w(ks[6], (DEPTH, D_FF, D_MODEL), D_FF),
        "g_mix_pre": gain(ks[7], D_MODEL),
        "g_mix_post": gain(ks[8], D_MODEL),
        "w_in": w(ks[9], (DEPTH, D_MODEL, 3 * MIX_WIDTH), D_MODEL),
        "g_out_sb": gain(ks[10], W_SB),
        "g_out_ch": gain(ks[11], W_CH),
        "rel_bias": 0.02 * jax.random.normal(ks[12], (DEPTH, H_CH, 2 * REL_CLIP + 1), f32),
        "w_out": w(ks[13], (DEPTH, MIX_WIDTH, D_MODEL), MIX_WIDTH),
        "g_ffn2_pre": gain(ks[14], D_MODEL),
        "g_ffn2_post": gain(ks[15], D_MODEL),
        "w_ffn2_gate": w(ks[16], (DEPTH, D_MODEL, D_FF), D_MODEL),
        "w_ffn2_up": w(ks[17], (DEPTH, D_MODEL, D_FF), D_MODEL),
        "w_ffn2_down": w(ks[18], (DEPTH, D_FF, D_MODEL), D_FF),
        "w_ple_proj": w(ks[19], (DEPTH, PLE_DIM, D_MODEL), PLE_DIM),
        "w_ple_gate": w(ks[20], (DEPTH, D_MODEL, D_MODEL), D_MODEL),
        "g_ple_post": gain(ks[21], D_MODEL),
    }

def second_block(x, p, g_ffn1_pre, g_ffn1_post, w_ffn1_gate, w_ffn1_up, w_ffn1_down,
              g_mix_pre, g_mix_post, w_in, g_out_sb, g_out_ch, rel_bias, w_out,
              g_ffn2_pre, g_ffn2_post, w_ffn2_gate, w_ffn2_up, w_ffn2_down,
              w_ple_proj, w_ple_gate, g_ple_post):
    h = x
    for i in range(DEPTH):
        f = swiglu(rms_norm_2(h, g_ffn1_pre[i]), w_ffn1_gate[i], w_ffn1_up[i], w_ffn1_down[i])
        h = h + 0.5 * rms_norm_2(f, g_ffn1_post[i])

        u = rms_norm_2(h, g_mix_pre[i])
        qkv = u @ w_in[i]
        q_a, k_a, v_a, q_b, k_b, v_b = jnp.split(
            qkv, np.cumsum([W_SB, W_SB, W_SB, W_CH, W_CH])[:5].tolist(), axis=-1)
        o_a = stick_breaking_attention(split_heads(q_a, H_SB), split_heads(k_a, H_SB),
                                       split_heads(v_a, H_SB))
        o_b = chunk_band_attention(split_heads(q_b, H_CH), split_heads(k_b, H_CH),
                                   split_heads(v_b, H_CH), rel_bias[i])
        mixed = jnp.concatenate([rms_norm_2(merge_heads(o_a), g_out_sb[i]),
                                 rms_norm_2(merge_heads(o_b), g_out_ch[i])], axis=-1)
        h = h + rms_norm_2(mixed @ w_out[i], g_mix_post[i])

        f = swiglu(rms_norm_2(h, g_ffn2_pre[i]), w_ffn2_gate[i], w_ffn2_up[i], w_ffn2_down[i])
        h = h + 0.5 * rms_norm_2(f, g_ffn2_post[i])

        e = (p[i] @ w_ple_proj[i]) * jax.nn.sigmoid(h @ w_ple_gate[i])
        h = h + rms_norm_2(e, g_ple_post[i])
    return h


def setup_inputs(seed=0):
    out = dict(first_inputs(seed))
    for name, value in second_inputs(seed + 1).items():
        if name != "x":
            out[name + "_2"] = value
    return out


def reference(
    x, c, ctx, c_ctx, w_mod, b_mod, norm1_g, w_in, q_norm_g, k_norm_g, w_attn_out, conv_dw_w,
    conv_dw_b, conv_ln_g, conv_ln_b, w_conv_out, w_out, norm2_g, w_up, ffn_dw_w, ffn_dw_b,
    w_down, final_g, p_2, g_ffn1_pre_2, g_ffn1_post_2, w_ffn1_gate_2, w_ffn1_up_2,
    w_ffn1_down_2, g_mix_pre_2, g_mix_post_2, w_in_2, g_out_sb_2, g_out_ch_2, rel_bias_2,
    w_out_2, g_ffn2_pre_2, g_ffn2_post_2, w_ffn2_gate_2, w_ffn2_up_2, w_ffn2_down_2,
    w_ple_proj_2, w_ple_gate_2, g_ple_post_2,
):
    x = first_block(
        x, c, ctx, c_ctx, w_mod, b_mod, norm1_g, w_in, q_norm_g, k_norm_g, w_attn_out,
        conv_dw_w, conv_dw_b, conv_ln_g, conv_ln_b, w_conv_out, w_out, norm2_g, w_up, ffn_dw_w,
        ffn_dw_b, w_down, final_g,
    )
    return second_block(
        x, p_2, g_ffn1_pre_2, g_ffn1_post_2, w_ffn1_gate_2, w_ffn1_up_2, w_ffn1_down_2,
        g_mix_pre_2, g_mix_post_2, w_in_2, g_out_sb_2, g_out_ch_2, rel_bias_2, w_out_2,
        g_ffn2_pre_2, g_ffn2_post_2, w_ffn2_gate_2, w_ffn2_up_2, w_ffn2_down_2, w_ple_proj_2,
        w_ple_gate_2, g_ple_post_2,
    )


_drawn_inputs = setup_inputs


def setup_inputs(seed=0):
    import zlib

    import numpy as np

    out = dict(_drawn_inputs(seed))
    spreads = {}
    factors = {'ctx': 3.254,
     'norm1_g': 8.0,
     'q_norm_g': 8.0,
     'k_norm_g': 8.0,
     'conv_dw_b': 6.132,
     'conv_ln_g': 23.648,
     'conv_ln_b': 23.872,
     'norm2_g': 6.739,
     'ffn_dw_b': 8.0,
     'rel_bias_2': 7.431,
     'g_ffn2_pre_2': 2.803,
     'g_ffn2_post_2': 4.09,
     'g_ple_post_2': 3.073}
    for name, (base, spread) in spreads.items():
        noise = np.random.default_rng([zlib.crc32(name.encode()), seed]).standard_normal(out[name].shape)
        drawn = base * np.exp(spread * noise) if base else spread * noise
        out[name] = __import__('jax').numpy.asarray(drawn.astype(out[name].dtype))
    for name, factor in factors.items():
        out[name] = (out[name] * factor).astype(out[name].dtype)
    return out
```

```python
from contextlib import ExitStack

import numpy as np

import concourse.bass as bass
from concourse import mybir

P = 128
D = 1024
KD = D // P
T = 256
TT = T // P
HD = 128
NH = 8
NKV = 2
CD = 512
KC = CD // P
TAPS = 31
KP = 2
PAD = TAPS // 2
F = 2816
KF = F // P
NPAIR = KF // 2
H2 = 8
HD2 = 64
W2 = H2 * HD2
EPS = 1e-6
CH = 2048
NR = 4
SC = 3 * P
GH = 4

F32 = mybir.dt.float32
F32R = mybir.dt.float32r
ALU = mybir.AluOpType
ACT = mybir.ActivationFunctionType
AX = mybir.AxisListType.X

VROWS = [("norm1_g", 8), ("norm2_g", 8), ("g_ffn1_pre_2", 8), ("g_mix_pre_2", 8), ("g_out_sb_2", 4),
         ("g_out_ch_2", 4), ("g_ffn2_pre_2", 8), ("conv_dw_b", 4), ("conv_ln_g", 4), ("conv_ln_b", 4),
         ("b_mod", 48), ("c", 8), ("c_ctx", 8)]
VAT = {}
_n = 0
for _name, _rows in VROWS:
    VAT[_name] = _n
    _n += _rows
assert _n <= P

C_ID, C_TRI, C_NEG, C_AVG, C_COS, C_SIN, C_END = 0, 128, 256, 384, 512, 768, 1024

STAGES = [("mod1", 8, 8), ("q", 4, 4), ("kv", 2, 4), ("u", 4, 4)]
for _h in range(NH):
    if _h:
        STAGES.append((f"pv{_h - 1}", 0, 1))
    STAGES += [(f"g{_h}", 1, 1), (f"mod2_{_h}", 1, 1)]
STAGES += [("pv7", 0, 1), ("convout", 2, 4)]
for _j in range(4):
    STAGES += [(f"attnout{_j}", 1, 1), (f"mod3_{_j}", 1, 1)]
STAGES += [("mod4", 4, 4), ("g1b", 0, 2), ("g2b", 0, 2), ("wout", 4, 4)]
STAGES += [("up0", 22, 22), ("down0", 11, 4), ("up1", 22, 22), ("down1", 11, 4)]
STAGES += [("qa", 2, 2), ("ka", 2, 2), ("va", 2, 2), ("qb", 2, 2), ("stick0", 0, 1), ("kb", 2, 2),
           ("vb", 2, 2), ("stick1", 0, 1), ("band0", 0, 1), ("band1", 0, 1), ("wout2", 4, 4),
           ("up2", 22, 22), ("down2", 11, 4), ("proj", 1, 4), ("gate", 4, 4)]
CHUNK, SPLIT, ACC, MODN = {}, {}, {}, {}
_c = _s = _a = _m = 0
for _name, _nc, _na in STAGES:
    CHUNK[_name], SPLIT[_name], ACC[_name], MODN[_name] = _c, _s, _a, _m
    _c += _nc
    _a += _na
    if _name.startswith("mod"):
        _m += _nc
    else:
        _s += _nc
N_CHUNK, N_SPLIT = _c, _s
TOKEN_STAGES = ("q", "kv", "wout", "down0", "down1", "va", "vb", "wout2", "down2", "proj", "gate")
USED = []
CHUNK_NO = {}
_u = 0
for _name, _nc, _na in STAGES:
    if _name.startswith("mod"):
        continue
    _runs = 2 if _name == "q" else 1
    for _j in range(_nc):
        _per = _nc // _runs
        if _name in TOKEN_STAGES:
            if _j % _per == _per - 1:
                USED.append(("acc_ready", ACC[_name] + _na // _runs * (_j // _per + 1)))
            else:
                _u += 1
                USED.append(("chunk_used", _u))
        else:
            USED.append(("acc_ready", ACC[_name] + _na // _nc * (_j + 1)))
FREED = {}


def _freed(stage, sem, first):
    n = {st[0]: st[2] for st in STAGES}[stage]
    for j in range(n):
        FREED[ACC[stage] + j] = (sem, first + j)


_freed("mod1", "mod_out", 1)
_freed("q", "q_norm", 1)
_freed("kv", "q_norm", 5)
for _j in range(4):
    FREED[ACC["u"] + _j] = ("conv_in", _j // 2 + 1)
for _h in range(NH):
    _freed(f"pv{_h}", "a_lo", _h + 1)
    _freed(f"g{_h}", "g_raw", _h + 1)
    _freed(f"mod2_{_h}", "mod_out", 9 + _h)
_freed("convout", "yb_done", 1)
for _j in range(4):
    _freed(f"attnout{_j}", "ya_done", _j + 1)
    _freed(f"mod3_{_j}", "mod_out", 17 + _j)
_freed("g1b", "g1b_done", 1)
_freed("g2b", "g2b_done", 1)
_freed("mod4", "mod_out", 21)
_freed("wout", "res_y", 1)
_freed("down0", "res_y", 5)
for _n in range(3):
    for _j in range(22):
        FREED[ACC[f"up{_n}"] + _j] = ("h_full", NPAIR * _n + _j // 2 + 1)
for _n, _name in enumerate(("down1", "wout2", "down2")):
    _freed(_name, "f_y", 4 * _n + 1)
for _n, _name in enumerate(("qa", "ka", "qb", "kb")):
    _freed(_name, "qk2", 2 * _n + 1)
_freed("va", "v2", 1)
_freed("vb", "v2", 3)
for _n in range(2):
    _freed(f"stick{_n}", "stick_o", _n + 1)
    _freed(f"band{_n}", "band_o", _n + 1)
_freed("proj", "pw_done", 1)
_freed("gate", "gate_s", 1)
for _name in ("wout", "down0", "down1", "wout2", "down2", "proj", "gate"):
    assert ACC[_name] % 2 == 0, _name

SEMS = """hi_done lo_done chunk_used acc_ready const_in vec_in x_in ctx_in p_in gain_in table_in
pads vec_ps vec_sb silu_c mod_out affine1 affine1c tables
ss_act ss_dve ri_ready xn_ready xt_ps full_dve full_act xhi xlo
q_sq q_ss q_ri q_norm q_rot q_tps q_t
glu_sig conv_in conv_out conv_dve ln_mean ln_c ln_sq ln_var ln_ve ln_r ln_n ln_y ln_hi ln_lo
sc_ready nm_ready p_exp p_scaled pt_ps pt_done a_hi a_lo g_raw g_sig yb_done ya_done mg_full mg_hi mg_lo
diag g1b_done g2b_done res_y res1 res2 cv_act cv_dve glu_act h_full h_hi h_lo
fin_ss fin_ri fin_x f_ss f_ri f_y f_x fgain
qk2 v2 z_ps z_abs z_exp z_ln sp_raw sp_ready arg_ready a_raw a_ready stick_o
b_ps b_z b_exp b_tps b_t band_o mx_ss mx_ri
p_ps p_full pt_hi pt_lo pw_done gate_s e_y out_x dve_chain pool_chain out_done""".split()


def build(nc, a):
    ctx = ExitStack()
    with ctx:
        def sb(name, shape, dt=F32, where=ctx):
            return where.enter_context(nc.sbuf_tensor(name, shape, dt))

        raw = [sb(f"raw{i}", [P, CH]) for i in range(NR)]
        whi = [sb(f"whi{i}", [P, CH], F32R) for i in range(NR)]
        wlo = [sb(f"wlo{i}", [P, CH], F32R) for i in range(NR)]
        X = sb("X", [P, TT, D])
        XN = sb("XN", [P, TT, D])
        FULL = sb("FULL", [P, KD, T])
        xhi = sb("x_hi", [P, KD, T], F32R)
        xlo = sb("x_lo", [P, KD, T], F32R)
        consts = sb("consts", [P, C_END])
        vt = sb("vt", [P, 3, P])
        sct = sb("sct", [P, KD, 2])
        modv = sb("modv", [P, 16, 2])
        mod2 = sb("mod2", [P, 32])
        gainA = sb("gainA", [P, 3, KD])
        small = sb("small", [P, 160])
        ss, ri = small[:, 0:2], small[:, 2:4]
        fss, fri = small[:, 4:6], small[:, 6:8]
        qss, qri = small[:, 8:40], small[:, 40:72]
        nmax, psum_, prec = small[:, 72:74], small[:, 74:76], small[:, 76:78]
        bmax, bsum, brec = small[:, 80:96], small[:, 96:112], small[:, 112:128]
        mss, mri = small[:, 128:132], small[:, 132:136]
        minus_half = small[:, 136:137]

        ph1 = ExitStack()
        QT = sb("QT", [P, NH, T], F32, ph1)
        KT = sb("KT", [P, NKV, 2 * T], F32, ph1)
        V = sb("V", [P, 4, NKV * HD], F32, ph1)
        G = sb("G", [P, 16, T], F32, ph1)
        conv_x = sb("conv_x", [P, KC, T + 2 * PAD], F32, ph1)
        side_hi = sb("side_hi", [P, KD, T], F32R, ph1)
        side_lo = sb("side_lo", [P, KD, T], F32R, ph1)
        cvt_hi = sb("cvt_hi", [P, KC, T], F32R, ph1)
        cvt_lo = sb("cvt_lo", [P, KC, T], F32R, ph1)
        rope = G[:, 8:13, :]
        ph1.close()
        bc = sb("bc", [P, 3, D])
        ph2 = ExitStack()
        hhi = sb("h_hi", [P, KF, T], F32R, ph2)
        hlo = sb("h_lo", [P, KF, T], F32R, ph2)
        phi = sb("p_hi", [P, 2, T], F32R, ph2)
        plo = sb("p_lo", [P, 2, T], F32R, ph2)
        ph2.close()
        ph3 = ExitStack()
        qk2t = [sb(f"qk2_{n}", [P, H2 // 2, T], F32, ph3) for n in ("qa", "ka", "qb", "kb")]
        v2t = [sb(f"v2_{n}", [P, TT, W2], F32, ph3) for n in "ab"]
        toe = sb("toe", [P, H2, SC], F32, ph3)
        MX = sb("MX", [P, TT, D], F32, ph3)
        ph3.close()

        acc = ctx.enter_context(nc.psum_tensor("acc", [P, NR, 512], F32))
        tp = ctx.enter_context(nc.psum_tensor("tp", [P, 4, 512], F32))
        s = {n: ctx.enter_context(nc.semaphore(n)) for n in SEMS}
        landed = [ctx.enter_context(nc.semaphore(f"landed{i}")) for i in range(NR)]

        ident = consts[:, C_ID:C_ID + P]
        negtri = consts[:, C_TRI:C_TRI + P]
        negone = consts[:, C_NEG:C_NEG + P]
        avg = consts[:, C_AVG:C_AVG + P]

        def vec(name, n, off=0):
            at = VAT[name] + off
            return vt[:, 0, at:at + n]

        def accb(i):
            return acc[:, i % NR, :]

        def half(buf, t):
            flat = buf[:, :, :].rearrange("p a b -> p (a b)")
            return flat[:, t * 512:(t + 1) * 512]

        full2 = FULL[:, :, :].rearrange("p a b -> p (a b)")
        xn2 = XN[:, :, :].rearrange("p a b -> p (a b)")

        def cols(w, k, c0, n):
            return w[0:k * P, c0:c0 + n].rearrange("(k p) n -> p k n", p=P)

        def rows(w, r, k):
            return w[r * P:(r + k) * P, :].rearrange("(k p) n -> p k n", p=P)

        def deep(w, r, c0):
            return w[r * P:(r + 4) * P, c0:c0 + 512].rearrange("(k p) n -> p k n", p=P)

        w_in, w_in2, w_mod = a["w_in"], a["w_in_2"], a["w_mod"]
        QKV = NH * HD
        U0, G0 = QKV + 2 * NKV * HD, QKV + 2 * NKV * HD + 2 * CD
        src = {"mod1": [cols(w_mod, 8, 256 * j, 256) for j in range(8)],
               "q": [deep(w_in, 4 * r, 512 * b) for b in range(2) for r in range(2)],
               "kv": [deep(w_in, 4 * r, QKV) for r in range(2)],
               "u": [cols(w_in, 8, U0 + CD * h + 256 * j, 256) for j in range(2) for h in range(2)],
               "convout": [cols(a["w_conv_out"], 4, 512 * j, 512) for j in range(2)],
               "wout": [rows(a["w_out"], 2 * r, 2) for r in range(4)],
               "mod4": [cols(w_mod, 8, 5120 + 256 * j, 256) for j in range(4)],
               "qa": [cols(w_in2, 8, 256 * j, 256) for j in range(2)],
               "ka": [cols(w_in2, 8, W2 + 256 * j, 256) for j in range(2)],
               "va": [deep(w_in2, 4 * r, 2 * W2) for r in range(2)],
               "qb": [cols(w_in2, 8, 3 * W2 + 256 * j, 256) for j in range(2)],
               "kb": [cols(w_in2, 8, 4 * W2 + 256 * j, 256) for j in range(2)],
               "vb": [deep(w_in2, 4 * r, 5 * W2) for r in range(2)],
               "wout2": [rows(a["w_out_2"], 2 * r, 2) for r in range(4)],
               "proj": [rows(a["w_ple_proj_2"], 0, 2)],
               "gate": [rows(a["w_ple_gate_2"], 2 * r, 2) for r in range(4)]}
        for j in range(NH):
            src[f"g{j}"] = [cols(w_in, 8, G0 + 256 * j, 256)]
            src[f"mod2_{j}"] = [cols(w_mod, 8, 2048 + 256 * j, 256)]
        for j in range(4):
            src[f"attnout{j}"] = [cols(a["w_attn_out"], 8, 256 * j, 256)]
            src[f"mod3_{j}"] = [cols(w_mod, 8, 4096 + 256 * j, 256)]
        glu = [((a["w_up"], 0), (a["w_up"], F)), ((a["w_ffn1_gate_2"], 0), (a["w_ffn1_up_2"], 0)),
               ((a["w_ffn2_gate_2"], 0), (a["w_ffn2_up_2"], 0))]
        down = [a["w_down"], a["w_ffn1_down_2"], a["w_ffn2_down_2"]]
        for n in range(3):
            src[f"down{n}"] = [rows(down[n], 2 * r, min(2, KF - 2 * r)) for r in range(11)]
        kind = []
        for name, n, _ in STAGES:
            for j in range(n):
                kind.append(("acc_ready", ACC[name] + j + 1) if name.startswith("mod")
                            else ("lo_done", SPLIT[name] + j + 1))

        block = ctx.enter_context(nc.Block())

        @block.sync
        def _(sp):
            def slot_free(c):
                if c >= NR:
                    sem, value = kind[c - NR]
                    sp.wait_ge(s[sem], value)

            for name, n, _ in STAGES:
                c0 = CHUNK[name]
                if not name.startswith("up"):
                    for j in range(n):
                        slot_free(c0 + j)
                        w = src[name][j]
                        sp.dma_start(raw[(c0 + j) % NR][:, :].rearrange("p (k n) -> p k n", k=w.shape[1]), w)\
                            .then_inc(landed[(c0 + j) % NR], 16)
                    continue
                halves = glu[int(name[2:])]

                def pair_load(j, q):
                    w, first = halves[q % 2]
                    sp.dma_start(raw[(c0 + q) % NR][:, :].rearrange("p (k n) -> p k n", k=8),
                                 w[:, bass.ds(first + 256 * j, 256)].rearrange("(k p) n -> p k n", p=P))\
                        .then_inc(landed[(c0 + q) % NR], 16)

                for q in range(4):
                    slot_free(c0 + q)
                    pair_load(q // 2, q)
                with sp.Fori(1, 5) as m:
                    for q in range(4):
                        sp.wait_ge(s["lo_done"], SPLIT[name] + 4 * m + q - NR + 1)
                        pair_load(2 * m + q // 2, q)
                for q in range(2):
                    slot_free(c0 + 20 + q)
                    pair_load(10, q)

        @block.gpsimd
        def _(pool):
            n_chain = [0]

            def chain(ins):
                n_chain[0] += 1
                ins.then_inc(s["pool_chain"], 1)
                pool.wait_ge(s["pool_chain"], n_chain[0])

            def bcast(v, n):
                return v.rearrange("(a n) -> a n", a=1).broadcast_to([P, n])

            chain(pool.memset(minus_half, -0.5))
            chain(pool.memset(conv_x[:, :, 0:PAD], 0.0))
            chain(pool.memset(conv_x[:, :, T + PAD:T + 2 * PAD], 0.0))
            pool.dma_start(rope[:, 4, 0:HD], bcast(a["k_norm_g"], HD)).then_inc(s["gain_in"], 16)
            pool.dma_start(rope[:, 4, HD:2 * HD], bcast(a["q_norm_g"], HD)).then_inc(s["gain_in"], 16)
            pool.wait_ge(s["gain_in"], 32)
            pool.wait_ge(s["const_in"], 16)
            for w, gat, factor in ((0, HD, 1.0), (2, 0, float(HD) ** 0.5)):
                g_ = rope[:, 4, gat:gat + HD]
                gsw = g_.rearrange("p (i two) -> p i two", two=2)[:, :, ::-1]
                for t in range(TT):
                    pool.tensor_tensor(rope[:, w, t * HD:(t + 1) * HD], g_,
                                       consts[:, C_COS + t * HD:C_COS + (t + 1) * HD], ALU.mult)
                    chain(pool.tensor_tensor(
                        rope[:, w + 1, t * HD:(t + 1) * HD].rearrange("p (i two) -> p i two", two=2), gsw,
                        consts[:, C_SIN + t * HD:C_SIN + (t + 1) * HD].rearrange("p (i two) -> p i two", two=2),
                        ALU.mult))
                if factor != 1.0:
                    chain(pool.tensor_scalar(rope[:, w:w + 2, :], rope[:, w:w + 2, :], factor, None, ALU.mult))
                    pool.tensor_scalar(rope[:, 4, 0:HD], rope[:, 4, 0:HD], factor, None, ALU.mult)\
                        .then_inc(s["tables"], 1)

            def rsqrt(out, in_, width, sem):
                chain(pool.tensor_scalar(out, in_, width * EPS, None, ALU.add))
                n = out.shape[1]
                pool.tensor_tensor(out, out, minus_half.broadcast_to([P, n]), ALU.pow).then_inc(sem, 1)

            def norm(n):
                pool.wait_ge(s["ss_act"], n + 1)
                rsqrt(ri[:, 0:1], ss[:, 0:1], D, s["ri_ready"])
                pool.wait_ge(s["ss_dve"], n + 1)
                rsqrt(ri[:, 1:2], ss[:, 1:2], D, s["ri_ready"])

            norm(0)
            norm(1)
            for u in range(8):
                pool.wait_ge(s["q_ss"], u + 1)
                rsqrt(qri[:, 4 * u:4 * u + 4], qss[:, 4 * u:4 * u + 4], HD, s["q_ri"])

            pool.wait_ge(s["conv_in"], 2)
            conv = XN[:, 1, :].rearrange("p (k n) -> p k n", k=KC)[:, KC - KP:KC, :]
            for i in range(TAPS):
                term = half(XN, i % 2)[:, 0:KP * T].rearrange("p (k n) -> p k n", k=KP)
                for q in range(KP):
                    k = KC - KP + q
                    w = vt[:, 1, KC * i + k:KC * i + k + 1]
                    if i == 0:
                        ins = pool.tensor_scalar(conv[:, q, :], conv_x[:, k, 0:T], w, vec("conv_dw_b", 1, k), ALU.mult,
                                                 ALU.add)
                    else:
                        ins = pool.tensor_scalar(term[:, q, :], conv_x[:, k, i:i + T], w, None, ALU.mult)
                chain(ins)
                if i == TAPS - 1:
                    pool.tensor_tensor(conv, conv, term, ALU.add).then_inc(s["conv_out"], 1)
                elif i:
                    chain(pool.tensor_tensor(conv, conv, term, ALU.add))
            pool.wait_ge(s["ln_ve"], 1)
            rsqrt(half(XN, 1)[:, 0:T], half(XN, 1)[:, 0:T], 1, s["ln_r"])

            gains = [0]

            def load_gain(name, slot):
                if gains[0]:
                    pool.wait_ge(s["fgain"], 16 * gains[0])
                pool.dma_start(bc[:, slot, :], bcast(a[name], D)).then_inc(s["fgain"], 16)
                gains[0] += 1

            pool.wait_ge(s["sc_ready"], TT * NH)
            load_gain("final_g", 2)
            norm(2)
            load_gain("g_ffn1_post_2", 0)
            for t in range(TT):
                pool.wait_ge(s["fin_ss"], t + 1)
                rsqrt(fri[:, t:t + 1], fss[:, t:t + 1], D, s["fin_ri"])
            load_gain("g_mix_post_2", 1)
            norm(3)
            load_gain("g_ffn2_post_2", 2)

            def post(m):
                for t in range(TT):
                    pool.wait_ge(s["f_ss"], TT * m + t + 1)
                    rsqrt(fri[:, t:t + 1], fss[:, t:t + 1], D, s["f_ri"])

            post(0)
            e = a["bias"]
            windows = bass.AP(e.tensor, 0, [[1, P], [e.shape[1], H2], [1, T]])
            pool.wait_ge(s["acc_ready"], ACC["down1"] + 4)
            pool.dma_start(MX[:, :, :].rearrange("p a b -> p (a b)").rearrange("p (h n) -> p h n", h=H2), windows)\
                .then_inc(s["table_in"], 16)
            norm(4)
            pool.dma_start(bc[:, 0, 0:TT * T].rearrange("p (t d) -> p t d", t=TT),
                           a["p_2"].rearrange("(t p) d -> p t d", p=P)).then_inc(s["p_in"], 16)
            sp4 = full2[:, 0:GH * SC].rearrange("p (h n) -> p h n", h=GH)

            def mask(view, sem):
                for blk in (0, 2):
                    v = view[:, :, blk * P:(blk + 1) * P]
                    ins = pool.affine_select(out=v, in_=v, pattern=[[0, GH], [1, P]], compare_op=ALU.is_gt,
                                             fill=0.0, base=0, channel_multiplier=-1)
                ins.then_inc(sem, 1)

            for g in range(2):
                pool.wait_ge(s["sp_raw"], GH * (g + 1))
                mask(sp4, s["sp_ready"])
                pool.wait_ge(s["a_raw"], GH * (g + 1))
                mask(sp4, s["a_ready"])
            for i in range(2):
                for t in range(TT):
                    pool.wait_ge(s["mx_ss"], 2 * i + t + 1)
                    q = 2 * i + t
                    rsqrt(mri[:, q:q + 1], mss[:, q:q + 1], W2, s["mx_ri"])
            post(1)
            norm(5)
            load_gain("g_ple_post_2", 1)
            post(2)
            post(3)

        @block.tensor
        def _(pe):
            def chunk_ready(n):
                pe.wait_ge(s["lo_done"], n + 1)

            def bank_free(i):
                if i >= NR:
                    sem, value = FREED[i - NR]
                    pe.wait_ge(s[sem], value)

            def product(out, xh, xl, wh, wl, x_stationary, start, stop):
                if x_stationary:
                    pe.matmul(out, xh, wh, start=start, stop=False)
                    pe.matmul(out, xh, wl, start=False, stop=False)
                    return pe.matmul(out, xl, wh, start=False, stop=stop)
                pe.matmul(out, wh, xh, start=start, stop=False)
                pe.matmul(out, wh, xl, start=False, stop=False)
                return pe.matmul(out, wl, xh, start=False, stop=stop)

            def feature_tiles(si, i, xh, xl, kt, bank):
                w = [r[si % NR][:, :].rearrange("p (k n) -> p k n", k=kt) for r in (whi, wlo)]
                for q in range(2):
                    at = (2 * bank + q) * P
                    for k in range(kt):
                        mm = product(acc[:, i % NR, q * T:(q + 1) * T], xh[:, k, :], xl[:, k, :],
                                     w[0][:, k, at:at + P], w[1][:, k, at:at + P], False, k == 0, k == kt - 1)
                return mm

            def tiles_stage(si, i, xh=xhi, xl=xlo, kt=KD, banks=1):
                chunk_ready(si)
                for b in range(banks):
                    bank_free(i + b)
                    mm = feature_tiles(si, i + b, xh, xl, kt, b)
                    mm.then_inc(s["acc_ready"], 1)

            def token_stage(si0, i0, chunks, kt, nb, stats, total, k_ready=None):
                n = len(stats) * nb
                for b in range(n):
                    bank_free(i0 + b)
                for c in range(chunks):
                    chunk_ready(si0 + c)
                    if k_ready is not None:
                        k_ready(c)
                    w = [r[(si0 + c) % NR][:, :].rearrange("p (k n) -> p k n", k=kt) for r in (whi, wlo)]
                    for k in range(kt):
                        kk = c * kt + k
                        for x, (xh, xl, t) in enumerate(stats):
                            for b in range(nb):
                                out = accb(i0 + x * nb + b)
                                h = w[0][:, k, b * 512:(b + 1) * 512]
                                l_ = w[1][:, k, b * 512:(b + 1) * 512]
                                mm = product(out, xh[:, kk, t * P:(t + 1) * P], xl[:, kk, t * P:(t + 1) * P], h, l_,
                                             True, kk == 0, kk == total - 1)
                                if kk == total - 1:
                                    mm.then_inc(s["acc_ready"], 1)
                    if c < chunks - 1:
                        mm.then_inc(s["chunk_used"], 1)

            def mod_chunk(c, m, i):
                pe.wait_ge(landed[c % NR], 16 * (c // NR + 1))
                bank_free(i)
                w = raw[c % NR][:, :].rearrange("p (k n) -> p k n", k=8)
                for q in range(2):
                    for k in range(KD):
                        mm = pe.matmul(acc[:, i % NR, 2 * q:2 * q + 2], w[:, k, q * P:(q + 1) * P], sct[:, k, :],
                                       start=(k == 0), stop=(k == KD - 1))
                mm.then_inc(s["acc_ready"], 1)

            def transpose_tokens(n, source, ready="xn_ready", first=None):
                for t in range(TT):
                    pe.wait_ge(s[ready], (TT * n if first is None else first) + t + 1)
                    for k in range(KD):
                        mm = pe.transpose(tp[:, k // 2, (k % 2) * T + t * P:(k % 2) * T + (t + 1) * P],
                                          source[:, t, k * P:(k + 1) * P], ident)
                    mm.then_inc(s["xt_ps"], 1)

            def x_ready(n):
                pe.wait_ge(s["xlo"], 2 * n + 2)

            x_tiles = [(xhi, xlo, 0), (xhi, xlo, 1)]

            pe.wait_ge(s["const_in"], 16)
            pe.wait_ge(s["vec_in"], 16 * (len(VROWS) + 3))
            pe.wait_ge(s["pads"], 1)
            for r in range(3):
                mm = pe.transpose(tp[:, 3, r * P:(r + 1) * P], full2[:, r * P:(r + 1) * P], ident)
            mm.then_inc(s["vec_ps"], 1)
            pe.wait_ge(s["vec_sb"], 1)
            transpose_tokens(0, XN)
            pe.wait_ge(s["silu_c"], 1)
            for j in range(8):
                mod_chunk(CHUNK["mod1"] + j, j, ACC["mod1"] + j)
            x_ready(0)
            for b in range(2):
                token_stage(SPLIT["q"] + 2 * b, ACC["q"] + 2 * b, 2, 4, 1, x_tiles, KD)
                if b == 0:
                    transpose_tokens(1, XN)
            def rope_transposes(u):
                heads = 4 if u < 4 else 2
                pe.wait_ge(s["q_rot"], u + 1)
                if u >= 4:
                    pe.wait_ge(s["q_t"], u - 3)
                for h in range(heads):
                    mm = pe.transpose(tp[:, u % 4, h * P:(h + 1) * P], half(FULL, 2)[:, h * P:(h + 1) * P], ident)
                mm.then_inc(s["q_tps"], 1)

            for u in range(2):
                rope_transposes(u)
            x_ready(1)
            token_stage(SPLIT["kv"], ACC["kv"], 2, 4, 1, x_tiles + [(side_hi, side_lo, 0), (side_hi, side_lo, 1)], KD)
            for u in range(2, 4):
                rope_transposes(u)
            for j in range(4):
                tiles_stage(SPLIT["u"] + j, ACC["u"] + j)
                rope_transposes(4 + j)

            def scores(h):
                for t in range(TT):
                    if h == 0:
                        pe.wait_ge(s["q_t"], 8)
                    else:
                        pe.wait_ge(s["p_exp"], TT * (h - 1) + t + 1)
                    pe.matmul(tp[:, t, :], QT[:, h, t * P:(t + 1) * P], KT[:, h // 4, :], start=True, stop=True)\
                        .then_inc(s["sc_ready"], 1)

            def prob_transposes(h):
                for t in range(TT):
                    pe.wait_ge(s["p_scaled"], TT * h + t + 1)
                    if h:
                        pe.wait_ge(s["pt_done"], TT * (h - 1) + t + 1)
                    for k in range(4):
                        mm = pe.transpose(tp[:, 2 + t, k * P:(k + 1) * P], half(FULL, t)[:, k * P:(k + 1) * P], ident)
                    mm.then_inc(s["pt_ps"], 1)

            PT = FULL[:, 4:8, :]

            def values(h):
                i = ACC[f"pv{h}"]
                bank_free(i)
                pe.wait_ge(s["pt_done"], TT * (h + 1))
                for k in range(4):
                    mm = pe.matmul(acc[:, i % NR, 0:T], V[:, k, (h // 4) * HD:(h // 4 + 1) * HD], PT[:, k, :],
                                   start=(k == 0), stop=(k == 3))
                mm.then_inc(s["acc_ready"], 1)

            conv = XN[:, 1, :].rearrange("p (k n) -> p k n", k=KC)
            for h in range(NH):
                scores(h)
                if h:
                    values(h - 1)
                tiles_stage(SPLIT[f"g{h}"], ACC[f"g{h}"])
                mod_chunk(CHUNK[f"mod2_{h}"], h, ACC[f"mod2_{h}"])
                prob_transposes(h)
            pe.wait_ge(s["conv_out"], 1)
            pe.wait_ge(s["conv_dve"], TAPS * (KC - KP))
            pe.wait_ge(s["p_exp"], TT * NH)
            for k in range(KC):
                mm = pe.matmul(tp[:, 0, 0:T], avg, conv[:, k, :], start=(k == 0), stop=(k == KC - 1))
            mm.then_inc(s["ln_mean"], 1)
            values(NH - 1)
            pe.wait_ge(s["ln_sq"], 1)
            sq = QT[:, 0:4, :]
            for k in range(KC):
                mm = pe.matmul(tp[:, 1, 0:T], avg, sq[:, k, :], start=(k == 0), stop=(k == KC - 1))
            mm.then_inc(s["ln_var"], 1)
            pe.wait_ge(s["ln_lo"], 1)
            for j in range(2):
                tiles_stage(SPLIT["convout"] + j, ACC["convout"] + 2 * j, cvt_hi, cvt_lo, KC, 2)
            pe.wait_ge(s["a_lo"], NH)
            for j in range(4):
                tiles_stage(SPLIT[f"attnout{j}"], ACC[f"attnout{j}"], side_hi, side_lo)
                mod_chunk(CHUNK[f"mod3_{j}"], j, ACC[f"mod3_{j}"])

            def broadcast(i, n):
                pe.wait_ge(s["diag"], n + 1)
                for b in range(2):
                    bank_free(i + b)
                    pe.matmul(accb(i + b), negone, half(FULL, 2 * n + b), start=True, stop=True)\
                        .then_inc(s["acc_ready"], 1)

            for j in range(4):
                mod_chunk(CHUNK["mod4"] + j, j, ACC["mod4"] + j)
            broadcast(ACC["g1b"], 0)
            broadcast(ACC["g2b"], 1)
            token_stage(SPLIT["wout"], ACC["wout"], 4, 2, 2, x_tiles, KD,
                        lambda c: pe.wait_ge(s["mg_lo"], c + 1))

            def ffn_up(n):
                si, i = SPLIT[f"up{n}"], ACC[f"up{n}"]

                def chunk(m, q):
                    pe.wait_ge(s["lo_done"], si + 4 * m + q + 1)
                    if isinstance(m, int) and m == 0:
                        bank_free(i + q)
                    else:
                        pe.wait_ge(s["h_full"], NPAIR * n + 2 * m + q // 2 - 1)
                    w = [r[(si + q) % NR][:, :].rearrange("p (k n) -> p k n", k=KD) for r in (whi, wlo)]
                    for o in range(2):
                        for k in range(KD):
                            mm = product(acc[:, (i + q) % NR, o * T:(o + 1) * T], xhi[:, k, :], xlo[:, k, :],
                                         w[0][:, k, o * P:(o + 1) * P], w[1][:, k, o * P:(o + 1) * P], False,
                                         k == 0, k == KD - 1)
                    mm.then_inc(s["acc_ready"], 1)

                for q in range(4):
                    chunk(0, q)
                with pe.Fori(1, 5) as m:
                    for q in range(4):
                        chunk(m, q)
                for q in range(2):
                    chunk(5, q)

            def ffn_down(n):
                token_stage(SPLIT[f"down{n}"], ACC[f"down{n}"], 11, 2, 2, [(hhi, hlo, 0), (hhi, hlo, 1)], KF,
                            lambda c: pe.wait_ge(s["h_lo"], NPAIR * n + c + 1))

            transpose_tokens(2, XN)
            x_ready(2)
            ffn_up(0)
            ffn_down(0)
            transpose_tokens(3, XN)
            x_ready(3)
            ffn_up(1)
            ffn_down(1)
            transpose_tokens(4, XN)
            x_ready(4)

            def project2(name, j0):
                for j in range(2):
                    tiles_stage(SPLIT[name] + j, ACC[name] + j)

            sp4 = full2[:, 0:GH * SC].rearrange("p (h n) -> p h n", h=GH)

            def head2(which, h):
                return qk2t[which][HD2 * (h % 2):HD2 * (h % 2) + HD2, h // 2, :]

            def stick_scores(g):
                pe.wait_ge(s["qk2"], 4)
                if g:
                    pe.wait_ge(s["a_raw"], GH)
                for h in range(GH):
                    q_, k_ = head2(0, g * GH + h), head2(1, g * GH + h)
                    pe.matmul(tp[:, h, 0:T], k_[:, 0:P], q_[:, :], start=True, stop=True, skip_group_check=True)
                    pe.matmul(tp[:, h, T:SC], k_[:, P:T], q_[:, P:T], start=False, stop=True,
                              skip_group_check=True).then_inc(s["z_ps"], 1)

            def stick_sums(g):
                pe.wait_ge(s["sp_ready"], g + 1)
                for h in range(GH):
                    pe.matmul(tp[:, h, 0:SC], negtri, sp4[:, h, :], start=False, stop=True, skip_group_check=True)
                    pe.matmul(tp[:, h, P:T], negone, sp4[:, h, T:SC], start=False, stop=True,
                              skip_group_check=True).then_inc(s["arg_ready"], 1)

            def weigh_values(i, at, vv, h0):
                bank_free(i)
                for h in range(GH):
                    w, v = at(h), vv[:, :, (h0 + h) * HD2:(h0 + h + 1) * HD2]
                    o = acc[:, i % NR, :]
                    pe.matmul(o[:, h * HD2:(h + 1) * HD2], w[:, 0:P], v[:, 0, :], start=True, stop=True)
                    pe.matmul(o[:, T + h * HD2:T + (h + 1) * HD2], w[:, P:T], v[:, 0, :], start=True, stop=False)
                    mm = pe.matmul(o[:, T + h * HD2:T + (h + 1) * HD2], w[:, T:SC], v[:, 1, :], start=False,
                                   stop=True)
                return mm

            project2("qa", 0)
            project2("ka", 2)
            token_stage(SPLIT["va"], ACC["va"], 2, 4, 1, x_tiles, KD)
            stick_scores(0)
            project2("qb", 4)
            stick_sums(0)
            pe.wait_ge(s["v2"], TT)
            pe.wait_ge(s["a_ready"], 1)
            weigh_values(ACC["stick0"], lambda h: sp4[:, h, :], v2t[0], 0).then_inc(s["acc_ready"], 1)
            stick_scores(1)
            project2("kb", 6)
            stick_sums(1)
            token_stage(SPLIT["vb"], ACC["vb"], 2, 4, 1, x_tiles, KD)
            pe.wait_ge(s["a_ready"], 2)
            weigh_values(ACC["stick1"], lambda h: sp4[:, h, :], v2t[0], GH).then_inc(s["acc_ready"], 1)

            bpt = xn2[:, 0:2 * SC].rearrange("p (b n) -> p b n", b=2)
            bt = xn2[:, 1024:1024 + 2 * SC].rearrange("p (b n) -> p b n", b=2)

            def band_scores(h):
                if h >= 2:
                    pe.wait_ge(s["b_z"], 2 * (h - 1))
                q_, k_ = head2(2, h), head2(3, h)
                pe.matmul(tp[:, h % 2, 0:P], q_[:, 0:P], k_[:, 0:P], start=True, stop=True)
                pe.matmul(tp[:, h % 2, P:SC], q_[:, P:T], k_[:, :], start=True, stop=True).then_inc(s["b_ps"], 1)

            def band_transposes(h):
                pe.wait_ge(s["b_exp"], h + 1)
                if h >= 2:
                    pe.wait_ge(s["b_t"], h - 1)
                for k in range(3):
                    mm = pe.transpose(tp[:, 2 + h % 2, k * P:(k + 1) * P], bpt[:, h % 2, k * P:(k + 1) * P], ident)
                mm.then_inc(s["b_tps"], 1)

            def band_values(h):
                i = ACC[f"band{h // GH}"]
                if h % GH == 0:
                    bank_free(i)
                pe.wait_ge(s["b_t"], h + 1)
                w, v = bt[:, h % 2, :], v2t[1][:, :, h * HD2:(h + 1) * HD2]
                o, at = acc[:, i % NR, :], (h % GH) * HD2
                pe.matmul(o[:, at:at + HD2], w[:, 0:P], v[:, 0, :], start=True, stop=True)
                pe.matmul(o[:, T + at:T + at + HD2], w[:, P:T], v[:, 0, :], start=True, stop=False)
                mm = pe.matmul(o[:, T + at:T + at + HD2], w[:, T:SC], v[:, 1, :], start=False, stop=True)
                if h % GH == GH - 1:
                    mm.then_inc(s["acc_ready"], 1)

            pe.wait_ge(s["qk2"], 8)
            pe.wait_ge(s["a_raw"], 2 * GH)
            band_scores(0)
            pe.wait_ge(s["v2"], 2 * TT)
            for h in range(H2):
                if h + 1 < H2:
                    band_scores(h + 1)
                if h:
                    band_values(h - 1)
                band_transposes(h)
            band_values(H2 - 1)

            transpose_tokens(5, MX)
            x_ready(5)
            token_stage(SPLIT["wout2"], ACC["wout2"], 4, 2, 2, x_tiles, KD)
            transpose_tokens(6, XN)
            x_ready(6)
            ffn_up(2)
            pe.wait_ge(s["p_in"], 16)
            for t in range(TT):
                for k in range(2):
                    mm = pe.transpose(tp[:, 0, k * T + t * P:k * T + (t + 1) * P],
                                      bc[:, 0, t * T + k * P:t * T + (k + 1) * P], ident)
            mm.then_inc(s["p_ps"], 1)
            ffn_down(2)
            pe.wait_ge(s["pt_lo"], 1)
            token_stage(SPLIT["proj"], ACC["proj"], 1, 2, 2, [(phi, plo, 0), (phi, plo, 1)], 2)
            transpose_tokens(7, X, "f_x", 4)
            x_ready(7)
            token_stage(SPLIT["gate"], ACC["gate"], 4, 2, 2, x_tiles, KD)

        @block.scalar
        def _(act):
            n_split = [0]

            def split(si_slot, raw_slot, landed_at, used):
                act.wait_ge(landed[raw_slot], landed_at)
                if used is not None:
                    act.wait_ge(s[used[0]], used[1])
                act.copy(whi[si_slot][:, :], raw[raw_slot][:, :]).then_inc(s["hi_done"], 1)

            chunk_of = [c for c, (what, _) in enumerate(kind) if what == "lo_done"]

            def splits_to(n):
                while n_split[0] < min(n, N_SPLIT):
                    si = n_split[0]
                    c = chunk_of[si]
                    split(si % NR, c % NR, 16 * (c // NR + 1), USED[si - NR] if si >= NR else None)
                    n_split[0] += 1

            def bank_ready(i):
                act.wait_ge(s["acc_ready"], i + 1)

            def norm(n, source):
                act.activation(XN[:, 0, :], source[:, 0, :], ACT.Square, accum_out=ss[:, 0:1])\
                    .then_inc(s["ss_act"], 1)

            def full_and_hi(n, gain, shift, dst):
                act.wait_ge(s["xt_ps"], TT * (n + 1))
                for k in range(4, KD):
                    ins = act.activation(FULL[:, k, :], tp[:, k // 2, (k % 2) * T:(k % 2 + 1) * T], ACT.Identity,
                                         scale=1.0 if gain is None else gain[:, k:k + 1],
                                         bias=0.0 if shift is None else shift(k))
                ins.then_inc(s["full_act"], 1)
                act.wait_ge(s["full_dve"], n + 1)
                act.copy(dst[:, 0:4, :], FULL[:, 0:4, :]).then_inc(s["xhi"], 1)
                act.wait_ge(s["full_act"], n + 1)
                act.copy(dst[:, 4:8, :], FULL[:, 4:8, :]).then_inc(s["xhi"], 1)

            act.dma_start(consts[:, :], a["consts"]).then_inc(s["const_in"], 16)
            act.wait_ge(s["pads"], 1)
            for name, n in VROWS:
                at = VAT[name]
                act.dma_start(full2[at:at + n, 0:P], a[name].rearrange("(k p) -> k p", p=P)).then_inc(s["vec_in"], 16)
            act.dma_start(X[:, :, :], a["x"].rearrange("(t p) d -> p t d", p=P)).then_inc(s["x_in"], 16)
            act.dma_start(full2[0:TAPS * KC, P:2 * P], a["conv_dw_w"].rearrange("i (k p) -> (i k) p", p=P))\
                .then_inc(s["vec_in"], 16)
            act.dma_start(full2[0:3 * KF, 2 * P:3 * P], a["ffn_dw_w"].rearrange("i (k p) -> (i k) p", p=P))\
                .then_inc(s["vec_in"], 16)
            act.dma_start(full2[3 * KF:4 * KF, 2 * P:3 * P], a["ffn_dw_b"].rearrange("(k p) -> k p", p=P))\
                .then_inc(s["vec_in"], 16)
            CTX = G[:, 0:8, :].rearrange("p (t k) n -> p t (k n)", t=TT)
            act.dma_start(CTX, a["ctx"].rearrange("(t p) d -> p t d", p=P)).then_inc(s["ctx_in"], 16)
            act.wait_ge(s["x_in"], 16)
            norm(0, X)
            act.wait_ge(s["vec_sb"], 1)
            act.activation(sct[:, :, 0], vec("c", 8), ACT.Silu)
            act.activation(sct[:, :, 1], vec("c_ctx", 8), ACT.Silu).then_inc(s["silu_c"], 1)
            splits_to(2)
            act.wait_ge(s["affine1"], 1)
            full_and_hi(0, gainA[:, 0, :], lambda k: modv[:, k, 0:1], xhi)
            act.wait_ge(s["ctx_in"], 16)
            norm(1, CTX)
            splits_to(4)
            act.wait_ge(s["affine1c"], 1)
            full_and_hi(1, gainA[:, 1, :], lambda k: modv[:, k, 1:2], side_hi)

            def unit_squares(u, i, heads, v_tile):
                bank_ready(i)
                if u:
                    act.wait_ge(s["q_ss"], u)
                ins = act.activation(half(FULL, 0)[:, 0:heads * HD], accb(i)[:, 0:heads * HD], ACT.Square)
                if v_tile is not None:
                    ins = act.copy(V[:, v_tile, :], accb(i)[:, NKV * HD:2 * NKV * HD])
                ins.then_inc(s["q_sq"], 1)

            def unit_out(u):
                act.wait_ge(s["q_tps"], u + 1)
                if u < 4:
                    b, t = u // 2, u % 2
                    dst = QT[:, 4 * b:4 * b + 4, t * P:(t + 1) * P]
                    ps = tp[:, u % 4, :].rearrange("p (h n) -> p h n", h=4)
                else:
                    t = (u - 4 + 2) % 4
                    dst = KT[:, :, t * P:(t + 1) * P]
                    ps = tp[:, u % 4, 0:NKV * P].rearrange("p (h n) -> p h n", h=NKV)
                act.copy(dst, ps).then_inc(s["q_t"], 1)

            splits_to(SPLIT["q"] + 4)
            act.wait_ge(s["xlo"], 4)
            for u in range(4):
                unit_squares(u, ACC["q"] + u, 4, None)
                splits_to(SPLIT["kv"] + min(u + 1, 2))
            splits_to(SPLIT["u"] + 2)
            for u in range(4, 8):
                unit_squares(u, ACC["kv"] + u - 4, NKV, (u - 4 + 2) % 4)
                splits_to(SPLIT["u"] + min(u - 1, 4))
                unit_out(u - 4)
            for j in range(2):
                bank_ready(ACC["u"] + 2 * j + 1)
                act.activation(half(XN, j), accb(ACC["u"] + 2 * j + 1), ACT.Sigmoid)\
                    .then_inc(s["glu_sig"], 1)
                unit_out(4 + 2 * j)
                splits_to(SPLIT["g0"] + 2 + 2 * j - 1)
                unit_out(5 + 2 * j)

            def pv_hi(h):
                bank_ready(ACC[f"pv{h}"])
                act.copy(side_hi[:, h, :], acc[:, ACC[f"pv{h}"] % NR, 0:T]).then_inc(s["a_hi"], 1)

            PT = FULL[:, 4:8, :]
            for h in range(NH):
                for t in range(TT):
                    act.wait_ge(s["nm_ready"], TT * h + t + 1)
                    if h:
                        act.wait_ge(s["pt_ps"], TT * (h - 1) + t + 1)
                    act.activation(half(FULL, t), tp[:, t, :], ACT.Exp, bias=nmax[:, t:t + 1],
                                   accum_out=psum_[:, t:t + 1]).then_inc(s["p_exp"], 1)
                if h:
                    pv_hi(h - 1)
                splits_to(SPLIT[f"g{h}"] + 3)
                bank_ready(ACC[f"g{h}"])
                act.copy(G[:, 2 * h:2 * h + 2, :], acc[:, ACC[f"g{h}"] % NR, :].rearrange("p (q n) -> p q n", q=2))\
                    .then_inc(s["g_raw"], 1)
                splits_to(SPLIT[f"g{h}"] + 4)
                for t in range(TT):
                    act.wait_ge(s["pt_ps"], TT * h + t + 1)
                    act.copy(PT[:, :, t * P:(t + 1) * P], tp[:, 2 + t, :].rearrange("p (k n) -> p k n", k=4))\
                        .then_inc(s["pt_done"], 1)
            pv_hi(NH - 1)
            sq = QT[:, 0:4, :]
            act.wait_ge(s["ln_c"], 1)
            act.activation(sq, QT[:, 4:8, :], ACT.Square).then_inc(s["ln_sq"], 1)
            splits_to(SPLIT["attnout0"] + 1)
            act.wait_ge(s["ln_n"], 1)
            for k in range(KC):
                ins = act.activation(QT[:, k, :], QT[:, 4 + k, :], ACT.Silu, scale=vec("conv_ln_g", 1, k),
                                     bias=vec("conv_ln_b", 1, k))
            ins.then_inc(s["ln_y"], 1)
            act.wait_ge(s["ln_y"], 1)
            act.copy(cvt_hi[:, :, :], QT[:, 0:4, :]).then_inc(s["ln_hi"], 1)
            for q in (1, 0):
                act.wait_ge(s["g_raw"], NH)
                act.activation(G[:, 8 * q:8 * q + 8, :], G[:, 8 * q:8 * q + 8, :], ACT.Sigmoid)\
                    .then_inc(s["g_sig"], 1)
            for j in range(4):
                splits_to(min(SPLIT[f"attnout{j}"] + 3, SPLIT["wout"]))
                act.wait_ge(s["mg_full"], j + 1)
                act.copy(xhi[:, 2 * j:2 * j + 2, :], FULL[:, 2 * j:2 * j + 2, :]).then_inc(s["mg_hi"], 1)
            splits_to(SPLIT["wout"] + 4)
            for b in range(2):
                bank_ready(ACC["g1b"] + b)
                if b == 0:
                    act.wait_ge(s["ln_lo"], 1)
                act.copy(bc[:, 0, b * 512:(b + 1) * 512], accb(ACC["g1b"] + b)).then_inc(s["g1b_done"], 1)
            for b in range(2):
                bank_ready(ACC["g2b"] + b)
                act.copy(bc[:, 1, b * 512:(b + 1) * 512], accb(ACC["g2b"] + b)).then_inc(s["g2b_done"], 1)
            splits_to(SPLIT["up0"] + 2)
            act.wait_ge(s["res1"], 2)
            norm(2, X)
            splits_to(SPLIT["up0"] + 4)
            full_and_hi(2, gainA[:, 2, :], lambda k: mod2[:, 8 + k:9 + k], xhi)

            def ffn_up(n):
                si, i, c = SPLIT[f"up{n}"], ACC[f"up{n}"], CHUNK[f"up{n}"]
                assert n_split[0] == si + 4
                pairs = NPAIR * n

                def ahead(m, o):
                    split((si + o) % NR, (c + o) % NR, 16 * ((c + o) // NR + 2 + m), ("acc_ready", i + o + 1 + 4 * m))

                def pair(m, q, more):
                    j = 2 * m + q
                    g = i + 2 * q
                    act.wait_ge(s["acc_ready"], g + 4 * m + 1)
                    if n == 0:
                        for o in range(2):
                            w = 2 * j + o
                            act.activation(half(XN, q)[:, o * T:(o + 1) * T], acc[:, g % NR, o * T:(o + 1) * T],
                                           ACT.Identity, scale=vt[:, 2, bass.ds(KF + w, 1)],
                                           bias=vt[:, 2, bass.ds(3 * KF + w, 1)]).then_inc(s["cv_act"], 1)
                        if more:
                            ahead(m, 2 * q)
                        act.wait_ge(s["cv_dve"], 4 * j + 4)
                        act.activation(half(XN, 2 + q), half(XN, q), ACT.Gelu_apprx_tanh).then_inc(s["glu_act"], 1)
                    else:
                        act.activation(half(XN, 2 + q), accb(g), ACT.Silu).then_inc(s["glu_act"], 1)
                        if more:
                            ahead(m, 2 * q)
                    if more:
                        ahead(m, 2 * q + 1)
                    act.wait_ge(s["h_full"], pairs + j + 1)
                    act.copy(hhi[:, bass.ds(2 * j, 2), :],
                             half(FULL, q).rearrange("p (o n) -> p o n", o=2)).then_inc(s["h_hi"], 1)

                with act.Fori(0, 5) as m:
                    for q in range(2):
                        pair(m, q, True)
                n_split[0] = si + 24
                pair(5, 0, False)

            ffn_up(0)
            splits_to(SPLIT["up1"] + 2)
            for t in range(TT):
                act.wait_ge(s["res2"], t + 1)
                act.activation(XN[:, t, :], X[:, t, :], ACT.Square, accum_out=fss[:, t:t + 1]).then_inc(s["fin_ss"], 1)
            act.wait_ge(s["fin_x"], 1)
            norm(3, X)
            splits_to(SPLIT["up1"] + 4)
            full_and_hi(3, vec("g_ffn1_pre_2", 8), None, xhi)
            ffn_up(1)

            def post(m, name):
                for t in range(TT):
                    bank_ready(ACC[name] + 2 * t + 1)
                    b = (ACC[name] + 2 * t) % NR
                    act.activation(XN[:, t, :].rearrange("p (b n) -> p b n", b=2), acc[:, b:b + 2, :], ACT.Square,
                                   accum_out=fss[:, t:t + 1]).then_inc(s["f_ss"], 1)

            splits_to(SPLIT["qa"] + 2)
            post(0, "down1")
            act.wait_ge(s["f_x"], 1)
            norm(4, X)
            splits_to(SPLIT["qa"] + 4)
            full_and_hi(4, vec("g_mix_pre_2", 8), None, xhi)

            def qk_out(w, name):
                for j in range(2):
                    bank_ready(ACC[name] + j)
                    act.activation(qk2t[w][:, 2 * j:2 * j + 2, :],
                                   acc[:, (ACC[name] + j) % NR, :].rearrange("p (q n) -> p q n", q=2),
                                   ACT.Copy, scale=HD2 ** -0.5 if w % 2 == 0 else 1.0).then_inc(s["qk2"], 1)

            ez = xn2[:, 0:GH * SC].rearrange("p (h n) -> p h n", h=GH)
            sp4 = full2[:, 0:GH * SC].rearrange("p (h n) -> p h n", h=GH)

            def stick_ln(g):
                for h in range(GH):
                    act.wait_ge(s["z_ps"], GH * g + h + 1)
                    act.activation(ez[:, h, :], tp[:, h, 0:SC], ACT.Abs).then_inc(s["z_abs"], 1)
                act.wait_ge(s["z_abs"], GH * (g + 1))
                for h in range(GH):
                    act.activation(ez[:, h, :], ez[:, h, :], ACT.Exp, scale=-1.0).then_inc(s["z_exp"], 1)
                act.wait_ge(s["z_exp"], GH * (g + 1))
                for h in range(GH):
                    act.activation(ez[:, h, :], ez[:, h, :], ACT.Ln, bias=1.0).then_inc(s["z_ln"], 1)

            def stick_exp(g):
                for h in range(GH):
                    act.wait_ge(s["arg_ready"], GH * g + h + 1)
                    act.activation(sp4[:, h, :], tp[:, h, 0:SC], ACT.Exp).then_inc(s["a_raw"], 1)

            qk_out(0, "qa")
            splits_to(SPLIT["va"] + 1)
            qk_out(1, "ka")
            splits_to(SPLIT["qb"] + 2)
            for t in range(TT):
                bank_ready(ACC["va"] + t)
                act.copy(v2t[0][:, t, :], accb(ACC["va"] + t)).then_inc(s["v2"], 1)
            stick_ln(0)
            splits_to(SPLIT["kb"] + 1)
            qk_out(2, "qb")
            splits_to(SPLIT["kb"] + 2)
            stick_exp(0)
            splits_to(SPLIT["vb"] + 1)
            stick_ln(1)
            qk_out(3, "kb")
            splits_to(SPLIT["vb"] + 2)
            stick_exp(1)
            for t in range(TT):
                bank_ready(ACC["vb"] + t)
                act.copy(v2t[1][:, t, :], accb(ACC["vb"] + t)).then_inc(s["v2"], 1)
            splits_to(SPLIT["wout2"] + 4)
            bz = full2[:, 0:2 * SC].rearrange("p (b n) -> p b n", b=2)
            bpt = xn2[:, 0:2 * SC].rearrange("p (b n) -> p b n", b=2)
            bt = xn2[:, 1024:1024 + 2 * SC].rearrange("p (b n) -> p b n", b=2)

            def band_exp(h):
                act.wait_ge(s["b_z"], 2 * (h + 1))
                if h >= 2:
                    act.wait_ge(s["b_tps"], h - 1)
                for t, (lo, hi) in enumerate(((0, P), (P, SC))):
                    ins = act.activation(bpt[:, h % 2, lo:hi], bz[:, h % 2, lo:hi], ACT.Exp,
                                         bias=bmax[:, 2 * h + t:2 * h + t + 1],
                                         accum_out=bsum[:, 8 * t + h:8 * t + h + 1])
                ins.then_inc(s["b_exp"], 1)

            band_exp(0)
            for h in range(H2):
                if h + 1 < H2:
                    band_exp(h + 1)
                act.wait_ge(s["b_tps"], h + 1)
                act.copy(bt[:, h % 2, :], tp[:, 2 + h % 2, 0:SC]).then_inc(s["b_t"], 1)
            full_and_hi(5, vec("g_out_sb_2", 8), None, xhi)
            post(1, "wout2")
            splits_to(SPLIT["up2"] + 2)
            act.wait_ge(s["f_x"], 3)
            norm(5, X)
            splits_to(SPLIT["up2"] + 4)
            full_and_hi(6, vec("g_ffn2_pre_2", 8), None, xhi)
            ffn_up(2)
            act.wait_ge(s["p_full"], 1)
            act.copy(phi[:, :, :], FULL[:, 4:6, :]).then_inc(s["pt_hi"], 1)
            splits_to(SPLIT["gate"] + 2)
            post(2, "down2")
            splits_to(SPLIT["gate"] + 4)
            full_and_hi(7, None, None, xhi)
            for t in range(TT):
                for b in range(2):
                    i = ACC["gate"] + 2 * t + b
                    bank_ready(i)
                    act.activation(half(XN, 2 * t + b), accb(i), ACT.Sigmoid).then_inc(s["gate_s"], 1)
            for t in range(TT):
                act.wait_ge(s["e_y"], t + 1)
                act.activation(FULL[:, 4 * t:4 * t + 4, :].rearrange("p k n -> p (k n)"), XN[:, t, :], ACT.Square,
                               accum_out=fss[:, t:t + 1]).then_inc(s["f_ss"], 1)
            for t in range(TT):
                act.wait_ge(s["out_x"], t + 1)
                act.dma_start(a["out"][t * P:(t + 1) * P, :], X[:, t, :]).then_inc(s["out_done"], 16)
            act.wait_ge(s["out_done"], 16 * TT)

        @block.vector
        def _(dve):
            n_split, n_chain = [0], [0]

            def chain(ins):
                n_chain[0] += 1
                ins.then_inc(s["dve_chain"], 1)
                dve.wait_ge(s["dve_chain"], n_chain[0])

            chunk_of = [c for c, (what, _) in enumerate(kind) if what == "lo_done"]

            def split(slot, raw_slot, n):
                dve.wait_ge(s["hi_done"], n)
                dve.tensor_tensor(wlo[slot][:, :], raw[raw_slot][:, :], whi[slot][:, :], ALU.subtract)\
                    .then_inc(s["lo_done"], 1)

            def splits_to(n):
                while n_split[0] < min(n, N_SPLIT):
                    si = n_split[0]
                    split(si % NR, chunk_of[si] % NR, si + 1)
                    n_split[0] += 1

            def bank_ready(i):
                dve.wait_ge(s["acc_ready"], i + 1)

            def norm(n, source):
                dve.tensor_tensor_reduce(XN[:, 1, :], source[:, 1, :], source[:, 1, :], 1.0, 0.0, ALU.mult, ALU.add,
                                         ss[:, 1:2]).then_inc(s["ss_dve"], 1)

            def scale_tokens(n, source):
                for t in range(TT):
                    dve.wait_ge(s["ri_ready"], TT * n + t + 1)
                    dve.tensor_scalar(XN[:, t, :], source[:, t, :], ri[:, t:t + 1], float(D) ** 0.5, ALU.mult,
                                      ALU.mult).then_inc(s["xn_ready"], 1)

            def full_and_lo(n, gain, shift, dh, dl):
                dve.wait_ge(s["xt_ps"], TT * (n + 1))
                for k in range(4):
                    ps = tp[:, k // 2, (k % 2) * T:(k % 2 + 1) * T]
                    if gain is None:
                        ins = dve.tensor_copy(FULL[:, k, :], ps)
                    elif shift is None:
                        ins = dve.tensor_scalar(FULL[:, k, :], ps, gain[:, k:k + 1], None, ALU.mult)
                    else:
                        ins = dve.tensor_scalar(FULL[:, k, :], ps, gain[:, k:k + 1], shift(k), ALU.mult, ALU.add)
                ins.then_inc(s["full_dve"], 1)
                for q in range(2):
                    dve.wait_ge(s["xhi"], 2 * n + q + 1)
                    if q == 0:
                        dve.wait_ge(s["full_dve"], n + 1)
                    dve.tensor_tensor(dl[:, 4 * q:4 * q + 4, :], FULL[:, 4 * q:4 * q + 4, :],
                                      dh[:, 4 * q:4 * q + 4, :], ALU.subtract).then_inc(s["xlo"], 1)

            dve.memset(full2[:, 0:3 * P], 0.0).then_inc(s["pads"], 1)
            dve.wait_ge(s["vec_ps"], 1)
            dve.tensor_copy(vt[:, :, :], tp[:, 3, 0:3 * P].rearrange("p (r n) -> p r n", r=3))\
                .then_inc(s["vec_sb"], 1)
            dve.wait_ge(s["x_in"], 16)
            norm(0, X)
            scale_tokens(0, X)
            for j in range(8):
                i = ACC["mod1"] + j
                bank_ready(i)
                b = vec("b_mod", 2, 2 * j)
                dve.tensor_tensor(modv[:, 2 * j:2 * j + 2, :], accb(i)[:, 0:4].rearrange("p (q c) -> p q c", q=2),
                                  b.rearrange("p (q c) -> p q c", c=1).broadcast_to([P, 2, 2]), ALU.add)\
                    .then_inc(s["mod_out"], 1)
            dve.wait_ge(s["mod_out"], 8)
            for w, sem in ((0, "affine1"), (1, "affine1c")):
                dve.scalar_tensor_tensor(gainA[:, w, :], modv[:, 8:16, w], 1.0, vec("norm1_g", 8), ALU.add, ALU.mult)\
                    .then_inc(s[sem], 1)
            dve.wait_ge(s["affine1"], 1)
            splits_to(1)
            full_and_lo(0, gainA[:, 0, :], lambda k: modv[:, k, 0:1], xhi, xlo)
            splits_to(2)
            CTX = G[:, 0:8, :].rearrange("p (t k) n -> p t (k n)", t=TT)
            dve.wait_ge(s["ctx_in"], 16)
            norm(1, CTX)
            scale_tokens(1, CTX)
            splits_to(4)
            full_and_lo(1, gainA[:, 1, :], lambda k: modv[:, k, 1:2], side_hi, side_lo)

            def unit(u, i, heads, t, kind_):
                w = heads * HD
                sq, qn, t1, t2 = (half(FULL, x)[:, 0:w] for x in (0, 1, 2, 3))

                def by_head(v):
                    return v.rearrange("p (h d) -> p h d", h=heads)

                def table(r):
                    return rope[:, r:r + 1, t * HD:(t + 1) * HD].broadcast_to([P, heads, HD])

                def swapped(v):
                    return v.rearrange("p (h i two) -> p h i two", h=heads, two=2)[:, :, :, ::-1]

                dve.wait_ge(s["q_sq"], u + 1)
                dve.tensor_reduce(qss[:, 4 * u:4 * u + heads], by_head(sq), AX, ALU.add).then_inc(s["q_ss"], 1)
                dve.wait_ge(s["q_ri"], u + 1)
                r = qri[:, 4 * u:4 * u + heads].rearrange("p (h d) -> p h d", d=1).broadcast_to([P, heads, HD])
                dve.tensor_tensor(by_head(qn), by_head(accb(i)[:, 0:w]), r, ALU.mult).then_inc(s["q_norm"], 1)
                dve.wait_ge(s["q_norm"], u + 1)
                if u:
                    dve.wait_ge(s["q_tps"], u)
                if kind_ is None:
                    g_ = rope[:, 4:5, 0:HD].broadcast_to([P, heads, HD])
                    dve.tensor_tensor(by_head(t1), by_head(qn), g_, ALU.mult).then_inc(s["q_rot"], 1)
                    return
                dve.tensor_tensor(by_head(t1), by_head(qn), table(kind_), ALU.mult)
                for h in range(heads):
                    ins = dve.tensor_tensor(
                        t2[:, h * HD:(h + 1) * HD].rearrange("p (i two) -> p i two", two=2),
                        qn[:, h * HD:(h + 1) * HD].rearrange("p (i two) -> p i two", two=2)[:, :, ::-1],
                        rope[:, kind_ + 1, t * HD:(t + 1) * HD].rearrange("p (i two) -> p i two", two=2), ALU.mult)
                chain(ins)
                dve.tensor_tensor(t1, t1, t2, ALU.add).then_inc(s["q_rot"], 1)

            dve.wait_ge(s["tables"], 1)
            chain(dve.memset(qss, 1.0))
            splits_to(SPLIT["q"] + 4)
            for u in range(4):
                unit(u, ACC["q"] + u, 4, u % 2, 0)
                splits_to(SPLIT["kv"] + min(u + 1, 2))
            splits_to(SPLIT["u"] + 2)
            for u in range(4, 8):
                unit(u, ACC["kv"] + u - 4, NKV, u % 2, 2 if u < 6 else None)
                splits_to(SPLIT["u"] + min(u - 1, 4))
            for j in range(2):
                dve.wait_ge(s["glu_sig"], j + 1)
                dve.tensor_tensor(conv_x[:, 2 * j:2 * j + 2, PAD:PAD + T],
                                  accb(ACC["u"] + 2 * j).rearrange("p (q n) -> p q n", q=2),
                                  half(XN, j).rearrange("p (q n) -> p q n", q=2), ALU.mult)\
                    .then_inc(s["conv_in"], 1)
                splits_to(SPLIT["g0"] + 2 + 2 * j - 1)

            def pv_lo(h):
                i = ACC[f"pv{h}"]
                dve.wait_ge(s["a_hi"], h + 1)
                dve.tensor_tensor(side_lo[:, h, :], acc[:, i % NR, 0:T], side_hi[:, h, :], ALU.subtract)\
                    .then_inc(s["a_lo"], 1)

            def mod_out(i, m, row):
                bank_ready(i)
                ps = accb(i)[:, 0:4].rearrange("p (q c) -> p q c", q=2)[:, :, 0]
                dve.tensor_tensor(mod2[:, m:m + 2], ps, vec("b_mod", 2, row), ALU.add).then_inc(s["mod_out"], 1)

            CTAPS = (TAPS + NH - 1) // NH
            KD_ = KC - KP

            def conv_taps(i0, i1):
                for i in range(i0, i1):
                    for k in range(KD_):
                        at = XN[:, 1, k * T:(k + 1) * T]
                        w = vt[:, 1, KC * i + k:KC * i + k + 1]
                        if i == 0:
                            dve.tensor_scalar(at, conv_x[:, k, 0:T], w, vec("conv_dw_b", 1, k), ALU.mult, ALU.add)\
                                .then_inc(s["conv_dve"], 1)
                        else:
                            dve.wait_ge(s["conv_dve"], KD_ * (i - 1) + k + 1)
                            dve.scalar_tensor_tensor(at, conv_x[:, k, i:i + T], w, at, ALU.mult, ALU.add)\
                                .then_inc(s["conv_dve"], 1)

            for h in range(NH):
                for t in range(TT):
                    dve.wait_ge(s["sc_ready"], TT * h + t + 1)
                    dve.tensor_reduce(nmax[:, t:t + 1], tp[:, t, :], AX, ALU.max, negate=True)\
                        .then_inc(s["nm_ready"], 1)
                for t in range(TT):
                    dve.wait_ge(s["p_exp"], TT * h + t + 1)
                    chain(dve.reciprocal(prec[:, t:t + 1], psum_[:, t:t + 1]))
                    dve.tensor_scalar(half(FULL, t), half(FULL, t), prec[:, t:t + 1], None, ALU.mult)\
                        .then_inc(s["p_scaled"], 1)
                if h:
                    pv_lo(h - 1)
                splits_to(SPLIT[f"g{h}"] + 3)
                conv_taps(CTAPS * h, min(TAPS, CTAPS * (h + 1)))
                mod_out(ACC[f"mod2_{h}"], 2 * h, 16 + 2 * h)
                splits_to(SPLIT[f"g{h}"] + 4)
            conv = XN[:, 1, :].rearrange("p (k n) -> p k n", k=KC)
            cent = QT[:, 4:8, :]

            def over_tiles(v):
                return v.rearrange("p (k n) -> p k n", k=1).broadcast_to([P, KC, T])

            dve.wait_ge(s["ln_mean"], 1)
            dve.tensor_tensor(cent, conv, over_tiles(tp[:, 0, 0:T]), ALU.subtract).then_inc(s["ln_c"], 1)
            pv_lo(NH - 1)
            dve.wait_ge(s["ln_var"], 1)
            var = half(XN, 1)[:, 0:T]
            dve.tensor_copy(var, tp[:, 1, 0:T]).then_inc(s["ln_ve"], 1)
            dve.wait_ge(s["ln_r"], 1)
            dve.tensor_tensor(cent, cent, over_tiles(var), ALU.mult).then_inc(s["ln_n"], 1)
            splits_to(SPLIT["attnout0"] + 1)
            dve.wait_ge(s["ln_hi"], 1)
            dve.tensor_tensor(cvt_lo[:, :, :], QT[:, 0:4, :], cvt_hi[:, :, :], ALU.subtract).then_inc(s["ln_lo"], 1)
            dve.wait_ge(s["g_sig"], 1)
            for i in range(4):
                b = ACC["convout"] + i
                bank_ready(b)
                v = G[:, 8 + 2 * i:10 + 2 * i, :]
                dve.tensor_tensor(v, accb(b).rearrange("p (q n) -> p q n", q=2), v, ALU.mult)\
                    .then_inc(s["yb_done"], 1)
            dve.wait_ge(s["g_sig"], 2)
            for j in range(4):
                splits_to(min(SPLIT[f"attnout{j}"] + 3, SPLIT["wout"]))
                b = ACC[f"attnout{j}"]
                bank_ready(b)
                v = G[:, 2 * j:2 * j + 2, :]
                dve.tensor_tensor(v, accb(b).rearrange("p (q n) -> p q n", q=2), v, ALU.mult)\
                    .then_inc(s["ya_done"], 1)
                dve.wait_ge(s["ya_done"], j + 1)
                dve.tensor_tensor(FULL[:, 2 * j:2 * j + 2, :], v, G[:, 8 + 2 * j:10 + 2 * j, :], ALU.add)\
                    .then_inc(s["mg_full"], 1)
                dve.wait_ge(s["mg_hi"], j + 1)
                dve.tensor_tensor(xlo[:, 2 * j:2 * j + 2, :], FULL[:, 2 * j:2 * j + 2, :], xhi[:, 2 * j:2 * j + 2, :],
                                  ALU.subtract).then_inc(s["mg_lo"], 1)
                mod_out(ACC[f"mod3_{j}"], 16 + 2 * j, 32 + 2 * j)

            def diagonal(n, at, sem):
                for k in range(KD):
                    ins = dve.tensor_scalar(full2[:, n * D + k * P:n * D + (k + 1) * P], ident, mod2[:, at + k:at + k + 1], -1.0,
                                            ALU.mult, ALU.mult)
                ins.then_inc(sem, 1)

            for j in range(4):
                mod_out(ACC["mod4"] + j, 24 + 2 * j, 40 + 2 * j)
            dve.wait_ge(s["mod_out"], 24)
            dve.wait_ge(s["mg_lo"], 4)
            diagonal(0, 0, s["diag"])
            diagonal(1, 24, s["diag"])
            chain(dve.scalar_tensor_tensor(gainA[:, 2, :], mod2[:, 16:24], 1.0, vec("norm2_g", 8), ALU.add, ALU.mult))
            splits_to(SPLIT["wout"] + 4)

            def residual(name, gate, first, sem):
                for t in range(TT):
                    for b in range(2):
                        i = ACC[name] + 2 * t + b
                        bank_ready(i)
                        dve.tensor_tensor(XN[:, t, b * 512:(b + 1) * 512], accb(i),
                                          bc[:, gate, b * 512:(b + 1) * 512], ALU.mult).then_inc(s["res_y"], 1)
                    dve.wait_ge(s["res_y"], first + 2 * t + 2)
                    dve.tensor_tensor(X[:, t, :], X[:, t, :], XN[:, t, :], ALU.add).then_inc(sem, 1)

            dve.wait_ge(s["g1b_done"], 2)
            splits_to(SPLIT["up0"] + 2)
            residual("wout", 0, 0, s["res1"])
            dve.wait_ge(s["res1"], 2)
            norm(2, X)
            splits_to(SPLIT["up0"] + 4)
            scale_tokens(2, X)
            full_and_lo(2, gainA[:, 2, :], lambda k: mod2[:, 8 + k:9 + k], xhi, xlo)

            def ffn_up(n):
                si, i, c = SPLIT[f"up{n}"], ACC[f"up{n}"], CHUNK[f"up{n}"]
                assert n_split[0] == si + 4
                pairs = NPAIR * n

                def ahead(m, o):
                    split((si + o) % NR, (c + o) % NR, si + o + 5 + 4 * m)

                def pair(m, q, more):
                    j = 2 * m + q
                    g, u = i + 2 * q, i + 2 * q + 1
                    if n == 0:
                        for tap, (dst, sr) in enumerate((((1, T), (0, T - 1)), ((0, T - 1), (1, T)))):
                            for o in range(2):
                                if tap == 0:
                                    dve.wait_ge(s["cv_act"], 2 * j + 2)
                                else:
                                    dve.wait_ge(s["cv_dve"], 4 * j + o + 1)
                                at = half(XN, q)[:, o * T + dst[0]:o * T + dst[1]]
                                ins = dve.scalar_tensor_tensor(
                                    at, acc[:, g % NR, o * T + sr[0]:o * T + sr[1]],
                                    vt[:, 2, bass.ds(2 * tap * KF + 2 * j + o, 1)], at, ALU.mult, ALU.add)
                                ins.then_inc(s["cv_dve"], 1)
                    if more:
                        ahead(m, 2 * q)
                    dve.wait_ge(s["glu_act"], pairs + j + 1)
                    dve.wait_ge(s["acc_ready"], u + 4 * m + 1)
                    dve.tensor_tensor(half(FULL, q), accb(u), half(XN, 2 + q), ALU.mult).then_inc(s["h_full"], 1)
                    if more:
                        ahead(m, 2 * q + 1)
                    dve.wait_ge(s["h_hi"], pairs + j + 1)
                    dve.tensor_tensor(hlo[:, bass.ds(2 * j, 2), :], half(FULL, q).rearrange("p (o n) -> p o n", o=2),
                                      hhi[:, bass.ds(2 * j, 2), :], ALU.subtract).then_inc(s["h_lo"], 1)

                with dve.Fori(0, 5) as m:
                    for q in range(2):
                        pair(m, q, True)
                n_split[0] = si + 24
                pair(5, 0, False)

            ffn_up(0)
            splits_to(SPLIT["up1"] + 2)
            dve.wait_ge(s["g2b_done"], 2)
            residual("down0", 1, 4, s["res2"])
            dve.wait_ge(s["fgain"], 16)
            for t in range(TT):
                dve.wait_ge(s["fin_ri"], t + 1)
                chain(dve.tensor_scalar(X[:, t, :], X[:, t, :], fri[:, t:t + 1], float(D) ** 0.5, ALU.mult, ALU.mult))
                dve.tensor_tensor(X[:, t, :], X[:, t, :], bc[:, 2, :], ALU.mult).then_inc(s["fin_x"], 1)
            dve.wait_ge(s["fin_x"], 2)
            norm(3, X)
            splits_to(SPLIT["up1"] + 4)
            scale_tokens(3, X)
            full_and_lo(3, vec("g_ffn1_pre_2", 8), None, xhi, xlo)
            ffn_up(1)

            def post(m, name, gain, factor):
                dve.wait_ge(s["fgain"], 16 * (m + 2))
                for t in range(TT):
                    dve.wait_ge(s["f_ri"], TT * m + t + 1)
                    for b in range(2):
                        i = ACC[name] + 2 * t + b
                        dve.scalar_tensor_tensor(XN[:, t, b * 512:(b + 1) * 512], accb(i), fri[:, t:t + 1],
                                                 bc[:, gain, b * 512:(b + 1) * 512], ALU.mult, ALU.mult)\
                            .then_inc(s["f_y"], 1)
                    dve.wait_ge(s["f_y"], 4 * m + 2 * t + 2)
                    dve.scalar_tensor_tensor(X[:, t, :], XN[:, t, :], factor * float(D) ** 0.5, X[:, t, :], ALU.mult,
                                             ALU.add).then_inc(s["f_x"], 1)

            splits_to(SPLIT["qa"] + 2)
            post(0, "down1", 0, 0.5)
            dve.wait_ge(s["f_x"], 2)
            norm(4, X)
            splits_to(SPLIT["qa"] + 4)
            scale_tokens(4, X)
            full_and_lo(4, vec("g_mix_pre_2", 8), None, xhi, xlo)

            dve.wait_ge(s["table_in"], 16)
            tin = MX[:, :, :].rearrange("p a b -> p (a b)").rearrange("p (h n) -> p h n", h=H2)
            chain(dve.memset(tin[0:64, :, 0:64], -1e30))
            for h in range(H2):
                dve.tensor_copy(toe[:, h, 0:P], tin[:, h, P - 1::-1])
                ins = dve.tensor_copy(toe[:, h, P:SC], tin[:, h, ::-1])
            chain(ins)

            ez = xn2[:, 0:GH * SC].rearrange("p (h n) -> p h n", h=GH)
            sp4 = full2[:, 0:GH * SC].rearrange("p (h n) -> p h n", h=GH)

            def stick_softplus(g):
                for h in range(GH):
                    dve.wait_ge(s["z_ln"], GH * g + h + 1)
                    dve.scalar_tensor_tensor(sp4[:, h, :], tp[:, h, 0:SC], 0.0, ez[:, h, :], ALU.max, ALU.add)\
                        .then_inc(s["sp_raw"], 1)

            def heads_out(i, g, base, recips, sem):
                bank_ready(i)
                for t in range(TT):
                    dst = MX[:, t, base + g * T:base + (g + 1) * T]
                    ps = acc[:, i % NR, t * T:(t + 1) * T]
                    if recips is None:
                        ins = dve.tensor_copy(dst, ps)
                    else:
                        r = recips[:, 8 * t + g * GH:8 * t + g * GH + GH].rearrange("p (h d) -> p h d", d=1)
                        ins = dve.tensor_tensor(dst.rearrange("p (h d) -> p h d", h=GH),
                                                ps.rearrange("p (h d) -> p h d", h=GH),
                                                r.broadcast_to([P, GH, HD2]), ALU.mult)
                ins.then_inc(s[sem], 1)
                dve.wait_ge(s[sem], g + 1)

            splits_to(SPLIT["va"] + 1)
            splits_to(SPLIT["qb"] + 2)
            splits_to(SPLIT["kb"] + 1)
            stick_softplus(0)
            splits_to(SPLIT["kb"] + 2)
            heads_out(ACC["stick0"], 0, 0, None, "stick_o")
            splits_to(SPLIT["vb"] + 1)
            stick_softplus(1)
            splits_to(SPLIT["vb"] + 2)
            heads_out(ACC["stick1"], 1, 0, None, "stick_o")
            splits_to(SPLIT["wout2"] + 4)
            bz = full2[:, 0:2 * SC].rearrange("p (b n) -> p b n", b=2)

            def band_bias(h):
                dve.wait_ge(s["b_ps"], h + 1)
                if h >= 2:
                    dve.wait_ge(s["b_exp"], h - 1)
                chain(dve.tensor_tensor(bz[:, h % 2, :], tp[:, h % 2, 0:SC], toe[:, h, :], ALU.add))
                for t, (lo, hi) in enumerate(((0, P), (P, SC))):
                    dve.tensor_reduce(bmax[:, 2 * h + t:2 * h + t + 1], bz[:, h % 2, lo:hi], AX, ALU.max,
                                      negate=True).then_inc(s["b_z"], 1)

            def group_norm(i):
                for t in range(TT):
                    at = MX[:, t, i * W2:(i + 1) * W2]
                    dve.tensor_tensor_reduce(full2[:, 1024:1024 + W2], at, at, 1.0, 0.0, ALU.mult, ALU.add,
                                             mss[:, 2 * i + t:2 * i + t + 1]).then_inc(s["mx_ss"], 1)
                    dve.wait_ge(s["mx_ss"], 2 * i + t + 1)

            for h in range(H2):
                band_bias(h)
                if h % GH == GH - 1:
                    g = h // GH
                    dve.wait_ge(s["b_exp"], h + 1)
                    for t in range(TT):
                        r = slice(8 * t + g * GH, 8 * t + g * GH + GH)
                        ins = dve.reciprocal(brec[:, r], bsum[:, r])
                    chain(ins)
                if h == GH - 1:
                    group_norm(0)
                if h == GH + 1:
                    heads_out(ACC["band0"], 0, W2, brec, "band_o")
            heads_out(ACC["band1"], 1, W2, brec, "band_o")
            group_norm(1)
            for t in range(TT):
                for i in range(2):
                    dve.wait_ge(s["mx_ri"], 2 * i + t + 1)
                    at = MX[:, t, i * W2:(i + 1) * W2]
                    ins = dve.tensor_scalar(at, at, mri[:, 2 * i + t:2 * i + t + 1], float(W2) ** 0.5, ALU.mult,
                                            ALU.mult)
                ins.then_inc(s["xn_ready"], 1)
            full_and_lo(5, vec("g_out_sb_2", 8), None, xhi, xlo)
            post(1, "wout2", 1, 1.0)
            splits_to(SPLIT["up2"] + 2)
            dve.wait_ge(s["f_x"], 4)
            norm(5, X)
            splits_to(SPLIT["up2"] + 4)
            for t in range(TT):
                dve.wait_ge(s["ri_ready"], TT * 5 + t + 1)
                dve.tensor_scalar(XN[:, t, :], X[:, t, :], ri[:, t:t + 1], float(D) ** 0.5, ALU.mult,
                                  ALU.mult).then_inc(s["xn_ready"], 1)
            full_and_lo(6, vec("g_ffn2_pre_2", 8), None, xhi, xlo)
            ffn_up(2)
            dve.wait_ge(s["p_ps"], 1)
            dve.tensor_copy(FULL[:, 4:6, :], tp[:, 0, :].rearrange("p (k n) -> p k n", k=2)).then_inc(s["p_full"], 1)
            dve.wait_ge(s["pt_hi"], 1)
            dve.tensor_tensor(plo[:, :, :], FULL[:, 4:6, :], phi[:, :, :], ALU.subtract).then_inc(s["pt_lo"], 1)
            splits_to(SPLIT["gate"] + 2)
            post(2, "down2", 2, 0.5)
            dve.wait_ge(s["f_x"], 6)
            for q in range(4):
                i = ACC["proj"] + q
                bank_ready(i)
                dve.tensor_copy(MX[:, q // 2, (q % 2) * 512:(q % 2 + 1) * 512], accb(i))\
                    .then_inc(s["pw_done"], 1)
            splits_to(SPLIT["gate"] + 4)
            full_and_lo(7, None, None, xhi, xlo)
            for t in range(TT):
                dve.wait_ge(s["gate_s"], 2 * t + 2)
                dve.tensor_tensor(XN[:, t, :], XN[:, t, :], MX[:, t, :], ALU.mult).then_inc(s["e_y"], 1)
            dve.wait_ge(s["fgain"], 16 * 5)
            for t in range(TT):
                dve.wait_ge(s["f_ri"], TT * 3 + t + 1)
                chain(dve.scalar_tensor_tensor(XN[:, t, :], XN[:, t, :], fri[:, t:t + 1], bc[:, 1, :], ALU.mult,
                                               ALU.mult))
                dve.scalar_tensor_tensor(X[:, t, :], XN[:, t, :], float(D) ** 0.5, X[:, t, :], ALU.mult, ALU.add)\
                    .then_inc(s["out_x"], 1)


def constants():
    k = np.zeros((P, C_END), np.float32)
    k[:, C_ID:C_ID + P] = np.eye(P)
    k[:, C_TRI:C_TRI + P] = -np.tril(np.ones((P, P)))
    k[:, C_NEG:C_NEG + P] = -1.0
    k[:, C_AVG:C_AVG + P] = 1.0 / CD
    half_, grid = HD // 2, 64
    inv = (np.float32(10000.0) ** (-np.arange(0, half_, 2, dtype=np.float32) / np.float32(half_))).astype(np.float32)
    pos = np.arange(T)
    ang = np.concatenate([(pos // grid).astype(np.float32)[:, None] * inv,
                          (pos % grid).astype(np.float32)[:, None] * inv], axis=-1)
    for t in range(TT):
        at = ang[t * P:(t + 1) * P]
        k[:, C_COS + t * HD:C_COS + (t + 1) * HD] = np.repeat(np.cos(at), 2, axis=1)
        sin = np.repeat(np.sin(at), 2, axis=1)
        sin[:, 0::2] *= -1.0
        k[:, C_SIN + t * HD:C_SIN + (t + 1) * HD] = sin
    return k


SHAPES = {"x": (T, D), "ctx": (T, D), "c": (D,), "c_ctx": (D,), "w_mod": (D, 6 * D), "b_mod": (6 * D,),
          "norm1_g": (D,), "w_in": (D, 4608), "q_norm_g": (HD,), "k_norm_g": (HD,), "w_attn_out": (D, D),
          "conv_dw_w": (TAPS, CD), "conv_dw_b": (CD,), "conv_ln_g": (CD,), "conv_ln_b": (CD,),
          "w_conv_out": (CD, D), "w_out": (D, D), "norm2_g": (D,), "w_up": (D, 2 * F), "ffn_dw_w": (3, F),
          "ffn_dw_b": (F,), "w_down": (F, D), "final_g": (D,), "p_2": (T, 256), "g_ffn1_pre_2": (D,),
          "g_ffn1_post_2": (D,), "w_ffn1_gate_2": (D, F), "w_ffn1_up_2": (D, F), "w_ffn1_down_2": (F, D),
          "g_mix_pre_2": (D,), "g_mix_post_2": (D,), "w_in_2": (D, 6 * W2), "g_out_sb_2": (W2,),
          "g_out_ch_2": (W2,), "w_out_2": (D, D), "g_ffn2_pre_2": (D,), "g_ffn2_post_2": (D,),
          "w_ffn2_gate_2": (D, F), "w_ffn2_up_2": (D, F), "w_ffn2_down_2": (F, D), "w_ple_proj_2": (256, D),
          "w_ple_gate_2": (D, D), "g_ple_post_2": (D,)}


def kernel(**inputs):
    import concourse.bacc as bacc
    from concourse.bass_utils import run_bass_kernel_spmd

    nc = bacc.Bacc("TRN2", target_bir_lowering=False, num_devices=1)
    arrays = {name: np.ascontiguousarray(inputs[name]).reshape(shape) for name, shape in SHAPES.items()}
    rel = np.ascontiguousarray(inputs["rel_bias_2"])[0]
    arrays["bias"] = np.pad(rel[:, 1:], ((0, 0), (0, 2 * T - 2 * P + P - 1)), mode="edge")
    arrays["consts"] = constants()
    aps = {name: nc.dram_tensor(f"in_{name}", v.shape, mybir.dt.from_np(v.dtype), kind="ExternalInput").ap()
           for name, v in arrays.items()}
    aps["out"] = nc.dram_tensor("out_0", (T, D), F32, kind="ExternalOutput").ap()
    build(nc, aps)
    r = run_bass_kernel_spmd(nc, [{f"in_{name}": v for name, v in arrays.items()}], core_ids=[0])
    return r.results[0]["out_0"].reshape(1, T, D)
```

```python
from contextlib import ExitStack

import numpy as np

import concourse.bass as bass
from concourse import mybir

P = 128
D = 1024
KD = D // P
T = 256
TT = T // P
HD = 128
NH = 8
NKV = 2
CD = 512
KC = CD // P
TAPS = 31
KP = 2
PAD = TAPS // 2
F = 2816
KF = F // P
NPAIR = KF // 2
H2 = 8
HD2 = 64
W2 = H2 * HD2
EPS = 1e-6
CH = 2048
NR = 4
SC = 3 * P
GH = 4

F32 = mybir.dt.float32
F32R = mybir.dt.float32r
ALU = mybir.AluOpType
ACT = mybir.ActivationFunctionType
AX = mybir.AxisListType.X

VROWS = [("norm1_g", 8), ("norm2_g", 8), ("g_ffn1_pre_2", 8), ("g_mix_pre_2", 8), ("g_out_sb_2", 4),
         ("g_out_ch_2", 4), ("g_ffn2_pre_2", 8), ("conv_dw_b", 4), ("conv_ln_g", 4), ("conv_ln_b", 4),
         ("b_mod", 48), ("c", 8), ("c_ctx", 8)]
VAT = {}
_n = 0
for _name, _rows in VROWS:
    VAT[_name] = _n
    _n += _rows
assert _n <= P

C_ID, C_TRI, C_NEG, C_AVG, C_COS, C_SIN, C_END = 0, 128, 256, 384, 512, 768, 1024

STAGES = [("mod1", 8, 8), ("q", 4, 4), ("u", 4, 4), ("kv", 2, 4), ("g0", 1, 1), ("g1", 1, 1)]
for _h in range(NH):
    if _h:
        STAGES.append((f"pv{_h - 1}", 0, 1))
    if _h + 2 < NH:
        STAGES.append((f"g{_h + 2}", 1, 1))
    STAGES.append((f"mod2_{_h}", 1, 1))
STAGES += [("pv7", 0, 1)]
for _j in range(4):
    STAGES += [(f"attnout{_j}", 1, 1), (f"mod3_{_j}", 1, 1)]
STAGES += [("convout", 2, 4), ("mod4_0", 1, 1), ("mod4_1", 1, 1), ("mod4_2", 1, 1), ("mod4_3", 1, 1),
           ("g1b", 0, 2), ("g2b", 0, 2), ("wout", 4, 4)]
MOD1 = [0, 2, 1, 4, 3, 6, 5, 7]
STAGES += [("up0", 22, 22), ("down0", 11, 4), ("up1", 22, 22), ("down1", 11, 4)]
STAGES += [("qa", 2, 2), ("ka", 2, 2), ("va", 2, 2), ("qb", 2, 2), ("stick0", 0, 1), ("kb", 2, 2),
           ("vb", 2, 2), ("stick1", 0, 1), ("band0", 0, 1), ("band1", 0, 1), ("wout2", 4, 4),
           ("up2", 22, 22), ("down2", 11, 4), ("proj", 1, 4), ("gate", 4, 4)]
CHUNK, SPLIT, ACC = {}, {}, {}
_c = _s = _a = 0
for _name, _nc, _na in STAGES:
    CHUNK[_name], SPLIT[_name], ACC[_name] = _c, _s, _a
    _c += _nc
    _a += _na
    if not _name.startswith("mod"):
        _s += _nc
N_SPLIT = _s
MODS = [n for n, _, _ in STAGES if n.startswith("mod") and n != "mod1"]
TOKEN_STAGES = ("q", "kv", "wout", "down0", "down1", "va", "vb", "wout2", "down2", "proj", "gate")
USED = []
_u = 0
for _name, _nc, _na in STAGES:
    if _name.startswith("mod"):
        continue
    _runs = 2 if _name == "q" else 1
    for _j in range(_nc):
        _per = _nc // _runs
        if _name in TOKEN_STAGES:
            if _j % _per == _per - 1:
                USED.append(("acc_ready", ACC[_name] + _na // _runs * (_j // _per + 1)))
            else:
                _u += 1
                USED.append(("chunk_used", _u))
        else:
            USED.append(("acc_ready", ACC[_name] + _na // _nc * (_j + 1)))
FREED = {}


def _freed(stage, sem, first):
    n = {st[0]: st[2] for st in STAGES}[stage]
    for j in range(n):
        FREED[ACC[stage] + j] = (sem, first + j)


_freed("mod1", "mod_out", 1)
_freed("q", "q_norm", 1)
_freed("kv", "q_norm", 5)
for _j in range(4):
    FREED[ACC["u"] + _j] = ("conv_in", _j // 2 + 1)
for _h in range(NH):
    _freed(f"pv{_h}", "a_lo", _h + 1)
    _freed(f"g{_h}", "g_raw", _h + 1)
_freed("convout", "yb_done", 1)
for _j in range(4):
    _freed(f"attnout{_j}", "ya_done", _j + 1)
for _j, _name in enumerate(MODS):
    _freed(_name, "mod_out", 9 + _j)
_freed("g1b", "g1b_done", 1)
_freed("g2b", "g2b_done", 1)
_freed("wout", "res_y", 1)
_freed("down0", "res_y", 5)
for _n in range(3):
    for _j in range(22):
        FREED[ACC[f"up{_n}"] + _j] = ("h_full", NPAIR * _n + _j // 2 + 1)
for _n, _name in enumerate(("down1", "wout2", "down2")):
    _freed(_name, "f_y", 4 * _n + 1)
for _n, _name in enumerate(("qa", "ka", "qb", "kb")):
    _freed(_name, "qk2", 2 * _n + 1)
_freed("va", "v2", 1)
_freed("vb", "v2", 3)
for _n in range(2):
    _freed(f"stick{_n}", "stick_o", _n + 1)
    _freed(f"band{_n}", "band_o", _n + 1)
_freed("proj", "pw_done", 1)
_freed("gate", "gate_s", 1)
for _name in ("wout", "down0", "down1", "wout2", "down2", "proj", "gate"):
    assert ACC[_name] % 2 == 0, _name

SEMS = """hi_done lo_done mod_acc weigh chunk_used acc_ready const_in vec_in x_in ctx_in p_in gain_in table_in
pads vec_ps vec_sb silu_c mod_out affine1 affine1c tables
ss_act ss_dve ri_ready xn_ready xt_ps shift_dve xhi xlo
q_ss v_done q_ri q_norm q_rot q_tps q_t
glu_sig conv_in conv_out conv_dve ln_mean ln_c ln_sq ln_var ln_ve ln_r ln_diag ln_bc ln_n ln_y ln_hi ln_lo
sc_ready nm_ready p_exp p_scaled pt_ps pt_done a_hi a_lo g_raw g_sig yb_done ya_done mg_full mg_hi mg_lo
diag g1b_done g2b_done res_y res1 res2 cv_act cv_dve glu_act h_full h_hi h_lo
fin_ss fin_ri fin_x f_ss f_ri f_y f_x fgain
qk2 v2 z_ps z_abs z_exp z_ln sp_raw sp_ready arg_ready a_raw a_ready stick_o
b_ps b_z b_exp b_tps b_t band_o mx_ss mx_ri
p_ps p_full pt_hi pt_lo pw_done gate_s e_y out_x dve_chain pool_chain out_done""".split()


def build(nc, a):
    ctx = ExitStack()
    with ctx:
        def sb(name, shape, dt=F32, where=ctx):
            return where.enter_context(nc.sbuf_tensor(name, shape, dt))

        raw = [sb(f"raw{i}", [P, CH]) for i in range(NR)]
        whi = [sb(f"whi{i}", [P, CH], F32R) for i in range(NR)]
        wlo = [sb(f"wlo{i}", [P, CH], F32R) for i in range(NR)]
        X = sb("X", [P, TT, D])
        XN = sb("XN", [P, TT, D])
        FULL = sb("FULL", [P, KD, T])
        xhi = sb("x_hi", [P, KD, T], F32R)
        xlo = sb("x_lo", [P, KD, T], F32R)
        consts = sb("consts", [P, C_END])
        vt = sb("vt", [P, 3, P])
        sct = sb("sct", [P, KD, 2])
        modv = sb("modv", [P, 16, 2])
        mod2 = sb("mod2", [P, 32])
        gainA = sb("gainA", [P, 3, KD])
        small = sb("small", [P, 160])
        ss, ri = small[:, 0:2], small[:, 2:4]
        fss, fri = small[:, 4:6], small[:, 6:8]
        qss, qri = small[:, 8:40], small[:, 40:72]
        nmax, psum_, prec = small[:, 72:74], small[:, 74:76], small[:, 76:78]
        bmax, bsum, brec = small[:, 80:96], small[:, 96:112], small[:, 112:128]
        mss, mri = small[:, 128:132], small[:, 132:136]
        minus_half = small[:, 136:137]
        fss2 = small[:, 140:144]
        lnv = small[:, 138:140]
        modacc = sb("modacc", [P, 2, 256])

        ph1 = ExitStack()
        QT = sb("QT", [P, NH, T], F32, ph1)
        KT = sb("KT", [P, NKV, 2 * T], F32, ph1)
        V = sb("V", [P, 4, NKV * HD], F32, ph1)
        G = sb("G", [P, 16, T], F32, ph1)
        conv_x = sb("conv_x", [P, KC, T + 2 * PAD], F32, ph1)
        side_hi = sb("side_hi", [P, KD, T], F32R, ph1)
        side_lo = sb("side_lo", [P, KD, T], F32R, ph1)
        cvt_hi = sb("cvt_hi", [P, KC, T], F32R, ph1)
        cvt_lo = sb("cvt_lo", [P, KC, T], F32R, ph1)
        rope = G[:, 8:13, :]
        ph1.close()
        bc = sb("bc", [P, 3, D])
        ph2 = ExitStack()
        hhi = sb("h_hi", [P, KF, T], F32R, ph2)
        hlo = sb("h_lo", [P, KF, T], F32R, ph2)
        phi = sb("p_hi", [P, 2, T], F32R, ph2)
        plo = sb("p_lo", [P, 2, T], F32R, ph2)
        ph2.close()
        ph3 = ExitStack()
        qk2t = [sb(f"qk2_{n}", [P, H2 // 2, T], F32, ph3) for n in ("qa", "ka", "qb", "kb")]
        v2t = [sb(f"v2_{n}", [P, TT, W2], F32, ph3) for n in "ab"]
        toe = sb("toe", [P, H2, SC], F32, ph3)
        MX = sb("MX", [P, TT, D], F32, ph3)
        ph3.close()

        acc = ctx.enter_context(nc.psum_tensor("acc", [P, NR, 512], F32))
        tp = ctx.enter_context(nc.psum_tensor("tp", [P, 4, 512], F32))
        s = {n: ctx.enter_context(nc.semaphore(n)) for n in SEMS}
        landed = [ctx.enter_context(nc.semaphore(f"landed{i}")) for i in range(NR)]

        ident = consts[:, C_ID:C_ID + P]
        negtri = consts[:, C_TRI:C_TRI + P]
        negone = consts[:, C_NEG:C_NEG + P]
        avg = consts[:, C_AVG:C_AVG + P]

        def vec(name, n, off=0):
            at = VAT[name] + off
            return vt[:, 0, at:at + n]

        def accb(i):
            return acc[:, i % NR, :]

        def half(buf, t):
            flat = buf[:, :, :].rearrange("p a b -> p (a b)")
            return flat[:, t * 512:(t + 1) * 512]

        full2 = FULL[:, :, :].rearrange("p a b -> p (a b)")
        xn2 = XN[:, :, :].rearrange("p a b -> p (a b)")

        def cols(w, k, c0, n):
            return w[0:k * P, c0:c0 + n].rearrange("(k p) n -> p k n", p=P)

        def rows(w, r, k):
            return w[r * P:(r + k) * P, :].rearrange("(k p) n -> p k n", p=P)

        def deep(w, r, c0):
            return w[r * P:(r + 4) * P, c0:c0 + 512].rearrange("(k p) n -> p k n", p=P)

        w_in, w_in2, w_mod = a["w_in"], a["w_in_2"], a["w_mod"]
        QKV = NH * HD
        U0, G0 = QKV + 2 * NKV * HD, QKV + 2 * NKV * HD + 2 * CD
        src = {"mod1": [cols(w_mod, 8, 256 * j, 256) for j in range(8)],
               "q": [deep(w_in, 4 * r, 512 * b) for b in range(2) for r in range(2)],
               "kv": [deep(w_in, 4 * r, QKV) for r in range(2)],
               "u": [cols(w_in, 8, U0 + CD * h + 256 * j, 256) for j in range(2) for h in range(2)],
               "convout": [cols(a["w_conv_out"], 4, 512 * j, 512) for j in range(2)],
               "wout": [rows(a["w_out"], 2 * r, 2) for r in range(4)],
               "qa": [cols(w_in2, 8, 256 * j, 256) for j in range(2)],
               "ka": [cols(w_in2, 8, W2 + 256 * j, 256) for j in range(2)],
               "va": [deep(w_in2, 4 * r, 2 * W2) for r in range(2)],
               "qb": [cols(w_in2, 8, 3 * W2 + 256 * j, 256) for j in range(2)],
               "kb": [cols(w_in2, 8, 4 * W2 + 256 * j, 256) for j in range(2)],
               "vb": [deep(w_in2, 4 * r, 5 * W2) for r in range(2)],
               "wout2": [rows(a["w_out_2"], 2 * r, 2) for r in range(4)],
               "proj": [rows(a["w_ple_proj_2"], 0, 2)],
               "gate": [rows(a["w_ple_gate_2"], 2 * r, 2) for r in range(4)]}
        for j in range(NH):
            src[f"g{j}"] = [cols(w_in, 8, G0 + 256 * j, 256)]
            src[f"mod2_{j}"] = [cols(w_mod, 8, 2048 + 256 * j, 256)]
        for j in range(4):
            src[f"attnout{j}"] = [cols(a["w_attn_out"], 8, 256 * j, 256)]
            src[f"mod3_{j}"] = [cols(w_mod, 8, 4096 + 256 * j, 256)]
            src[f"mod4_{j}"] = [cols(w_mod, 8, 5120 + 256 * j, 256)]
        glu = [((a["w_up"], 0), (a["w_up"], F)), ((a["w_ffn1_gate_2"], 0), (a["w_ffn1_up_2"], 0)),
               ((a["w_ffn2_gate_2"], 0), (a["w_ffn2_up_2"], 0))]
        down = [a["w_down"], a["w_ffn1_down_2"], a["w_ffn2_down_2"]]
        for n in range(3):
            src[f"down{n}"] = [rows(down[n], 2 * r, min(2, KF - 2 * r)) for r in range(11)]
        kind = []
        for name, n, _ in STAGES:
            for j in range(n):
                if name == "mod1":
                    kind.append(("acc_ready", ACC[name] + MOD1.index(j) + 1) if j % 2 == 0 else ("mod_acc", j // 2 + 1))
                elif name in MODS:
                    kind.append(("mod_acc", 5 + MODS.index(name)))
                else:
                    kind.append(("lo_done", SPLIT[name] + j + 1))

        block = ctx.enter_context(nc.Block())

        @block.sync
        def _(sp):
            def slot_free(c):
                if c >= NR:
                    sem, value = kind[c - NR]
                    sp.wait_ge(s[sem], value)

            sp.wait_ge(s["pads"], 1)
            for name, n in VROWS:
                at = VAT[name]
                sp.dma_start(full2[at:at + n, 0:P], a[name].rearrange("(k p) -> k p", p=P)).then_inc(s["vec_in"], 16)
            for name, n, _ in STAGES:
                c0 = CHUNK[name]
                if not name.startswith("up"):
                    for j in range(n):
                        slot_free(c0 + j)
                        w = src[name][j]
                        sp.dma_start(raw[(c0 + j) % NR][:, :].rearrange("p (k n) -> p k n", k=w.shape[1]), w)\
                            .then_inc(landed[(c0 + j) % NR], 16)
                    continue
                halves = glu[int(name[2:])]

                def pair_load(j, q):
                    w, first = halves[q % 2]
                    sp.dma_start(raw[(c0 + q) % NR][:, :].rearrange("p (k n) -> p k n", k=8),
                                 w[:, bass.ds(first + 256 * j, 256)].rearrange("(k p) n -> p k n", p=P))\
                        .then_inc(landed[(c0 + q) % NR], 16)

                for q in range(4):
                    slot_free(c0 + q)
                    pair_load(q // 2, q)
                with sp.Fori(1, 5) as m:
                    for q in range(4):
                        sp.wait_ge(s["lo_done"], SPLIT[name] + 4 * m + q - NR + 1)
                        pair_load(2 * m + q // 2, q)
                for q in range(2):
                    slot_free(c0 + 20 + q)
                    pair_load(10, q)

        @block.gpsimd
        def _(pool):
            n_chain = [0]

            def chain(ins):
                n_chain[0] += 1
                ins.then_inc(s["pool_chain"], 1)
                pool.wait_ge(s["pool_chain"], n_chain[0])

            def bcast(v, n):
                return v.rearrange("(a n) -> a n", a=1).broadcast_to([P, n])

            chain(pool.memset(minus_half, -0.5))
            chain(pool.memset(conv_x[:, :, 0:PAD], 0.0))
            chain(pool.memset(conv_x[:, :, T + PAD:T + 2 * PAD], 0.0))
            pool.dma_start(rope[:, 4, 0:HD], bcast(a["k_norm_g"], HD)).then_inc(s["gain_in"], 16)
            pool.dma_start(rope[:, 4, HD:2 * HD], bcast(a["q_norm_g"], HD)).then_inc(s["gain_in"], 16)
            pool.wait_ge(s["gain_in"], 32)
            pool.wait_ge(s["const_in"], 16)
            for w, gat, factor in ((0, HD, float(HD) ** -0.5), (2, 0, 1.0)):
                g_ = rope[:, 4, gat:gat + HD]
                gsw = g_.rearrange("p (i two) -> p i two", two=2)[:, :, ::-1]
                for t in range(TT):
                    pool.tensor_tensor(rope[:, w, t * HD:(t + 1) * HD], g_,
                                       consts[:, C_COS + t * HD:C_COS + (t + 1) * HD], ALU.mult)
                    chain(pool.tensor_tensor(
                        rope[:, w + 1, t * HD:(t + 1) * HD].rearrange("p (i two) -> p i two", two=2), gsw,
                        consts[:, C_SIN + t * HD:C_SIN + (t + 1) * HD].rearrange("p (i two) -> p i two", two=2),
                        ALU.mult))
                if factor != 1.0:
                    pool.tensor_scalar(rope[:, w:w + 2, :], rope[:, w:w + 2, :], factor, None, ALU.mult)\
                        .then_inc(s["tables"], 1)

            def power(out, sem):
                pool.tensor_tensor(out, out, minus_half.broadcast_to([P, out.shape[1]]), ALU.pow).then_inc(sem, 1)

            def rsqrt(out, in_, width, sem):
                chain(pool.tensor_scalar(out, in_, 1.0 / width, EPS, ALU.mult, ALU.add))
                power(out, sem)

            def norm(n):
                pool.wait_ge(s["ss_act"], n + 1)
                rsqrt(ri[:, 0:1], ss[:, 0:1], D, s["ri_ready"])
                pool.wait_ge(s["ss_dve"], n + 1)
                pool.tensor_tensor(ri[:, 1:2], ss[:, 1:2], minus_half, ALU.pow).then_inc(s["ri_ready"], 1)

            norm(0)
            norm(1)
            for u in range(8):
                pool.wait_ge(s["q_ss"], u + 1)
                heads = 4 if u < 4 else NKV
                rsqrt(qri[:, 4 * u:4 * u + heads], qss[:, 4 * u:4 * u + heads], HD, s["q_ri"])

            pool.wait_ge(s["conv_in"], 2)
            conv = XN[:, 1, :].rearrange("p (k n) -> p k n", k=KC)[:, KC - KP:KC, :]

            def per_channel(v):
                return v.rearrange("p (k n) -> p k n", n=1).broadcast_to([P, KP, T])

            for i in range(TAPS):
                w = per_channel(vt[:, 1, KC * (i + 1) - KP:KC * (i + 1)])
                x = conv_x[:, KC - KP:KC, i:i + T]
                if i == 0:
                    chain(pool.tensor_tensor(conv, x, w, ALU.mult))
                    chain(pool.tensor_tensor(conv, conv, per_channel(vec("conv_dw_b", KP, KC - KP)), ALU.add))
                    continue
                term = half(XN, i % 2)[:, 0:KP * T].rearrange("p (k n) -> p k n", k=KP)
                chain(pool.tensor_tensor(term, x, w, ALU.mult))
                ins = pool.tensor_tensor(conv, conv, term, ALU.add)
                if i < TAPS - 1:
                    chain(ins)
            ins.then_inc(s["conv_out"], 1)
            pool.wait_ge(s["ln_ve"], 1)
            rsqrt(lnv, lnv, 1, s["ln_r"])

            gains = [0]

            def load_gain(name, slot):
                if gains[0]:
                    pool.wait_ge(s["fgain"], 16 * gains[0])
                pool.dma_start(bc[:, slot, :], bcast(a[name], D)).then_inc(s["fgain"], 16)
                gains[0] += 1

            pool.wait_ge(s["sc_ready"], TT * NH)
            load_gain("final_g", 2)
            norm(2)
            load_gain("g_ffn1_post_2", 0)
            for t in range(TT):
                pool.wait_ge(s["fin_ss"], t + 1)
                rsqrt(fri[:, t:t + 1], fss[:, t:t + 1], D, s["fin_ri"])
            load_gain("g_mix_post_2", 1)
            norm(3)
            load_gain("g_ffn2_post_2", 2)

            def post(m):
                for t in range(TT):
                    pool.wait_ge(s["f_ss"], 2 * TT * m + 2 * t + 2)
                    chain(pool.tensor_scalar(fri[:, t:t + 1], fss2[:, 2 * t:2 * t + 1], fss2[:, 2 * t + 1:2 * t + 2],
                                             EPS, ALU.add, ALU.add))
                    power(fri[:, t:t + 1], s["f_ri"])

            post(0)
            e = a["bias"]
            windows = bass.AP(e.tensor, 0, [[1, P], [e.shape[1], H2], [1, T]])
            pool.wait_ge(s["acc_ready"], ACC["down1"] + 4)
            pool.dma_start(MX[:, :, :].rearrange("p a b -> p (a b)").rearrange("p (h n) -> p h n", h=H2), windows)\
                .then_inc(s["table_in"], 16)
            norm(4)
            pool.dma_start(bc[:, 0, 0:TT * T].rearrange("p (t d) -> p t d", t=TT),
                           a["p_2"].rearrange("(t p) d -> p t d", p=P)).then_inc(s["p_in"], 16)
            sp4 = full2[:, 0:GH * SC].rearrange("p (h n) -> p h n", h=GH)

            def mask(view, sem):
                for blk in (0, 2):
                    v = view[:, :, blk * P:(blk + 1) * P]
                    ins = pool.affine_select(out=v, in_=v, pattern=[[0, GH], [1, P]], compare_op=ALU.is_gt,
                                             fill=0.0, base=0, channel_multiplier=-1)
                ins.then_inc(sem, 1)

            for g in range(2):
                pool.wait_ge(s["sp_raw"], GH * (g + 1))
                mask(sp4, s["sp_ready"])
                pool.wait_ge(s["a_raw"], GH * (g + 1))
                mask(sp4, s["a_ready"])
            for i in range(2):
                for t in range(TT):
                    pool.wait_ge(s["mx_ss"], 2 * i + t + 1)
                    q = 2 * i + t
                    rsqrt(mri[:, q:q + 1], mss[:, q:q + 1], W2, s["mx_ri"])
            post(1)
            norm(5)
            load_gain("g_ple_post_2", 1)
            post(2)
            post(3)

        @block.tensor
        def _(pe):
            def chunk_ready(n):
                pe.wait_ge(s["lo_done"], n + 1)

            def bank_free(i):
                if i >= NR:
                    sem, value = FREED[i - NR]
                    pe.wait_ge(s[sem], value)

            def product(out, xh, xl, wh, wl, x_stationary, start, stop):
                if x_stationary:
                    pe.matmul(out, xh, wh, start=start, stop=False)
                    pe.matmul(out, xh, wl, start=False, stop=False)
                    return pe.matmul(out, xl, wh, start=False, stop=stop)
                pe.matmul(out, wh, xh, start=start, stop=False)
                pe.matmul(out, wh, xl, start=False, stop=False)
                return pe.matmul(out, wl, xh, start=False, stop=stop)

            def feature_tiles(si, i, xh, xl, kt, bank, n=None):
                w = [r[si % NR][:, :].rearrange("p (k n) -> p k n", k=kt) for r in (whi, wlo)]
                for q in range(2):
                    at = (2 * bank + q) * P
                    for k in range(kt):
                        if n is not None and q == 0 and k % 2 == 0:
                            x_ready(n, k // 2)
                        mm = product(acc[:, i % NR, q * T:(q + 1) * T], xh[:, k, :], xl[:, k, :],
                                     w[0][:, k, at:at + P], w[1][:, k, at:at + P], False, k == 0, k == kt - 1)
                return mm

            def tiles_stage(si, i, xh=xhi, xl=xlo, kt=KD, banks=1, n=None):
                chunk_ready(si)
                for b in range(banks):
                    bank_free(i + b)
                    mm = feature_tiles(si, i + b, xh, xl, kt, b, n)
                    mm.then_inc(s["acc_ready"], 1)

            def token_stage(si0, i0, chunks, kt, nb, stats, total, k_ready=None):
                n = len(stats) * nb
                for b in range(n):
                    bank_free(i0 + b)
                for c in range(chunks):
                    chunk_ready(si0 + c)
                    if k_ready is not None:
                        k_ready(c)
                    w = [r[(si0 + c) % NR][:, :].rearrange("p (k n) -> p k n", k=kt) for r in (whi, wlo)]
                    blocks = [(x, b) for x in range(len(stats)) for b in range(nb)]
                    order = [(k, xb) for k in range(kt) for xb in blocks] if c < chunks - 1 \
                        else [(k, xb) for xb in blocks for k in range(kt)]
                    for k, (x, b) in order:
                        kk = c * kt + k
                        xh, xl, t = stats[x]
                        mm = product(accb(i0 + x * nb + b), xh[:, kk, t * P:(t + 1) * P],
                                     xl[:, kk, t * P:(t + 1) * P], w[0][:, k, b * 512:(b + 1) * 512],
                                     w[1][:, k, b * 512:(b + 1) * 512], True, kk == 0, kk == total - 1)
                        if kk == total - 1:
                            mm.then_inc(s["acc_ready"], 1)
                    if c < chunks - 1:
                        mm.then_inc(s["chunk_used"], 1)

            def mod_chunk(c, m, i):
                pe.wait_ge(landed[c % NR], 16 * (c // NR + 1))
                bank_free(i)
                w = raw[c % NR][:, :].rearrange("p (k n) -> p k n", k=8)
                for q in range(2):
                    for k in range(KD):
                        mm = pe.matmul(acc[:, i % NR, 2 * q:2 * q + 2], w[:, k, q * P:(q + 1) * P], sct[:, k, :],
                                       start=(k == 0), stop=(k == KD - 1))
                mm.then_inc(s["acc_ready"], 1)

            def mod_sum(name):
                i, j = ACC[name], MODS.index(name)
                pe.wait_ge(s["mod_acc"], 5 + j)
                bank_free(i)
                for q in range(2):
                    mm = pe.matmul(acc[:, i % NR, 2 * q:2 * q + 2], modacc[:, j % 2, q * P:(q + 1) * P], negone[:, 0:2],
                                   start=True, stop=True)
                mm.then_inc(s["acc_ready"], 1)

            def transpose_tokens(n, source, ready="xn_ready", first=None):
                for t in range(TT):
                    pe.wait_ge(s[ready], (TT * n if first is None else first) + t + 1)
                    for k in range(KD):
                        mm = pe.transpose(tp[:, k // 2, (k % 2) * T + t * P:(k % 2) * T + (t + 1) * P],
                                          source[:, t, k * P:(k + 1) * P], ident)
                        if t == TT - 1 and k % 2:
                            mm.then_inc(s["xt_ps"], 1)

            def x_ready(n, b):
                pe.wait_ge(s["xlo"], 4 * n + b + 1)

            x_tiles = [(xhi, xlo, 0), (xhi, xlo, 1)]

            pe.wait_ge(s["const_in"], 16)
            pe.wait_ge(s["vec_in"], 16 * (len(VROWS) + 3))
            pe.wait_ge(s["pads"], 1)
            for r in range(3):
                mm = pe.transpose(tp[:, 3, r * P:(r + 1) * P], full2[:, r * P:(r + 1) * P], ident)
            mm.then_inc(s["vec_ps"], 1)
            pe.wait_ge(s["vec_sb"], 1)
            transpose_tokens(0, XN)
            pe.wait_ge(s["silu_c"], 1)
            for i, j in enumerate(MOD1):
                if j % 2 == 0:
                    mod_chunk(CHUNK["mod1"] + j, j, ACC["mod1"] + i)
                    continue
                pe.wait_ge(s["mod_acc"], j // 2 + 1)
                bank_free(ACC["mod1"] + i)
                for q in range(2):
                    for v in range(2):
                        mm = pe.matmul(accb(ACC["mod1"] + i)[:, 2 * q + v:2 * q + v + 1],
                                       half(FULL, j // 2)[:, v * 256 + q * P:v * 256 + (q + 1) * P], negone[:, 0:1],
                                       start=True, stop=True)
                mm.then_inc(s["acc_ready"], 1)
            def rope_transposes(u):
                heads = 4 if u < 4 else 2
                pe.wait_ge(s["q_rot"], u + 1)
                if u >= 4:
                    pe.wait_ge(s["q_t"], u - 3)
                for h in range(heads):
                    mm = pe.transpose(tp[:, u % 4, h * P:(h + 1) * P], half(FULL, 2)[:, h * P:(h + 1) * P], ident)
                mm.then_inc(s["q_tps"], 1)

            for b in range(2):
                token_stage(SPLIT["q"] + 2 * b, ACC["q"] + 2 * b, 2, 4, 1, x_tiles, KD,
                            (lambda c: (x_ready(0, 2 * c), x_ready(0, 2 * c + 1))) if b == 0 else None)
                if b == 0:
                    transpose_tokens(1, XN)
            for j in range(4):
                tiles_stage(SPLIT["u"] + j, ACC["u"] + j)
                rope_transposes(j)
            x_ready(1, 3)
            token_stage(SPLIT["kv"], ACC["kv"], 2, 4, 1, x_tiles + [(side_hi, side_lo, 0), (side_hi, side_lo, 1)], KD)
            for j in range(2):
                tiles_stage(SPLIT[f"g{j}"], ACC[f"g{j}"])
                rope_transposes(4 + j)
            for j in range(2, 4):
                rope_transposes(4 + j)

            def scores(h):
                for t in range(TT):
                    if h == 0:
                        pe.wait_ge(s["q_t"], 8)
                    else:
                        pe.wait_ge(s["p_exp"], TT * (h - 1) + t + 1)
                    pe.matmul(tp[:, t, :], QT[:, h, t * P:(t + 1) * P], KT[:, h // 4, :], start=True, stop=True)\
                        .then_inc(s["sc_ready"], 1)

            def prob_transposes(h):
                for t in range(TT):
                    pe.wait_ge(s["p_scaled"], TT * h + t + 1)
                    if h:
                        pe.wait_ge(s["pt_done"], TT * (h - 1) + t + 1)
                    for k in range(4):
                        mm = pe.transpose(tp[:, 2 + t, k * P:(k + 1) * P], half(FULL, t)[:, k * P:(k + 1) * P], ident)
                    mm.then_inc(s["pt_ps"], 1)

            PT = FULL[:, 4:8, :]

            def values(h):
                i = ACC[f"pv{h}"]
                bank_free(i)
                pe.wait_ge(s["pt_done"], TT * (h + 1))
                if h == 0:
                    pe.wait_ge(s["v_done"], 4)
                for k in range(4):
                    mm = pe.matmul(acc[:, i % NR, 0:T], V[:, k, (h // 4) * HD:(h // 4 + 1) * HD], PT[:, k, :],
                                   start=(k == 0), stop=(k == 3))
                mm.then_inc(s["acc_ready"], 1)

            conv = XN[:, 1, :].rearrange("p (k n) -> p k n", k=KC)
            for h in range(NH):
                scores(h)
                if h:
                    values(h - 1)
                if h + 2 < NH:
                    tiles_stage(SPLIT[f"g{h + 2}"], ACC[f"g{h + 2}"])
                prob_transposes(h)
                mod_sum(f"mod2_{h}")
            values(NH - 1)
            sq = QT[:, 0:4, :]

            def ln_mean():
                pe.wait_ge(s["conv_out"], 1)
                pe.wait_ge(s["conv_dve"], TAPS * (KC - KP))
                pe.wait_ge(s["p_exp"], TT * NH)
                for k in range(KC):
                    mm = pe.matmul(tp[:, 0, 0:T], avg, conv[:, k, :], start=(k == 0), stop=(k == KC - 1))
                mm.then_inc(s["ln_mean"], 1)

            def ln_var():
                pe.wait_ge(s["ln_sq"], 1)
                for t in range(TT):
                    for k in range(KC):
                        mm = pe.matmul(tp[:, 1, t:t + 1], sq[:, k, t * P:(t + 1) * P], avg[:, 0:1], start=(k == 0),
                                       stop=(k == KC - 1))
                mm.then_inc(s["ln_var"], 1)

            def ln_broadcast():
                pe.wait_ge(s["ln_diag"], 1)
                for t in range(TT):
                    mm = pe.matmul(tp[:, 2, t * P:(t + 1) * P], negone, half(XN, 0)[:, t * P:(t + 1) * P], start=True,
                                   stop=True)
                mm.then_inc(s["ln_bc"], 1)

            pe.wait_ge(s["a_lo"], NH)
            for j in range(4):
                tiles_stage(SPLIT[f"attnout{j}"], ACC[f"attnout{j}"], side_hi, side_lo)
                if j == 0:
                    ln_mean()
                elif j == 1:
                    ln_var()
                elif j == 2:
                    ln_broadcast()
                mod_sum(f"mod3_{j}")
            pe.wait_ge(s["ln_lo"], 1)
            for j in range(2):
                tiles_stage(SPLIT["convout"] + j, ACC["convout"] + 2 * j, cvt_hi, cvt_lo, KC, 2)
            for j in range(4):
                mod_sum(f"mod4_{j}")

            def broadcast(i, n):
                pe.wait_ge(s["diag"], n + 1)
                for b in range(2):
                    bank_free(i + b)
                    pe.matmul(accb(i + b), negone, half(FULL, 2 * n + b), start=True, stop=True)\
                        .then_inc(s["acc_ready"], 1)

            broadcast(ACC["g1b"], 0)
            broadcast(ACC["g2b"], 1)
            token_stage(SPLIT["wout"], ACC["wout"], 4, 2, 2, x_tiles, KD,
                        lambda c: pe.wait_ge(s["mg_lo"], c + 1))

            def ffn_up(n):
                si, i = SPLIT[f"up{n}"], ACC[f"up{n}"]

                def chunk(m, q, norm=None):
                    pe.wait_ge(s["lo_done"], si + 4 * m + q + 1)
                    if isinstance(m, int) and m == 0:
                        bank_free(i + q)
                    else:
                        pe.wait_ge(s["h_full"], NPAIR * n + 2 * m + q // 2 - 1)
                    w = [r[(si + q) % NR][:, :].rearrange("p (k n) -> p k n", k=KD) for r in (whi, wlo)]
                    for o in range(2):
                        for k in range(KD):
                            if norm is not None and o == 0 and k % 2 == 0:
                                x_ready(norm, k // 2)
                            mm = product(acc[:, (i + q) % NR, o * T:(o + 1) * T], xhi[:, k, :], xlo[:, k, :],
                                         w[0][:, k, o * P:(o + 1) * P], w[1][:, k, o * P:(o + 1) * P], False,
                                         k == 0, k == KD - 1)
                    mm.then_inc(s["acc_ready"], 1)

                for q in range(4):
                    chunk(0, q, (2, 3, 6)[n] if q == 0 else None)
                with pe.Fori(1, 5) as m:
                    for q in range(4):
                        chunk(m, q)
                for q in range(2):
                    chunk(5, q)

            def ffn_down(n):
                token_stage(SPLIT[f"down{n}"], ACC[f"down{n}"], 11, 2, 2, [(hhi, hlo, 0), (hhi, hlo, 1)], KF,
                            lambda c: pe.wait_ge(s["h_lo"], NPAIR * n + c + 1))

            transpose_tokens(2, XN)
            ffn_up(0)
            ffn_down(0)
            transpose_tokens(3, XN)
            ffn_up(1)
            ffn_down(1)
            transpose_tokens(4, XN)

            def project2(name, n=None):
                for j in range(2):
                    tiles_stage(SPLIT[name] + j, ACC[name] + j, n=n if j == 0 else None)

            sp4 = full2[:, 0:GH * SC].rearrange("p (h n) -> p h n", h=GH)

            def head2(which, h):
                return qk2t[which][HD2 * (h % 2):HD2 * (h % 2) + HD2, h // 2, :]

            def stick_scores(g):
                pe.wait_ge(s["qk2"], 4)
                if g:
                    pe.wait_ge(s["a_raw"], GH)
                for h in range(GH):
                    q_, k_ = head2(0, g * GH + h), head2(1, g * GH + h)
                    pe.matmul(tp[:, h, 0:T], k_[:, 0:P], q_[:, :], start=True, stop=True, skip_group_check=True)
                    pe.matmul(tp[:, h, T:SC], k_[:, P:T], q_[:, P:T], start=False, stop=True,
                              skip_group_check=True).then_inc(s["z_ps"], 1)

            def stick_sums(g):
                pe.wait_ge(s["sp_ready"], g + 1)
                for h in range(GH):
                    pe.matmul(tp[:, h, 0:SC], negtri, sp4[:, h, :], start=False, stop=True, skip_group_check=True)
                    pe.matmul(tp[:, h, P:T], negone, sp4[:, h, T:SC], start=False, stop=True,
                              skip_group_check=True).then_inc(s["arg_ready"], 1)

            def weigh_values(i, at, vv, h0):
                bank_free(i)
                for h in range(GH):
                    w, v = at(h), vv[:, :, (h0 + h) * HD2:(h0 + h + 1) * HD2]
                    o = acc[:, i % NR, :]
                    pe.matmul(o[:, h * HD2:(h + 1) * HD2], w[:, 0:P], v[:, 0, :], start=True, stop=True)
                    pe.matmul(o[:, T + h * HD2:T + (h + 1) * HD2], w[:, P:T], v[:, 0, :], start=True, stop=False)
                    mm = pe.matmul(o[:, T + h * HD2:T + (h + 1) * HD2], w[:, T:SC], v[:, 1, :], start=False,
                                   stop=True)
                return mm

            project2("qa", 4)
            project2("ka")
            token_stage(SPLIT["va"], ACC["va"], 2, 4, 1, x_tiles, KD)
            stick_scores(0)
            project2("qb")
            stick_sums(0)
            pe.wait_ge(s["v2"], TT)
            pe.wait_ge(s["a_ready"], 1)
            weigh_values(ACC["stick0"], lambda h: sp4[:, h, :], v2t[0], 0).then_inc(s["acc_ready"], 1)
            stick_scores(1)
            project2("kb")
            stick_sums(1)
            token_stage(SPLIT["vb"], ACC["vb"], 2, 4, 1, x_tiles, KD)
            pe.wait_ge(s["a_ready"], 2)
            weigh_values(ACC["stick1"], lambda h: sp4[:, h, :], v2t[0], GH).then_inc(s["acc_ready"], 1)

            bpt = xn2[:, 0:2 * SC].rearrange("p (b n) -> p b n", b=2)
            bt = xn2[:, 1024:1024 + 2 * SC].rearrange("p (b n) -> p b n", b=2)

            def band_scores(h):
                if h >= 2:
                    pe.wait_ge(s["b_z"], 2 * (h - 1))
                q_, k_ = head2(2, h), head2(3, h)
                pe.matmul(tp[:, h % 2, 0:P], q_[:, 0:P], k_[:, 0:P], start=True, stop=True)
                pe.matmul(tp[:, h % 2, P:SC], q_[:, P:T], k_[:, :], start=True, stop=True).then_inc(s["b_ps"], 1)

            def band_transposes(h):
                pe.wait_ge(s["b_exp"], h + 1)
                if h >= 2:
                    pe.wait_ge(s["b_t"], h - 1)
                for k in range(3):
                    mm = pe.transpose(tp[:, 2 + h % 2, k * P:(k + 1) * P], bpt[:, h % 2, k * P:(k + 1) * P], ident)
                mm.then_inc(s["b_tps"], 1)

            def band_values(h):
                i = ACC[f"band{h // GH}"]
                if h % GH == 0:
                    bank_free(i)
                pe.wait_ge(s["b_t"], h + 1)
                w, v = bt[:, h % 2, :], v2t[1][:, :, h * HD2:(h + 1) * HD2]
                o, at = acc[:, i % NR, :], (h % GH) * HD2
                pe.matmul(o[:, at:at + HD2], w[:, 0:P], v[:, 0, :], start=True, stop=True)
                pe.matmul(o[:, T + at:T + at + HD2], w[:, P:T], v[:, 0, :], start=True, stop=False)
                mm = pe.matmul(o[:, T + at:T + at + HD2], w[:, T:SC], v[:, 1, :], start=False, stop=True)
                if h % GH == GH - 1:
                    mm.then_inc(s["acc_ready"], 1)

            pe.wait_ge(s["qk2"], 8)
            pe.wait_ge(s["a_raw"], 2 * GH)
            band_scores(0)
            pe.wait_ge(s["v2"], 2 * TT)
            for h in range(H2):
                if h + 1 < H2:
                    band_scores(h + 1)
                if h:
                    band_values(h - 1)
                band_transposes(h)
            band_values(H2 - 1)

            transpose_tokens(5, MX)
            token_stage(SPLIT["wout2"], ACC["wout2"], 4, 2, 2, x_tiles, KD, lambda c: x_ready(5, c))
            transpose_tokens(6, XN)
            ffn_up(2)
            pe.wait_ge(s["p_in"], 16)
            for t in range(TT):
                for k in range(2):
                    mm = pe.transpose(tp[:, 0, k * T + t * P:k * T + (t + 1) * P],
                                      bc[:, 0, t * T + k * P:t * T + (k + 1) * P], ident)
            mm.then_inc(s["p_ps"], 1)
            ffn_down(2)
            pe.wait_ge(s["pt_lo"], 1)
            token_stage(SPLIT["proj"], ACC["proj"], 1, 2, 2, [(phi, plo, 0), (phi, plo, 1)], 2)
            transpose_tokens(7, X, "f_x", 4)
            token_stage(SPLIT["gate"], ACC["gate"], 4, 2, 2, x_tiles, KD, lambda c: x_ready(7, c))

        @block.scalar
        def _(act):
            n_split = [0]

            def split(si_slot, raw_slot, landed_at, used):
                act.wait_ge(landed[raw_slot], landed_at)
                if used is not None:
                    act.wait_ge(s[used[0]], used[1])
                act.copy(whi[si_slot][:, :], raw[raw_slot][:, :]).then_inc(s["hi_done"], 1)

            chunk_of = [c for c, (what, _) in enumerate(kind) if what == "lo_done"]

            def splits_to(n):
                while n_split[0] < min(n, N_SPLIT):
                    si = n_split[0]
                    c = chunk_of[si]
                    split(si % NR, c % NR, 16 * (c // NR + 1), USED[si - NR] if si >= NR else None)
                    n_split[0] += 1

            def bank_ready(i):
                act.wait_ge(s["acc_ready"], i + 1)

            def norm(n, source):
                act.activation(XN[:, 0, :], source[:, 0, :], ACT.Square, accum_out=ss[:, 0:1])\
                    .then_inc(s["ss_act"], 1)

            def x_hi(n, gain, shift, dst):
                for b in range(4):
                    act.wait_ge(s["xt_ps"], 4 * n + b + 1)
                    if gain is None:
                        ins = act.copy(dst[:, 2 * b:2 * b + 2, :], tp[:, b, :].rearrange("p (k n) -> p k n", k=2))
                    else:
                        for k in (2 * b, 2 * b + 1):
                            ins = act.activation(dst[:, k, :], tp[:, b, (k % 2) * T:(k % 2 + 1) * T], ACT.Identity,
                                                 scale=gain[:, k:k + 1], bias=0.0 if shift is None else shift(k))
                    ins.then_inc(s["xhi"], 1)

            act.dma_start(consts[:, :], a["consts"]).then_inc(s["const_in"], 16)
            act.dma_start(X[:, :, :], a["x"].rearrange("(t p) d -> p t d", p=P)).then_inc(s["x_in"], 16)
            act.wait_ge(s["pads"], 1)
            act.dma_start(full2[0:TAPS * KC, P:2 * P], a["conv_dw_w"].rearrange("i (k p) -> (i k) p", p=P))\
                .then_inc(s["vec_in"], 16)
            act.dma_start(full2[0:3 * KF, 2 * P:3 * P], a["ffn_dw_w"].rearrange("i (k p) -> (i k) p", p=P))\
                .then_inc(s["vec_in"], 16)
            act.dma_start(full2[3 * KF:4 * KF, 2 * P:3 * P], a["ffn_dw_b"].rearrange("(k p) -> k p", p=P))\
                .then_inc(s["vec_in"], 16)
            CTX = G[:, 0:8, :].rearrange("p (t k) n -> p t (k n)", t=TT)
            act.dma_start(CTX, a["ctx"].rearrange("(t p) d -> p t d", p=P)).then_inc(s["ctx_in"], 16)
            act.wait_ge(s["x_in"], 16)
            norm(0, X)
            act.wait_ge(s["vec_sb"], 1)
            act.activation(sct[:, :, 0], vec("c", 8), ACT.Silu)
            act.activation(sct[:, :, 1], vec("c_ctx", 8), ACT.Silu).then_inc(s["silu_c"], 1)
            splits_to(2)
            act.wait_ge(s["affine1"], 1)
            x_hi(0, gainA[:, 0, :], lambda k: modv[:, k, 0:1], xhi)
            act.wait_ge(s["ctx_in"], 16)
            norm(1, CTX)
            splits_to(4)
            act.wait_ge(s["affine1c"], 1)
            x_hi(1, gainA[:, 1, :], lambda k: modv[:, k, 1:2], side_hi)

            def unit_squares(u, i, heads, v_tile):
                bank_ready(i)
                if u:
                    act.wait_ge(s["q_ss"], u)
                if v_tile is not None:
                    act.copy(V[:, v_tile, :], accb(i)[:, NKV * HD:2 * NKV * HD]).then_inc(s["v_done"], 1)
                for h in range(heads):
                    ins = act.activation(half(FULL, 0)[:, h * HD:(h + 1) * HD], accb(i)[:, h * HD:(h + 1) * HD],
                                         ACT.Square, accum_out=qss[:, 4 * u + h:4 * u + h + 1])
                ins.then_inc(s["q_ss"], 1)

            def unit_out(u):
                act.wait_ge(s["q_tps"], u + 1)
                if u < 4:
                    b, t = u // 2, u % 2
                    dst = QT[:, 4 * b:4 * b + 4, t * P:(t + 1) * P]
                    ps = tp[:, u % 4, :].rearrange("p (h n) -> p h n", h=4)
                else:
                    t = (u - 4 + 2) % 4
                    dst = KT[:, :, t * P:(t + 1) * P]
                    ps = tp[:, u % 4, 0:NKV * P].rearrange("p (h n) -> p h n", h=NKV)
                act.copy(dst, ps).then_inc(s["q_t"], 1)

            splits_to(SPLIT["q"] + 4)
            act.wait_ge(s["xlo"], 8)
            for u in range(4):
                unit_squares(u, ACC["q"] + u, 4, None)
                splits_to(SPLIT["u"] + min(u + 1, 3))
            for j in range(2):
                unit_out(2 * j)
                bank_ready(ACC["u"] + 2 * j + 1)
                act.activation(half(XN, j), accb(ACC["u"] + 2 * j + 1), ACT.Sigmoid)\
                    .then_inc(s["glu_sig"], 1)
                unit_out(2 * j + 1)
                splits_to(SPLIT["kv"] + j)
            splits_to(SPLIT["g0"] + 2)
            for u in range(4, 8):
                unit_squares(u, ACC["kv"] + u - 4, NKV, (u - 4 + 2) % 4)
            splits_to(SPLIT["g2"] + 1)
            for u in range(4, 8):
                unit_out(u)
            splits_to(SPLIT["g2"] + 2)

            def pv_hi(h):
                bank_ready(ACC[f"pv{h}"])
                act.copy(side_hi[:, h, :], acc[:, ACC[f"pv{h}"] % NR, 0:T]).then_inc(s["a_hi"], 1)

            def g_out(h):
                bank_ready(ACC[f"g{h}"])
                act.copy(G[:, 2 * h:2 * h + 2, :], acc[:, ACC[f"g{h}"] % NR, :].rearrange("p (q n) -> p q n", q=2))\
                    .then_inc(s["g_raw"], 1)

            PT = FULL[:, 4:8, :]
            for h in range(NH):
                for t in range(TT):
                    act.wait_ge(s["nm_ready"], TT * h + t + 1)
                    if h:
                        act.wait_ge(s["pt_ps"], TT * (h - 1) + t + 1)
                    act.activation(half(FULL, t), tp[:, t, :], ACT.Exp, bias=nmax[:, t:t + 1],
                                   accum_out=psum_[:, t:t + 1]).then_inc(s["p_exp"], 1)
                if h == 0:
                    g_out(0)
                    g_out(1)
                else:
                    pv_hi(h - 1)
                if h + 2 < NH:
                    g_out(h + 2)
                for t in range(TT):
                    act.wait_ge(s["pt_ps"], TT * h + t + 1)
                    act.copy(PT[:, :, t * P:(t + 1) * P], tp[:, 2 + t, :].rearrange("p (k n) -> p k n", k=4))\
                        .then_inc(s["pt_done"], 1)
                splits_to(min(SPLIT["g2"] + h + 3, SPLIT["attnout1"]))
            pv_hi(NH - 1)
            act.wait_ge(s["g_raw"], NH)
            for q in range(2):
                act.activation(G[:, 8 * q:8 * q + 8, :], G[:, 8 * q:8 * q + 8, :], ACT.Sigmoid)\
                    .then_inc(s["g_sig"], 1)
            sq = QT[:, 0:4, :]
            act.wait_ge(s["ln_c"], 1)
            act.activation(sq, QT[:, 4:8, :], ACT.Square).then_inc(s["ln_sq"], 1)
            splits_to(SPLIT["convout"])
            act.wait_ge(s["ln_n"], 1)
            for k in range(KC):
                ins = act.activation(QT[:, k, :], QT[:, 4 + k, :], ACT.Silu, scale=vec("conv_ln_g", 1, k),
                                     bias=vec("conv_ln_b", 1, k))
            ins.then_inc(s["ln_y"], 1)
            act.wait_ge(s["ln_y"], 1)
            act.copy(cvt_hi[:, :, :], QT[:, 0:4, :]).then_inc(s["ln_hi"], 1)
            splits_to(SPLIT["convout"] + 2)
            for j in range(4):
                act.wait_ge(s["mg_full"], j + 1)
                act.copy(xhi[:, 2 * j:2 * j + 2, :], FULL[:, 2 * j:2 * j + 2, :]).then_inc(s["mg_hi"], 1)
            splits_to(SPLIT["wout"] + 4)
            for b in range(2):
                bank_ready(ACC["g1b"] + b)
                act.copy(bc[:, 0, b * 512:(b + 1) * 512], accb(ACC["g1b"] + b)).then_inc(s["g1b_done"], 1)
            for b in range(2):
                bank_ready(ACC["g2b"] + b)
                act.copy(bc[:, 1, b * 512:(b + 1) * 512], accb(ACC["g2b"] + b)).then_inc(s["g2b_done"], 1)
            splits_to(SPLIT["up0"] + 3)
            act.wait_ge(s["res1"], 1)
            norm(2, X)
            x_hi(2, gainA[:, 2, :], lambda k: mod2[:, 8 + k:9 + k], xhi)
            splits_to(SPLIT["up0"] + 4)

            def ffn_up(n):
                si, i, c = SPLIT[f"up{n}"], ACC[f"up{n}"], CHUNK[f"up{n}"]
                assert n_split[0] == si + 4
                pairs = NPAIR * n

                def ahead(m, o):
                    split((si + o) % NR, (c + o) % NR, 16 * ((c + o) // NR + 2 + m), ("acc_ready", i + o + 1 + 4 * m))

                def pair(m, q, more):
                    j = 2 * m + q
                    g = i + 2 * q
                    act.wait_ge(s["acc_ready"], g + 4 * m + 1)
                    if n == 0:
                        for o in range(2):
                            w = 2 * j + o
                            act.activation(half(XN, q)[:, o * T:(o + 1) * T], acc[:, g % NR, o * T:(o + 1) * T],
                                           ACT.Identity, scale=vt[:, 2, bass.ds(KF + w, 1)],
                                           bias=vt[:, 2, bass.ds(3 * KF + w, 1)]).then_inc(s["cv_act"], 1)
                        if more:
                            ahead(m, 2 * q)
                        act.wait_ge(s["cv_dve"], 4 * j + 4)
                        act.activation(half(XN, 2 + q), half(XN, q), ACT.Gelu_apprx_tanh).then_inc(s["glu_act"], 1)
                    else:
                        act.activation(half(XN, 2 + q), accb(g), ACT.Silu).then_inc(s["glu_act"], 1)
                        if more:
                            ahead(m, 2 * q)
                    if more:
                        ahead(m, 2 * q + 1)
                    act.wait_ge(s["h_full"], pairs + j + 1)
                    act.copy(hhi[:, bass.ds(2 * j, 2), :],
                             half(FULL, q).rearrange("p (o n) -> p o n", o=2)).then_inc(s["h_hi"], 1)

                with act.Fori(0, 5) as m:
                    for q in range(2):
                        pair(m, q, True)
                n_split[0] = si + 24
                pair(5, 0, False)

            ffn_up(0)
            splits_to(SPLIT["up1"] + 3)
            for t in range(TT):
                act.wait_ge(s["res2"], t + 1)
                act.activation(XN[:, t, :], X[:, t, :], ACT.Square, accum_out=fss[:, t:t + 1]).then_inc(s["fin_ss"], 1)
            act.wait_ge(s["fin_x"], 1)
            norm(3, X)
            x_hi(3, vec("g_ffn1_pre_2", 8), None, xhi)
            splits_to(SPLIT["up1"] + 4)
            ffn_up(1)

            def post(m, name):
                for j in range(2 * TT):
                    i = ACC[name] + j
                    bank_ready(i)
                    act.activation(half(XN, j), accb(i), ACT.Square, scale=float(D) ** -0.5,
                                   accum_out=fss2[:, j:j + 1]).then_inc(s["f_ss"], 1)

            splits_to(SPLIT["qa"] + 3)
            post(0, "down1")
            act.wait_ge(s["f_x"], 1)
            norm(4, X)
            x_hi(4, vec("g_mix_pre_2", 8), None, xhi)
            splits_to(SPLIT["qa"] + 4)

            def qk_out(w, name):
                for j in range(2):
                    bank_ready(ACC[name] + j)
                    act.activation(qk2t[w][:, 2 * j:2 * j + 2, :],
                                   acc[:, (ACC[name] + j) % NR, :].rearrange("p (q n) -> p q n", q=2),
                                   ACT.Copy, scale=HD2 ** -0.5 if w % 2 == 0 else 1.0).then_inc(s["qk2"], 1)

            ez = xn2[:, 0:GH * SC].rearrange("p (h n) -> p h n", h=GH)
            sp4 = full2[:, 0:GH * SC].rearrange("p (h n) -> p h n", h=GH)

            def stick_ln(g):
                for h in range(GH):
                    act.wait_ge(s["z_ps"], GH * g + h + 1)
                    act.activation(ez[:, h, :], tp[:, h, 0:SC], ACT.Abs).then_inc(s["z_abs"], 1)
                act.wait_ge(s["z_abs"], GH * (g + 1))
                for h in range(GH):
                    act.activation(ez[:, h, :], ez[:, h, :], ACT.Exp, scale=-1.0).then_inc(s["z_exp"], 1)
                act.wait_ge(s["z_exp"], GH * (g + 1))
                for h in range(GH):
                    act.activation(ez[:, h, :], ez[:, h, :], ACT.Ln, bias=1.0).then_inc(s["z_ln"], 1)

            def stick_exp(g):
                for h in range(GH):
                    act.wait_ge(s["arg_ready"], GH * g + h + 1)
                    act.activation(sp4[:, h, :], tp[:, h, 0:SC], ACT.Exp).then_inc(s["a_raw"], 1)

            qk_out(0, "qa")
            splits_to(SPLIT["va"] + 1)
            qk_out(1, "ka")
            splits_to(SPLIT["qb"] + 2)
            for t in range(TT):
                bank_ready(ACC["va"] + t)
                act.copy(v2t[0][:, t, :], accb(ACC["va"] + t)).then_inc(s["v2"], 1)
            stick_ln(0)
            splits_to(SPLIT["kb"] + 1)
            qk_out(2, "qb")
            splits_to(SPLIT["kb"] + 2)
            stick_exp(0)
            splits_to(SPLIT["vb"] + 1)
            stick_ln(1)
            qk_out(3, "kb")
            splits_to(SPLIT["vb"] + 2)
            stick_exp(1)
            for t in range(TT):
                bank_ready(ACC["vb"] + t)
                act.copy(v2t[1][:, t, :], accb(ACC["vb"] + t)).then_inc(s["v2"], 1)
            bz = full2[:, 0:2 * SC].rearrange("p (b n) -> p b n", b=2)
            bpt = xn2[:, 0:2 * SC].rearrange("p (b n) -> p b n", b=2)
            bt = xn2[:, 1024:1024 + 2 * SC].rearrange("p (b n) -> p b n", b=2)

            def band_exp(h):
                act.wait_ge(s["b_z"], 2 * (h + 1))
                if h >= 2:
                    act.wait_ge(s["b_tps"], h - 1)
                for t, (lo, hi) in enumerate(((0, P), (P, SC))):
                    ins = act.activation(bpt[:, h % 2, lo:hi], bz[:, h % 2, lo:hi], ACT.Exp,
                                         bias=bmax[:, 2 * h + t:2 * h + t + 1],
                                         accum_out=bsum[:, 8 * t + h:8 * t + h + 1])
                ins.then_inc(s["b_exp"], 1)

            band_exp(0)
            for h in range(H2):
                if h + 1 < H2:
                    band_exp(h + 1)
                if h % 2:
                    splits_to(SPLIT["wout2"] + h // 2 + 1)
                act.wait_ge(s["b_tps"], h + 1)
                act.copy(bt[:, h % 2, :], tp[:, 2 + h % 2, 0:SC]).then_inc(s["b_t"], 1)
            x_hi(5, vec("g_out_sb_2", 8), None, xhi)
            splits_to(SPLIT["up2"] + 3)
            post(1, "wout2")
            act.wait_ge(s["f_x"], 3)
            norm(5, X)
            x_hi(6, vec("g_ffn2_pre_2", 8), None, xhi)
            splits_to(SPLIT["up2"] + 4)
            ffn_up(2)
            act.wait_ge(s["p_full"], 1)
            act.copy(phi[:, :, :], FULL[:, 4:6, :]).then_inc(s["pt_hi"], 1)
            splits_to(SPLIT["gate"] + 3)
            post(2, "down2")
            splits_to(SPLIT["gate"] + 4)
            x_hi(7, None, None, xhi)
            for t in range(TT):
                for b in range(2):
                    i = ACC["gate"] + 2 * t + b
                    bank_ready(i)
                    act.activation(half(XN, 2 * t + b), accb(i), ACT.Sigmoid).then_inc(s["gate_s"], 1)
            for j in range(2 * TT):
                act.wait_ge(s["e_y"], j + 1)
                act.activation(half(FULL, j), half(XN, j), ACT.Square, scale=float(D) ** -0.5,
                               accum_out=fss2[:, j:j + 1]).then_inc(s["f_ss"], 1)
            for t in range(TT):
                act.wait_ge(s["out_x"], t + 1)
                act.dma_start(a["out"][t * P:(t + 1) * P, :], X[:, t, :]).then_inc(s["out_done"], 16)
            act.wait_ge(s["out_done"], 16 * TT)

        @block.vector
        def _(dve):
            n_split, n_chain, n_shift = [0], [0], [0]

            def chain(ins):
                n_chain[0] += 1
                ins.then_inc(s["dve_chain"], 1)
                dve.wait_ge(s["dve_chain"], n_chain[0])

            chunk_of = [c for c, (what, _) in enumerate(kind) if what == "lo_done"]

            def split(slot, raw_slot, n):
                dve.wait_ge(s["hi_done"], n)
                dve.tensor_tensor(wlo[slot][:, :], raw[raw_slot][:, :], whi[slot][:, :], ALU.subtract)\
                    .then_inc(s["lo_done"], 1)

            def splits_to(n):
                while n_split[0] < min(n, N_SPLIT):
                    si = n_split[0]
                    split(si % NR, chunk_of[si] % NR, si + 1)
                    n_split[0] += 1

            def bank_ready(i):
                dve.wait_ge(s["acc_ready"], i + 1)

            def norm(n, source):
                dve.tensor_tensor_reduce(XN[:, 1, :], source[:, 1, :], source[:, 1, :], 1.0 / D, EPS, ALU.mult, ALU.add,
                                         ss[:, 1:2]).then_inc(s["ss_dve"], 1)

            def scale_tokens(n, source):
                for t in range(TT):
                    dve.wait_ge(s["ri_ready"], TT * n + t + 1)
                    dve.tensor_scalar(XN[:, t, :], source[:, t, :], ri[:, t:t + 1], None, ALU.mult)\
                        .then_inc(s["xn_ready"], 1)

            def x_lo(n, gain, shift, dh, dl):
                for b in range(4):
                    dve.wait_ge(s["xhi"], 4 * n + b + 1)
                    if gain is None:
                        dve.tensor_tensor(dl[:, 2 * b:2 * b + 2, :], tp[:, b, :].rearrange("p (k n) -> p k n", k=2),
                                          dh[:, 2 * b:2 * b + 2, :], ALU.subtract).then_inc(s["xlo"], 1)
                        continue
                    dst = dl if shift is None else FULL
                    for k in (2 * b, 2 * b + 1):
                        ins = dve.scalar_tensor_tensor(dst[:, k, :], tp[:, b, (k % 2) * T:(k % 2 + 1) * T],
                                                       gain[:, k:k + 1], dh[:, k, :], ALU.mult, ALU.subtract)
                    if shift is not None:
                        ins.then_inc(s["shift_dve"], 1)
                        dve.wait_ge(s["shift_dve"], n_shift[0] + 1)
                        n_shift[0] += 1
                        for k in (2 * b, 2 * b + 1):
                            ins = dve.tensor_scalar(dl[:, k, :], FULL[:, k, :], shift(k), None, ALU.add)
                    ins.then_inc(s["xlo"], 1)

            dve.memset(full2[:, 0:3 * P], 0.0).then_inc(s["pads"], 1)
            dve.wait_ge(s["vec_ps"], 1)
            dve.tensor_copy(vt[:, :, :], tp[:, 3, 0:3 * P].rearrange("p (r n) -> p r n", r=3))\
                .then_inc(s["vec_sb"], 1)
            dve.wait_ge(s["x_in"], 16)
            norm(0, X)
            scale_tokens(0, X)

            def weigh(c, out, column, k, sem=None):
                w = raw[c % NR][:, k * 256:(k + 1) * 256]
                if k == 0:
                    ins = dve.tensor_scalar(out, w, sct[:, k, column:column + 1], None, ALU.mult)
                else:
                    dve.wait_ge(s["weigh"], n_weigh[0])
                    ins = dve.scalar_tensor_tensor(out, w, sct[:, k, column:column + 1], out, ALU.mult, ALU.add)
                if k < KD - 1:
                    n_weigh[0] += 1
                    ins.then_inc(s["weigh"], 1)
                elif sem is not None:
                    ins.then_inc(s[sem], 1)

            n_weigh = [0]
            dve.wait_ge(s["silu_c"], 1)
            for step in range(4):
                c = CHUNK["mod1"] + 2 * step + 1
                dve.wait_ge(landed[c % NR], 16 * (c // NR + 1))
                for v in range(2):
                    for k in range(KD):
                        weigh(c, half(FULL, step)[:, v * 256:(v + 1) * 256], v, k, "mod_acc" if v == 1 else None)
                for i in ((), (0, 1), (2, 3), (4, 5, 6, 7))[step]:
                    j = MOD1[i]
                    bank_ready(ACC["mod1"] + i)
                    b = vec("b_mod", 2, 2 * j)
                    dve.tensor_tensor(modv[:, 2 * j:2 * j + 2, :],
                                      b.rearrange("p (q c) -> p q c", c=1).broadcast_to([P, 2, 2]),
                                      accb(ACC["mod1"] + i)[:, 0:4].rearrange("p (q c) -> p q c", q=2),
                                      ALU.subtract if j % 2 else ALU.add).then_inc(s["mod_out"], 1)
            dve.wait_ge(s["mod_out"], 8)
            for w, sem in ((0, "affine1"), (1, "affine1c")):
                dve.scalar_tensor_tensor(gainA[:, w, :], modv[:, 8:16, w], 1.0, vec("norm1_g", 8), ALU.add, ALU.mult)\
                    .then_inc(s[sem], 1)
            dve.wait_ge(s["affine1"], 1)
            splits_to(1)
            x_lo(0, gainA[:, 0, :], lambda k: modv[:, k, 0:1], xhi, xlo)
            splits_to(2)
            CTX = G[:, 0:8, :].rearrange("p (t k) n -> p t (k n)", t=TT)
            dve.wait_ge(s["ctx_in"], 16)
            norm(1, CTX)
            scale_tokens(1, CTX)
            splits_to(4)
            x_lo(1, gainA[:, 1, :], lambda k: modv[:, k, 1:2], side_hi, side_lo)

            def unit(u, i, heads, t, kind_):
                w = heads * HD
                qn, t1, t2 = (half(FULL, x)[:, 0:w] for x in (1, 2, 3))

                def by_head(v):
                    return v.rearrange("p (h d) -> p h d", h=heads)

                def table(r):
                    return rope[:, r:r + 1, t * HD:(t + 1) * HD].broadcast_to([P, heads, HD])

                def swapped(v):
                    return v.rearrange("p (h i two) -> p h i two", h=heads, two=2)[:, :, :, ::-1]

                dve.wait_ge(s["q_ri"], u + 1)
                if u:
                    dve.wait_ge(s["q_rot"], u)
                r = qri[:, 4 * u:4 * u + heads].rearrange("p (h d) -> p h d", d=1).broadcast_to([P, heads, HD])
                dve.tensor_tensor(by_head(qn), by_head(accb(i)[:, 0:w]), r, ALU.mult).then_inc(s["q_norm"], 1)
                dve.wait_ge(s["q_norm"], u + 1)
                if u:
                    dve.wait_ge(s["q_tps"], u)
                if kind_ is None:
                    g_ = rope[:, 4:5, 0:HD].broadcast_to([P, heads, HD])
                    dve.tensor_tensor(by_head(t1), by_head(qn), g_, ALU.mult).then_inc(s["q_rot"], 1)
                    return
                dve.tensor_tensor(by_head(t1), by_head(qn), table(kind_), ALU.mult)
                for h in range(heads):
                    ins = dve.tensor_tensor(
                        t2[:, h * HD:(h + 1) * HD].rearrange("p (i two) -> p i two", two=2),
                        qn[:, h * HD:(h + 1) * HD].rearrange("p (i two) -> p i two", two=2)[:, :, ::-1],
                        rope[:, kind_ + 1, t * HD:(t + 1) * HD].rearrange("p (i two) -> p i two", two=2), ALU.mult)
                chain(ins)
                dve.tensor_tensor(t1, t1, t2, ALU.add).then_inc(s["q_rot"], 1)

            dve.wait_ge(s["tables"], 1)
            splits_to(SPLIT["q"] + 4)
            for u in range(4):
                unit(u, ACC["q"] + u, 4, u % 2, 0)
                splits_to(SPLIT["u"] + min(u + 1, 3))
            for j in range(2):
                dve.wait_ge(s["glu_sig"], j + 1)
                dve.tensor_tensor(conv_x[:, 2 * j:2 * j + 2, PAD:PAD + T],
                                  accb(ACC["u"] + 2 * j).rearrange("p (q n) -> p q n", q=2),
                                  half(XN, j).rearrange("p (q n) -> p q n", q=2), ALU.mult)\
                    .then_inc(s["conv_in"], 1)
                splits_to(SPLIT["kv"] + j)
            splits_to(SPLIT["g0"] + 2)
            for u in range(4, 8):
                unit(u, ACC["kv"] + u - 4, NKV, u % 2, 2 if u < 6 else None)
            splits_to(SPLIT["g2"] + 2)

            def pv_lo(h):
                i = ACC[f"pv{h}"]
                dve.wait_ge(s["a_hi"], h + 1)
                dve.tensor_tensor(side_lo[:, h, :], acc[:, i % NR, 0:T], side_hi[:, h, :], ALU.subtract)\
                    .then_inc(s["a_lo"], 1)

            def mod_out(name):
                i, j = ACC[name], MODS.index(name)
                bank_ready(i)
                ps = accb(i)[:, 0:4].rearrange("p (q c) -> p q c", q=2)[:, :, 0]
                dve.tensor_tensor(mod2[:, 2 * j:2 * j + 2], vec("b_mod", 2, 16 + 2 * j), ps, ALU.subtract)\
                    .then_inc(s["mod_out"], 1)

            def mod_weigh(name, between=None):
                j, c = MODS.index(name), CHUNK[name]
                dve.wait_ge(landed[c % NR], 16 * (c // NR + 1))
                if j >= 2:
                    dve.wait_ge(s["acc_ready"], ACC[MODS[j - 2]] + 1)
                for k in range(KD):
                    weigh(c, modacc[:, j % 2, :], 0, k, "mod_acc")
                    if between is not None:
                        between(k)

            KV_ = KC - KP

            def conv_tap(i, k):
                if i >= TAPS:
                    return
                at = XN[:, 1, k * T:(k + 1) * T]
                w = vt[:, 1, KC * i + k:KC * i + k + 1]
                if i == 0:
                    dve.tensor_scalar(at, conv_x[:, k, 0:T], w, vec("conv_dw_b", 1, k), ALU.mult, ALU.add)\
                        .then_inc(s["conv_dve"], 1)
                else:
                    dve.wait_ge(s["conv_dve"], KV_ * (i - 1) + k + 1)
                    dve.scalar_tensor_tensor(at, conv_x[:, k, i:i + T], w, at, ALU.mult, ALU.add)\
                        .then_inc(s["conv_dve"], 1)

            per_slot = (TAPS + NH - 1) // NH
            assert per_slot * KV_ == KD
            for h in range(NH):
                for t in range(TT):
                    dve.wait_ge(s["sc_ready"], TT * h + t + 1)
                    dve.tensor_reduce(nmax[:, t:t + 1], tp[:, t, :], AX, ALU.max, negate=True)\
                        .then_inc(s["nm_ready"], 1)
                for t in range(TT):
                    dve.wait_ge(s["p_exp"], TT * h + t + 1)
                    chain(dve.reciprocal(prec[:, t:t + 1], psum_[:, t:t + 1]))
                    dve.tensor_scalar(half(FULL, t), half(FULL, t), prec[:, t:t + 1], None, ALU.mult)\
                        .then_inc(s["p_scaled"], 1)
                if h:
                    pv_lo(h - 1)
                splits_to(min(SPLIT["g2"] + h + 2, SPLIT["attnout1"]))
                mod_weigh(f"mod2_{h}", lambda k: conv_tap(per_slot * h + k // KV_, k % KV_))
                if h:
                    mod_out(f"mod2_{h - 1}")
            mod_out(f"mod2_{NH - 1}")
            pv_lo(NH - 1)
            conv = XN[:, 1, :].rearrange("p (k n) -> p k n", k=KC)
            cent = QT[:, 4:8, :]

            def over_tiles(v):
                return v.rearrange("p (k n) -> p k n", k=1).broadcast_to([P, KC, T])

            for j in range(4):
                b = ACC[f"attnout{j}"]
                bank_ready(b)
                dve.wait_ge(s["g_sig"], 1)
                v = G[:, 2 * j:2 * j + 2, :]
                dve.tensor_tensor(v, accb(b).rearrange("p (q n) -> p q n", q=2), v, ALU.mult)\
                    .then_inc(s["ya_done"], 1)
                if j == 0:
                    dve.wait_ge(s["ln_mean"], 1)
                    dve.tensor_tensor(cent, conv, over_tiles(tp[:, 0, 0:T]), ALU.subtract).then_inc(s["ln_c"], 1)
                elif j == 1:
                    dve.wait_ge(s["ln_var"], 1)
                    dve.tensor_copy(lnv, tp[:, 1, 0:TT]).then_inc(s["ln_ve"], 1)
                    dve.wait_ge(s["ln_r"], 1)
                    for t in range(TT):
                        ins = dve.tensor_scalar(half(XN, 0)[:, t * P:(t + 1) * P], ident, lnv[:, t:t + 1], -1.0,
                                                ALU.mult, ALU.mult)
                    ins.then_inc(s["ln_diag"], 1)
                elif j == 2:
                    dve.wait_ge(s["ln_bc"], 1)
                    dve.wait_ge(s["ln_c"], 1)
                    dve.tensor_tensor(cent, cent, over_tiles(tp[:, 2, 0:T]), ALU.mult).then_inc(s["ln_n"], 1)
                splits_to(min(SPLIT[f"attnout{j}"] + 2, SPLIT["convout"]))
                mod_weigh(f"mod3_{j}")
                if j:
                    mod_out(f"mod3_{j - 1}")
            mod_out("mod3_3")
            dve.wait_ge(s["ln_hi"], 1)
            dve.tensor_tensor(cvt_lo[:, :, :], QT[:, 0:4, :], cvt_hi[:, :, :], ALU.subtract).then_inc(s["ln_lo"], 1)
            splits_to(SPLIT["convout"] + 2)
            dve.wait_ge(s["g_sig"], 2)
            dve.wait_ge(s["ya_done"], 4)
            for j in range(4):
                b = ACC["convout"] + j
                bank_ready(b)
                v = G[:, 8 + 2 * j:10 + 2 * j, :]
                dve.tensor_tensor(v, accb(b).rearrange("p (q n) -> p q n", q=2), v, ALU.mult)\
                    .then_inc(s["yb_done"], 1)
                dve.wait_ge(s["yb_done"], j + 1)
                dve.tensor_tensor(FULL[:, 2 * j:2 * j + 2, :], v, G[:, 2 * j:2 * j + 2, :], ALU.add)\
                    .then_inc(s["mg_full"], 1)
                dve.wait_ge(s["mg_hi"], j + 1)
                dve.tensor_tensor(xlo[:, 2 * j:2 * j + 2, :], FULL[:, 2 * j:2 * j + 2, :], xhi[:, 2 * j:2 * j + 2, :],
                                  ALU.subtract).then_inc(s["mg_lo"], 1)
                mod_weigh(f"mod4_{j}")
                if j:
                    mod_out(f"mod4_{j - 1}")
            mod_out("mod4_3")

            def diagonal(n, at, sem):
                for k in range(KD):
                    ins = dve.tensor_scalar(full2[:, n * D + k * P:n * D + (k + 1) * P], ident, mod2[:, at + k:at + k + 1], -1.0,
                                            ALU.mult, ALU.mult)
                ins.then_inc(sem, 1)

            dve.wait_ge(s["mod_out"], 24)
            dve.wait_ge(s["mg_lo"], 4)
            diagonal(0, 0, s["diag"])
            diagonal(1, 24, s["diag"])
            chain(dve.scalar_tensor_tensor(gainA[:, 2, :], mod2[:, 16:24], 1.0, vec("norm2_g", 8), ALU.add, ALU.mult))
            splits_to(SPLIT["wout"] + 4)

            def residual(name, gate, first, sem):
                for t in range(TT):
                    for b in range(2):
                        i = ACC[name] + 2 * t + b
                        bank_ready(i)
                        dve.tensor_tensor(XN[:, t, b * 512:(b + 1) * 512], accb(i),
                                          bc[:, gate, b * 512:(b + 1) * 512], ALU.mult).then_inc(s["res_y"], 1)
                    dve.wait_ge(s["res_y"], first + 2 * t + 2)
                    dve.tensor_tensor(X[:, t, :], X[:, t, :], XN[:, t, :], ALU.add).then_inc(sem, 1)

            dve.wait_ge(s["g1b_done"], 2)
            splits_to(SPLIT["up0"] + 3)
            residual("wout", 0, 0, s["res1"])
            dve.wait_ge(s["res1"], 2)
            norm(2, X)
            scale_tokens(2, X)
            x_lo(2, gainA[:, 2, :], lambda k: mod2[:, 8 + k:9 + k], xhi, xlo)
            splits_to(SPLIT["up0"] + 4)

            def ffn_up(n):
                si, i, c = SPLIT[f"up{n}"], ACC[f"up{n}"], CHUNK[f"up{n}"]
                assert n_split[0] == si + 4
                pairs = NPAIR * n

                def ahead(m, o):
                    split((si + o) % NR, (c + o) % NR, si + o + 5 + 4 * m)

                def pair(m, q, more):
                    j = 2 * m + q
                    g, u = i + 2 * q, i + 2 * q + 1
                    if n == 0:
                        for tap, (dst, sr) in enumerate((((1, T), (0, T - 1)), ((0, T - 1), (1, T)))):
                            for o in range(2):
                                if tap == 0:
                                    dve.wait_ge(s["cv_act"], 2 * j + 2)
                                else:
                                    dve.wait_ge(s["cv_dve"], 4 * j + o + 1)
                                at = half(XN, q)[:, o * T + dst[0]:o * T + dst[1]]
                                ins = dve.scalar_tensor_tensor(
                                    at, acc[:, g % NR, o * T + sr[0]:o * T + sr[1]],
                                    vt[:, 2, bass.ds(2 * tap * KF + 2 * j + o, 1)], at, ALU.mult, ALU.add)
                                ins.then_inc(s["cv_dve"], 1)
                    if more:
                        ahead(m, 2 * q)
                    dve.wait_ge(s["glu_act"], pairs + j + 1)
                    dve.wait_ge(s["acc_ready"], u + 4 * m + 1)
                    dve.tensor_tensor(half(FULL, q), accb(u), half(XN, 2 + q), ALU.mult).then_inc(s["h_full"], 1)
                    if more:
                        ahead(m, 2 * q + 1)
                    dve.wait_ge(s["h_hi"], pairs + j + 1)
                    dve.tensor_tensor(hlo[:, bass.ds(2 * j, 2), :], half(FULL, q).rearrange("p (o n) -> p o n", o=2),
                                      hhi[:, bass.ds(2 * j, 2), :], ALU.subtract).then_inc(s["h_lo"], 1)

                with dve.Fori(0, 5) as m:
                    for q in range(2):
                        pair(m, q, True)
                n_split[0] = si + 24
                pair(5, 0, False)

            ffn_up(0)
            splits_to(SPLIT["up1"] + 3)
            dve.wait_ge(s["g2b_done"], 2)
            residual("down0", 1, 4, s["res2"])
            dve.wait_ge(s["fgain"], 16)
            for t in range(TT):
                dve.wait_ge(s["fin_ri"], t + 1)
                dve.scalar_tensor_tensor(X[:, t, :], X[:, t, :], fri[:, t:t + 1], bc[:, 2, :], ALU.mult, ALU.mult)\
                    .then_inc(s["fin_x"], 1)
            dve.wait_ge(s["fin_x"], 2)
            norm(3, X)
            scale_tokens(3, X)
            x_lo(3, vec("g_ffn1_pre_2", 8), None, xhi, xlo)
            splits_to(SPLIT["up1"] + 4)
            ffn_up(1)

            def post(m, name, gain, factor):
                dve.wait_ge(s["fgain"], 16 * (m + 2))
                for t in range(TT):
                    dve.wait_ge(s["f_ri"], TT * m + t + 1)
                    for b in range(2):
                        i = ACC[name] + 2 * t + b
                        dve.scalar_tensor_tensor(XN[:, t, b * 512:(b + 1) * 512], accb(i), fri[:, t:t + 1],
                                                 bc[:, gain, b * 512:(b + 1) * 512], ALU.mult, ALU.mult)\
                            .then_inc(s["f_y"], 1)
                    dve.wait_ge(s["f_y"], 4 * m + 2 * t + 2)
                    dve.scalar_tensor_tensor(X[:, t, :], XN[:, t, :], factor, X[:, t, :], ALU.mult, ALU.add).then_inc(s["f_x"], 1)

            splits_to(SPLIT["qa"] + 3)
            post(0, "down1", 0, 0.5)
            dve.wait_ge(s["f_x"], 2)
            norm(4, X)
            scale_tokens(4, X)
            x_lo(4, vec("g_mix_pre_2", 8), None, xhi, xlo)
            splits_to(SPLIT["qa"] + 4)

            dve.wait_ge(s["table_in"], 16)
            tin = MX[:, :, :].rearrange("p a b -> p (a b)").rearrange("p (h n) -> p h n", h=H2)
            chain(dve.memset(tin[0:64, :, 0:64], -1e30))
            for h in range(H2):
                dve.tensor_copy(toe[:, h, 0:P], tin[:, h, P - 1::-1])
                ins = dve.tensor_copy(toe[:, h, P:SC], tin[:, h, ::-1])
            chain(ins)

            ez = xn2[:, 0:GH * SC].rearrange("p (h n) -> p h n", h=GH)
            sp4 = full2[:, 0:GH * SC].rearrange("p (h n) -> p h n", h=GH)

            def stick_softplus(g):
                for h in range(GH):
                    dve.wait_ge(s["z_ln"], GH * g + h + 1)
                    dve.scalar_tensor_tensor(sp4[:, h, :], tp[:, h, 0:SC], 0.0, ez[:, h, :], ALU.max, ALU.add)\
                        .then_inc(s["sp_raw"], 1)

            def heads_out(i, g, base, recips, sem):
                bank_ready(i)
                for t in range(TT):
                    dst = MX[:, t, base + g * T:base + (g + 1) * T]
                    ps = acc[:, i % NR, t * T:(t + 1) * T]
                    if recips is None:
                        ins = dve.tensor_copy(dst, ps)
                    else:
                        r = recips[:, 8 * t + g * GH:8 * t + g * GH + GH].rearrange("p (h d) -> p h d", d=1)
                        ins = dve.tensor_tensor(dst.rearrange("p (h d) -> p h d", h=GH),
                                                ps.rearrange("p (h d) -> p h d", h=GH),
                                                r.broadcast_to([P, GH, HD2]), ALU.mult)
                ins.then_inc(s[sem], 1)
                dve.wait_ge(s[sem], g + 1)

            splits_to(SPLIT["va"] + 1)
            splits_to(SPLIT["qb"] + 2)
            splits_to(SPLIT["kb"] + 1)
            stick_softplus(0)
            splits_to(SPLIT["kb"] + 2)
            heads_out(ACC["stick0"], 0, 0, None, "stick_o")
            splits_to(SPLIT["vb"] + 1)
            stick_softplus(1)
            splits_to(SPLIT["vb"] + 2)
            heads_out(ACC["stick1"], 1, 0, None, "stick_o")
            bz = full2[:, 0:2 * SC].rearrange("p (b n) -> p b n", b=2)

            def band_bias(h):
                dve.wait_ge(s["b_ps"], h + 1)
                if h >= 2:
                    dve.wait_ge(s["b_exp"], h - 1)
                chain(dve.tensor_tensor(bz[:, h % 2, :], tp[:, h % 2, 0:SC], toe[:, h, :], ALU.add))
                for t, (lo, hi) in enumerate(((0, P), (P, SC))):
                    dve.tensor_reduce(bmax[:, 2 * h + t:2 * h + t + 1], bz[:, h % 2, lo:hi], AX, ALU.max,
                                      negate=True).then_inc(s["b_z"], 1)

            def group_norm(i):
                for t in range(TT):
                    at = MX[:, t, i * W2:(i + 1) * W2]
                    dve.tensor_tensor_reduce(full2[:, 1024:1024 + W2], at, at, 1.0, 0.0, ALU.mult, ALU.add,
                                             mss[:, 2 * i + t:2 * i + t + 1]).then_inc(s["mx_ss"], 1)
                    dve.wait_ge(s["mx_ss"], 2 * i + t + 1)

            for h in range(H2):
                band_bias(h)
                if h % 2 == 0:
                    splits_to(SPLIT["wout2"] + h // 2)
                if h % GH == GH - 1:
                    g = h // GH
                    dve.wait_ge(s["b_exp"], h + 1)
                    for t in range(TT):
                        r = slice(8 * t + g * GH, 8 * t + g * GH + GH)
                        ins = dve.reciprocal(brec[:, r], bsum[:, r])
                    chain(ins)
                if h == GH - 1:
                    group_norm(0)
                if h == GH + 1:
                    heads_out(ACC["band0"], 0, W2, brec, "band_o")
            splits_to(SPLIT["wout2"] + 4)
            heads_out(ACC["band1"], 1, W2, brec, "band_o")
            group_norm(1)
            for t in range(TT):
                for i in range(2):
                    dve.wait_ge(s["mx_ri"], 2 * i + t + 1)
                    at = MX[:, t, i * W2:(i + 1) * W2]
                    ins = dve.tensor_scalar(at, at, mri[:, 2 * i + t:2 * i + t + 1], None, ALU.mult)
                ins.then_inc(s["xn_ready"], 1)
            x_lo(5, vec("g_out_sb_2", 8), None, xhi, xlo)
            splits_to(SPLIT["up2"] + 3)
            post(1, "wout2", 1, 1.0)
            dve.wait_ge(s["f_x"], 4)
            norm(5, X)
            for t in range(TT):
                dve.wait_ge(s["ri_ready"], TT * 5 + t + 1)
                dve.tensor_scalar(XN[:, t, :], X[:, t, :], ri[:, t:t + 1], None, ALU.mult)\
                    .then_inc(s["xn_ready"], 1)
            x_lo(6, vec("g_ffn2_pre_2", 8), None, xhi, xlo)
            splits_to(SPLIT["up2"] + 4)
            ffn_up(2)
            dve.wait_ge(s["p_ps"], 1)
            dve.tensor_copy(FULL[:, 4:6, :], tp[:, 0, :].rearrange("p (k n) -> p k n", k=2)).then_inc(s["p_full"], 1)
            dve.wait_ge(s["pt_hi"], 1)
            dve.tensor_tensor(plo[:, :, :], FULL[:, 4:6, :], phi[:, :, :], ALU.subtract).then_inc(s["pt_lo"], 1)
            splits_to(SPLIT["gate"] + 3)
            post(2, "down2", 2, 0.5)
            dve.wait_ge(s["f_x"], 6)
            for q in range(4):
                i = ACC["proj"] + q
                bank_ready(i)
                dve.tensor_copy(MX[:, q // 2, (q % 2) * 512:(q % 2 + 1) * 512], accb(i))\
                    .then_inc(s["pw_done"], 1)
            splits_to(SPLIT["gate"] + 4)
            x_lo(7, None, None, xhi, xlo)
            for j in range(2 * TT):
                dve.wait_ge(s["gate_s"], j + 1)
                dve.tensor_tensor(half(XN, j), half(XN, j), MX[:, j // 2, (j % 2) * 512:(j % 2 + 1) * 512], ALU.mult)\
                    .then_inc(s["e_y"], 1)
            dve.wait_ge(s["fgain"], 16 * 5)
            for t in range(TT):
                dve.wait_ge(s["f_ri"], TT * 3 + t + 1)
                chain(dve.scalar_tensor_tensor(XN[:, t, :], XN[:, t, :], fri[:, t:t + 1], bc[:, 1, :], ALU.mult,
                                               ALU.mult))
                dve.tensor_tensor(X[:, t, :], XN[:, t, :], X[:, t, :], ALU.add)\
                    .then_inc(s["out_x"], 1)


def constants():
    k = np.zeros((P, C_END), np.float32)
    k[:, C_ID:C_ID + P] = np.eye(P)
    k[:, C_TRI:C_TRI + P] = -np.tril(np.ones((P, P)))
    k[:, C_NEG:C_NEG + P] = -1.0
    k[:, C_AVG:C_AVG + P] = 1.0 / CD
    half_, grid = HD // 2, 64
    inv = (np.float32(10000.0) ** (-np.arange(0, half_, 2, dtype=np.float32) / np.float32(half_))).astype(np.float32)
    pos = np.arange(T)
    ang = np.concatenate([(pos // grid).astype(np.float32)[:, None] * inv,
                          (pos % grid).astype(np.float32)[:, None] * inv], axis=-1)
    for t in range(TT):
        at = ang[t * P:(t + 1) * P]
        k[:, C_COS + t * HD:C_COS + (t + 1) * HD] = np.repeat(np.cos(at), 2, axis=1)
        sin = np.repeat(np.sin(at), 2, axis=1)
        sin[:, 0::2] *= -1.0
        k[:, C_SIN + t * HD:C_SIN + (t + 1) * HD] = sin
    return k


SHAPES = {"x": (T, D), "ctx": (T, D), "c": (D,), "c_ctx": (D,), "w_mod": (D, 6 * D), "b_mod": (6 * D,),
          "norm1_g": (D,), "w_in": (D, 4608), "q_norm_g": (HD,), "k_norm_g": (HD,), "w_attn_out": (D, D),
          "conv_dw_w": (TAPS, CD), "conv_dw_b": (CD,), "conv_ln_g": (CD,), "conv_ln_b": (CD,),
          "w_conv_out": (CD, D), "w_out": (D, D), "norm2_g": (D,), "w_up": (D, 2 * F), "ffn_dw_w": (3, F),
          "ffn_dw_b": (F,), "w_down": (F, D), "final_g": (D,), "p_2": (T, 256), "g_ffn1_pre_2": (D,),
          "g_ffn1_post_2": (D,), "w_ffn1_gate_2": (D, F), "w_ffn1_up_2": (D, F), "w_ffn1_down_2": (F, D),
          "g_mix_pre_2": (D,), "g_mix_post_2": (D,), "w_in_2": (D, 6 * W2), "g_out_sb_2": (W2,),
          "g_out_ch_2": (W2,), "w_out_2": (D, D), "g_ffn2_pre_2": (D,), "g_ffn2_post_2": (D,),
          "w_ffn2_gate_2": (D, F), "w_ffn2_up_2": (D, F), "w_ffn2_down_2": (F, D), "w_ple_proj_2": (256, D),
          "w_ple_gate_2": (D, D), "g_ple_post_2": (D,)}


def kernel(**inputs):
    import concourse.bacc as bacc
    from concourse.bass_utils import run_bass_kernel_spmd

    nc = bacc.Bacc("TRN2", target_bir_lowering=False, num_devices=1)
    arrays = {name: np.ascontiguousarray(inputs[name]).reshape(shape) for name, shape in SHAPES.items()}
    rel = np.ascontiguousarray(inputs["rel_bias_2"])[0]
    arrays["bias"] = np.pad(rel[:, 1:], ((0, 0), (0, 2 * T - 2 * P + P - 1)), mode="edge")
    arrays["consts"] = constants()
    aps = {name: nc.dram_tensor(f"in_{name}", v.shape, mybir.dt.from_np(v.dtype), kind="ExternalInput").ap()
           for name, v in arrays.items()}
    aps["out"] = nc.dram_tensor("out_0", (T, D), F32, kind="ExternalOutput").ap()
    build(nc, aps)
    r = run_bass_kernel_spmd(nc, [{f"in_{name}": v for name, v in arrays.items()}], core_ids=[0])
    return r.results[0]["out_0"].reshape(1, T, D)
```

```python
from contextlib import ExitStack

import numpy as np

import concourse.bass as bass
from concourse import mybir

P = 128
D = 1024
KD = D // P
T = 256
TT = T // P
HD = 128
NH = 8
NKV = 2
CD = 512
KC = CD // P
TAPS = 31
KP = 2
PAD = TAPS // 2
F = 2816
KF = F // P
NPAIR = KF // 2
H2 = 8
HD2 = 64
W2 = H2 * HD2
EPS = 1e-6
CH = 2048
NR = 4
SC = 3 * P
GH = 4

F32 = mybir.dt.float32
F32R = mybir.dt.float32r
ALU = mybir.AluOpType
ACT = mybir.ActivationFunctionType
AX = mybir.AxisListType.X

VROWS = [("norm1_g", 8), ("norm2_g", 8), ("g_ffn1_pre_2", 8), ("g_mix_pre_2", 8), ("g_out_sb_2", 4),
         ("g_out_ch_2", 4), ("g_ffn2_pre_2", 8), ("conv_dw_b", 4), ("conv_ln_g", 4), ("conv_ln_b", 4),
         ("b_mod", 48), ("c", 8), ("c_ctx", 8)]
VAT = {}
_n = 0
for _name, _rows in VROWS:
    VAT[_name] = _n
    _n += _rows
assert _n <= P

C_ID, C_TRI, C_NEG, C_AVG, C_COS, C_SIN, C_END = 0, 128, 256, 384, 512, 768, 1024

STAGES = [("mod1", 8, 8), ("q", 4, 4), ("u", 4, 4), ("kv", 2, 4), ("g0", 1, 1), ("g1", 1, 1)]
for _h in range(NH):
    if _h:
        STAGES += [(f"pv{_h - 1}", 0, 1), (f"sum_mod2_{_h - 1}", 0, 1)]
    if _h + 2 < NH:
        STAGES.append((f"g{_h + 2}", 1, 1))
    STAGES.append((f"mod2_{_h}", 1, 0))
STAGES += [("pv7", 0, 1), ("sum_mod2_7", 0, 1)]
for _j in range(4):
    if _j:
        STAGES.append((f"sum_mod3_{_j - 1}", 0, 1))
    STAGES += [(f"attnout{_j}", 1, 1), (f"mod3_{_j}", 1, 0)]
STAGES += [("sum_mod3_3", 0, 1), ("convout", 2, 4), ("g1b", 0, 2), ("wout", 4, 4), ("up0", 22, 22)]
STAGES += [("down0", 4, 4), ("mod4_0", 1, 0), ("down0.4", 1, 0), ("mod4_1", 1, 0), ("down0.5", 1, 0),
           ("mod4_2", 1, 0), ("down0.6", 1, 0), ("mod4_3", 1, 0), ("down0.7", 4, 0)]
STAGES += [("up1", 22, 22), ("down1", 11, 4)]
STAGES += [("qa", 2, 2), ("ka", 2, 2), ("va", 2, 2), ("qb", 2, 2), ("stick0", 0, 1), ("kb", 2, 2),
           ("vb", 2, 2), ("stick1", 0, 1), ("band0", 0, 1), ("band1", 0, 1), ("wout2", 4, 4),
           ("up2", 22, 22), ("proj", 1, 0), ("down2", 11, 4), ("gate", 4, 4)]
MOD1 = [0, 2, 1, 4, 3, 5, 6, 7]
MOD1_DVE = [1, 3, 5, 6, 7]
CHUNK, SPLIT, ACC = {}, {}, {}
_c = _s = _a = 0
for _name, _nc, _na in STAGES:
    CHUNK[_name], SPLIT[_name], ACC[_name] = _c, _s, _a
    _c += _nc
    _a += _na
    if not _name.startswith("mod"):
        _s += _nc
N_SPLIT = _s
MODS = [n for n, _, _ in STAGES if n.startswith("mod") and n != "mod1"]
TOKEN_STAGES = ("q", "kv", "wout", "down1", "va", "vb", "wout2", "down2", "gate")
USED = []
_u = 0
for _name, _nc, _na in STAGES:
    if _name.startswith("mod"):
        continue
    _runs = 2 if _name == "q" else 1
    for _j in range(_nc):
        _per = _nc // _runs
        if _name == "down0.7" and _j == _nc - 1:
            USED.append(("acc_ready", ACC["down0"] + 4))
        elif _name.startswith("down0") or _name == "proj":
            _u += 1
            USED.append(("chunk_used", _u))
        elif _name in TOKEN_STAGES:
            if _j % _per == _per - 1:
                USED.append(("acc_ready", ACC[_name] + _na // _runs * (_j // _per + 1)))
            else:
                _u += 1
                USED.append(("chunk_used", _u))
        else:
            USED.append(("acc_ready", ACC[_name] + _na // _nc * (_j + 1)))
FREED = {}


def _freed(stage, sem, first):
    n = {st[0]: st[2] for st in STAGES}[stage]
    for j in range(n):
        FREED[ACC[stage] + j] = (sem, first + j)


_freed("mod1", "mod_out", 1)
_freed("q", "q_norm", 1)
_freed("kv", "q_norm", 5)
for _j in range(4):
    FREED[ACC["u"] + _j] = ("conv_in", _j // 2 + 1)
for _h in range(NH):
    _freed(f"pv{_h}", "a_lo", _h + 1)
    _freed(f"g{_h}", "g_raw", _h + 1)
_freed("convout", "yb_done", 1)
for _j in range(4):
    _freed(f"attnout{_j}", "ya_done", _j + 1)
for _j, _name in enumerate(MODS[:12]):
    _freed("sum_" + _name, "mod_out", 9 + _j)
_freed("g1b", "g1b_done", 1)
_freed("wout", "res_y", 1)
_freed("down0", "res_y", 5)
for _n in range(3):
    for _j in range(22):
        FREED[ACC[f"up{_n}"] + _j] = ("h_full", NPAIR * _n + _j // 2 + 1)
for _n, _name in enumerate(("down1", "wout2", "down2")):
    _freed(_name, "f_y", 4 * _n + 1)
for _n, _name in enumerate(("qa", "ka", "qb", "kb")):
    _freed(_name, "qk2", 2 * _n + 1)
_freed("va", "v2", 1)
_freed("vb", "v2", 3)
for _n in range(2):
    _freed(f"stick{_n}", "stick_o", _n + 1)
    _freed(f"band{_n}", "band_o", _n + 1)
_freed("gate", "gate_s", 1)
for _name in ("wout", "down0", "down1", "wout2", "down2", "gate"):
    assert ACC[_name] % 2 == 0, _name

SEMS = """hi_done lo_done mod_acc weigh chunk_used acc_ready const_in vec_in x_in ctx_in p_in gain_in table_in
pads vec_ps vec_sb silu_c mod_out affine1 affine1c tables
ss_ready ri_ready xn_ready xt_ps shift_dve xhi xlo
q_ss v_done q_ri q_norm q_rot q_tps q_t
glu_sig conv_in conv_out conv_dve ln_mean ln_c ln_sq ln_var ln_ve ln_r ln_diag ln_bc ln_n ln_y ln_hi ln_lo
sc_ready nm_ready p_exp p_scaled pt_ps pt_done a_hi a_lo g_raw g_sig yb_done ya_done mg_full mg_hi mg_lo
diag g1b_done g2b_ps g2b_done mod4_ps res_y res1 res2 cv_act cv_dve glu_act h_full h_hi h_lo
fin_ss fin_ri fin_x f_ss f_ri f_y f_x fgain
qk2 v2 z_ps z_abs z_exp z_ln sp_raw sp_ready arg_ready a_raw a_ready stick_o
b_ps b_z b_exp b_tps b_t band_o mx_ss mx_ri mx_scaled
p_ps pt_hi pt_lo pw_done gate_s e_y out_x dve_chain pool_chain out_done""".split()


def build(nc, a):
    ctx = ExitStack()
    with ctx:
        def sb(name, shape, dt=F32, where=ctx):
            return where.enter_context(nc.sbuf_tensor(name, shape, dt))

        raw = [sb(f"raw{i}", [P, CH]) for i in range(NR)]
        whi = [sb(f"whi{i}", [P, CH], F32R) for i in range(NR)]
        wlo = [sb(f"wlo{i}", [P, CH], F32R) for i in range(NR)]
        X = sb("X", [P, TT, D])
        XN = sb("XN", [P, TT, D])
        FULL = sb("FULL", [P, KD, T])
        xhi = sb("x_hi", [P, KD, T], F32R)
        xlo = sb("x_lo", [P, KD, T], F32R)
        consts = sb("consts", [P, C_END])
        vt = sb("vt", [P, 3, P])
        sct = sb("sct", [P, KD, 2])
        modv = sb("modv", [P, 16, 2])
        mod2 = sb("mod2", [P, 32])
        gainA = sb("gainA", [P, 3, KD])
        small = sb("small", [P, 160])
        ss, ri = small[:, 0:2], small[:, 2:4]
        fss, fri = small[:, 4:6], small[:, 6:8]
        qss, qri = small[:, 8:40], small[:, 40:72]
        nmax, psum_, prec = small[:, 72:74], small[:, 74:76], small[:, 76:78]
        bmax, bsum, brec = small[:, 80:96], small[:, 96:112], small[:, 112:128]
        mss, mri = small[:, 128:132], small[:, 132:136]
        minus_half = small[:, 136:137]
        fss2 = small[:, 140:144]
        lnv = small[:, 138:140]
        modacc = sb("modacc", [P, 2, 256])

        ph1 = ExitStack()
        QT = sb("QT", [P, NH, T], F32, ph1)
        KT = sb("KT", [P, NKV, 2 * T], F32, ph1)
        V = sb("V", [P, 4, NKV * HD], F32, ph1)
        G = sb("G", [P, 16, T], F32, ph1)
        conv_x = sb("conv_x", [P, KC, T + 2 * PAD], F32, ph1)
        side_hi = sb("side_hi", [P, KD, T], F32R, ph1)
        side_lo = sb("side_lo", [P, KD, T], F32R, ph1)
        cvt_hi = sb("cvt_hi", [P, KC, T], F32R, ph1)
        cvt_lo = sb("cvt_lo", [P, KC, T], F32R, ph1)
        rope = G[:, 8:13, :]
        ph1.close()
        bc = sb("bc", [P, 3, D])
        ph2 = ExitStack()
        hhi = sb("h_hi", [P, KF, T], F32R, ph2)
        hlo = sb("h_lo", [P, KF, T], F32R, ph2)
        phi = sb("p_hi", [P, 2, T], F32R, ph2)
        plo = sb("p_lo", [P, 2, T], F32R, ph2)
        ph2.close()
        ph3 = ExitStack()
        qk2t = [sb(f"qk2_{n}", [P, H2 // 2, T], F32, ph3) for n in ("qa", "ka", "qb", "kb")]
        v2t = [sb(f"v2_{n}", [P, TT, W2], F32, ph3) for n in "ab"]
        toe = sb("toe", [P, H2, SC], F32, ph3)
        MX = sb("MX", [P, TT, D], F32, ph3)
        ph3.close()

        acc = ctx.enter_context(nc.psum_tensor("acc", [P, NR, 512], F32))
        tp = ctx.enter_context(nc.psum_tensor("tp", [P, 4, 512], F32))
        s = {n: ctx.enter_context(nc.semaphore(n)) for n in SEMS}
        landed = [ctx.enter_context(nc.semaphore(f"landed{i}")) for i in range(NR)]

        ident = consts[:, C_ID:C_ID + P]
        negtri = consts[:, C_TRI:C_TRI + P]
        negone = consts[:, C_NEG:C_NEG + P]
        avg = consts[:, C_AVG:C_AVG + P]

        def vec(name, n, off=0):
            at = VAT[name] + off
            return vt[:, 0, at:at + n]

        def accb(i):
            return acc[:, i % NR, :]

        def half(buf, t):
            flat = buf[:, :, :].rearrange("p a b -> p (a b)")
            return flat[:, t * 512:(t + 1) * 512]

        full2 = FULL[:, :, :].rearrange("p a b -> p (a b)")
        xn2 = XN[:, :, :].rearrange("p a b -> p (a b)")

        def mod1_acc(n):
            return half(FULL, n) if n < 4 else modacc[:, :, :].rearrange("p a b -> p (a b)")

        def cols(w, k, c0, n):
            return w[0:k * P, c0:c0 + n].rearrange("(k p) n -> p k n", p=P)

        def rows(w, r, k):
            return w[r * P:(r + k) * P, :].rearrange("(k p) n -> p k n", p=P)

        def deep(w, r, c0):
            return w[r * P:(r + 4) * P, c0:c0 + 512].rearrange("(k p) n -> p k n", p=P)

        w_in, w_in2, w_mod = a["w_in"], a["w_in_2"], a["w_mod"]
        QKV = NH * HD
        U0, G0 = QKV + 2 * NKV * HD, QKV + 2 * NKV * HD + 2 * CD
        src = {"mod1": [cols(w_mod, 8, 256 * j, 256) for j in range(8)],
               "q": [deep(w_in, 4 * r, 512 * b) for b in range(2) for r in range(2)],
               "kv": [deep(w_in, 4 * r, QKV) for r in range(2)],
               "u": [cols(w_in, 8, U0 + CD * h + 256 * j, 256) for j in range(2) for h in range(2)],
               "convout": [cols(a["w_conv_out"], 4, 512 * j, 512) for j in range(2)],
               "wout": [rows(a["w_out"], 2 * r, 2) for r in range(4)],
               "qa": [cols(w_in2, 8, 256 * j, 256) for j in range(2)],
               "ka": [cols(w_in2, 8, W2 + 256 * j, 256) for j in range(2)],
               "va": [deep(w_in2, 4 * r, 2 * W2) for r in range(2)],
               "qb": [cols(w_in2, 8, 3 * W2 + 256 * j, 256) for j in range(2)],
               "kb": [cols(w_in2, 8, 4 * W2 + 256 * j, 256) for j in range(2)],
               "vb": [deep(w_in2, 4 * r, 5 * W2) for r in range(2)],
               "wout2": [rows(a["w_out_2"], 2 * r, 2) for r in range(4)],
               "proj": [rows(a["w_ple_proj_2"], 0, 2)],
               "gate": [rows(a["w_ple_gate_2"], 2 * r, 2) for r in range(4)]}
        for j in range(NH):
            src[f"g{j}"] = [cols(w_in, 8, G0 + 256 * j, 256)]
            src[f"mod2_{j}"] = [cols(w_mod, 8, 2048 + 256 * j, 256)]
        for j in range(4):
            src[f"attnout{j}"] = [cols(a["w_attn_out"], 8, 256 * j, 256)]
            src[f"mod3_{j}"] = [cols(w_mod, 8, 4096 + 256 * j, 256)]
            src[f"mod4_{j}"] = [cols(w_mod, 8, 5120 + 256 * j, 256)]
        glu = [((a["w_up"], 0), (a["w_up"], F)), ((a["w_ffn1_gate_2"], 0), (a["w_ffn1_up_2"], 0)),
               ((a["w_ffn2_gate_2"], 0), (a["w_ffn2_up_2"], 0))]
        down = [a["w_down"], a["w_ffn1_down_2"], a["w_ffn2_down_2"]]
        for n in range(3):
            src[f"down{n}"] = [rows(down[n], 2 * r, min(2, KF - 2 * r)) for r in range(11)]
        for r in range(4, 8):
            src[f"down0.{r}"] = src["down0"][r:]
        kind = []
        for name, n, _ in STAGES:
            for j in range(n):
                if name == "mod1":
                    kind.append(("mod_acc", MOD1_DVE.index(j) + 1) if j in MOD1_DVE
                                else ("acc_ready", ACC[name] + MOD1.index(j) + 1))
                elif name in MODS:
                    kind.append(("mod_acc", len(MOD1_DVE) + 1 + MODS.index(name)))
                else:
                    kind.append(("lo_done", SPLIT[name] + j + 1))

        def slot_split(splits_to, h):
            if h < 5:
                splits_to(SPLIT["g2"] + h + 2)
            elif h == 7:
                splits_to(SPLIT["attnout0"] + 1)

        block = ctx.enter_context(nc.Block())

        @block.sync
        def _(sp):
            def slot_free(c):
                if c >= NR:
                    sem, value = kind[c - NR]
                    sp.wait_ge(s[sem], value)

            sp.wait_ge(s["pads"], 1)
            for name, n in VROWS:
                at = VAT[name]
                sp.dma_start(full2[at:at + n, 0:P], a[name].rearrange("(k p) -> k p", p=P)).then_inc(s["vec_in"], 16)
            for name, n, _ in STAGES:
                c0 = CHUNK[name]
                if not name.startswith("up"):
                    for j in range(n):
                        slot_free(c0 + j)
                        w = src[name][j]
                        sp.dma_start(raw[(c0 + j) % NR][:, :].rearrange("p (k n) -> p k n", k=w.shape[1]), w)\
                            .then_inc(landed[(c0 + j) % NR], 16)
                    continue
                halves = glu[int(name[2:])]

                def pair_load(j, q):
                    w, first = halves[q % 2]
                    sp.dma_start(raw[(c0 + q) % NR][:, :].rearrange("p (k n) -> p k n", k=8),
                                 w[:, bass.ds(first + 256 * j, 256)].rearrange("(k p) n -> p k n", p=P))\
                        .then_inc(landed[(c0 + q) % NR], 16)

                for q in range(4):
                    slot_free(c0 + q)
                    pair_load(q // 2, q)
                with sp.Fori(1, 5) as m:
                    for q in range(4):
                        sp.wait_ge(s["lo_done"], SPLIT[name] + 4 * m + q - NR + 1)
                        pair_load(2 * m + q // 2, q)
                for q in range(2):
                    slot_free(c0 + 20 + q)
                    pair_load(10, q)

        @block.gpsimd
        def _(pool):
            n_chain = [0]

            def chain(ins):
                n_chain[0] += 1
                ins.then_inc(s["pool_chain"], 1)
                pool.wait_ge(s["pool_chain"], n_chain[0])

            def bcast(v, n):
                return v.rearrange("(a n) -> a n", a=1).broadcast_to([P, n])

            chain(pool.memset(minus_half, -0.5))
            chain(pool.memset(conv_x[:, :, 0:PAD], 0.0))
            chain(pool.memset(conv_x[:, :, T + PAD:T + 2 * PAD], 0.0))
            pool.dma_start(rope[:, 4, 0:HD], bcast(a["k_norm_g"], HD)).then_inc(s["gain_in"], 16)
            pool.dma_start(rope[:, 4, HD:2 * HD], bcast(a["q_norm_g"], HD)).then_inc(s["gain_in"], 16)
            pool.wait_ge(s["gain_in"], 32)
            pool.wait_ge(s["const_in"], 16)
            for w, gat, factor in ((0, HD, float(HD) ** -0.5), (2, 0, 1.0)):
                g_ = rope[:, 4, gat:gat + HD]
                gsw = g_.rearrange("p (i two) -> p i two", two=2)[:, :, ::-1]
                for t in range(TT):
                    pool.tensor_tensor(rope[:, w, t * HD:(t + 1) * HD], g_,
                                       consts[:, C_COS + t * HD:C_COS + (t + 1) * HD], ALU.mult)
                    chain(pool.tensor_tensor(
                        rope[:, w + 1, t * HD:(t + 1) * HD].rearrange("p (i two) -> p i two", two=2), gsw,
                        consts[:, C_SIN + t * HD:C_SIN + (t + 1) * HD].rearrange("p (i two) -> p i two", two=2),
                        ALU.mult))
                if factor != 1.0:
                    pool.tensor_scalar(rope[:, w:w + 2, :], rope[:, w:w + 2, :], factor, None, ALU.mult)\
                        .then_inc(s["tables"], 1)

            def power(out, sem):
                pool.tensor_tensor(out, out, minus_half.broadcast_to([P, out.shape[1]]), ALU.pow).then_inc(sem, 1)

            def rsqrt(out, in_, width, sem):
                chain(pool.tensor_scalar(out, in_, 1.0 / width, EPS, ALU.mult, ALU.add))
                power(out, sem)

            def norm(n, tiles=(0, 1)):
                for t in tiles:
                    pool.wait_ge(s["ss_ready"], TT * n + t + 1)
                    pool.tensor_tensor(ri[:, t:t + 1], ss[:, t:t + 1], minus_half, ALU.pow).then_inc(s["ri_ready"], 1)

            norm(0)
            norm(1)
            for u in range(8):
                pool.wait_ge(s["q_ss"], u + 1)
                heads = 4 if u < 4 else NKV
                rsqrt(qri[:, 4 * u:4 * u + heads], qss[:, 4 * u:4 * u + heads], HD, s["q_ri"])

            pool.wait_ge(s["conv_in"], 2)
            conv = XN[:, 1, :].rearrange("p (k n) -> p k n", k=KC)[:, KC - KP:KC, :]

            def per_channel(v):
                return v.rearrange("p (k n) -> p k n", n=1).broadcast_to([P, KP, T])

            for i in range(TAPS):
                w = per_channel(vt[:, 1, KC * (i + 1) - KP:KC * (i + 1)])
                x = conv_x[:, KC - KP:KC, i:i + T]
                if i == 0:
                    chain(pool.tensor_tensor(conv, x, w, ALU.mult))
                    chain(pool.tensor_tensor(conv, conv, per_channel(vec("conv_dw_b", KP, KC - KP)), ALU.add))
                    continue
                term = half(XN, i % 2)[:, 0:KP * T].rearrange("p (k n) -> p k n", k=KP)
                chain(pool.tensor_tensor(term, x, w, ALU.mult))
                ins = pool.tensor_tensor(conv, conv, term, ALU.add)
                if i < TAPS - 1:
                    chain(ins)
            ins.then_inc(s["conv_out"], 1)
            pool.wait_ge(s["ln_ve"], 1)
            rsqrt(lnv, lnv, 1, s["ln_r"])

            gains = [0]

            def load_gain(name, slot):
                if gains[0]:
                    pool.wait_ge(s["fgain"], 16 * gains[0])
                pool.dma_start(bc[:, slot, :], bcast(a[name], D)).then_inc(s["fgain"], 16)
                gains[0] += 1

            pool.wait_ge(s["sc_ready"], TT * NH)
            load_gain("final_g", 2)
            norm(2)
            load_gain("g_ffn1_post_2", 0)
            for t in range(TT):
                pool.wait_ge(s["fin_ss"], t + 1)
                pool.tensor_tensor(fri[:, t:t + 1], fss[:, t:t + 1], minus_half, ALU.pow).then_inc(s["fin_ri"], 1)
                norm(3, (t,))
            load_gain("g_mix_post_2", 1)
            load_gain("g_ffn2_post_2", 2)

            def post(m, n=None):
                for t in range(TT):
                    pool.wait_ge(s["f_ss"], 2 * TT * m + 2 * t + 2)
                    chain(pool.tensor_scalar(fri[:, t:t + 1], fss2[:, 2 * t:2 * t + 1], fss2[:, 2 * t + 1:2 * t + 2],
                                             EPS, ALU.add, ALU.add))
                    power(fri[:, t:t + 1], s["f_ri"])
                    if n is not None:
                        norm(n, (t,))

            post(0, 4)
            e = a["bias"]
            windows = bass.AP(e.tensor, 0, [[1, P], [e.shape[1], H2], [1, T]])
            pool.wait_ge(s["acc_ready"], ACC["down1"] + 4)
            pool.dma_start(MX[:, :, :].rearrange("p a b -> p (a b)").rearrange("p (h n) -> p h n", h=H2), windows)\
                .then_inc(s["table_in"], 16)
            pool.dma_start(bc[:, 0, 0:TT * T].rearrange("p (t d) -> p t d", t=TT),
                           a["p_2"].rearrange("(t p) d -> p t d", p=P)).then_inc(s["p_in"], 16)
            sp4 = full2[:, 0:GH * SC].rearrange("p (h n) -> p h n", h=GH)

            def mask(view, sem):
                for blk in (0, 2):
                    v = view[:, :, blk * P:(blk + 1) * P]
                    ins = pool.affine_select(out=v, in_=v, pattern=[[0, GH], [1, P]], compare_op=ALU.is_gt,
                                             fill=0.0, base=0, channel_multiplier=-1)
                ins.then_inc(sem, 1)

            for g in range(2):
                pool.wait_ge(s["sp_raw"], GH * (g + 1))
                mask(sp4, s["sp_ready"])
                pool.wait_ge(s["a_raw"], GH * (g + 1))
                mask(sp4, s["a_ready"])
            for i in range(2):
                for t in range(TT):
                    pool.wait_ge(s["mx_ss"], 2 * i + t + 1)
                    q = 2 * i + t
                    rsqrt(mri[:, q:q + 1], mss[:, q:q + 1], W2, s["mx_ri"])
            post(1, 5)
            load_gain("g_ple_post_2", 1)
            post(2)
            post(3)

        @block.tensor
        def _(pe):
            def chunk_ready(n):
                pe.wait_ge(s["lo_done"], n + 1)

            def bank_free(i):
                if i >= NR:
                    sem, value = FREED[i - NR]
                    pe.wait_ge(s[sem], value)

            def product(out, xh, xl, wh, wl, x_stationary, start, stop):
                if x_stationary:
                    pe.matmul(out, xh, wh, start=start, stop=False)
                    pe.matmul(out, xh, wl, start=False, stop=False)
                    return pe.matmul(out, xl, wh, start=False, stop=stop)
                pe.matmul(out, wh, xh, start=start, stop=False)
                pe.matmul(out, wh, xl, start=False, stop=False)
                return pe.matmul(out, wl, xh, start=False, stop=stop)

            def feature_tiles(si, i, xh, xl, kt, bank, n=None):
                w = [r[si % NR][:, :].rearrange("p (k n) -> p k n", k=kt) for r in (whi, wlo)]
                for q in range(2):
                    at = (2 * bank + q) * P
                    for k in range(kt):
                        if n is not None and q == 0 and k % 2 == 0:
                            x_ready(n, k // 2)
                        mm = product(acc[:, i % NR, q * T:(q + 1) * T], xh[:, k, :], xl[:, k, :],
                                     w[0][:, k, at:at + P], w[1][:, k, at:at + P], False, k == 0, k == kt - 1)
                return mm

            def tiles_stage(si, i, xh=xhi, xl=xlo, kt=KD, banks=1, n=None):
                chunk_ready(si)
                for b in range(banks):
                    bank_free(i + b)
                    mm = feature_tiles(si, i + b, xh, xl, kt, b, n)
                    mm.then_inc(s["acc_ready"], 1)

            def token_stage(si0, i0, chunks, kt, nb, stats, total, k_ready=None):
                def ready(c):
                    chunk_ready(si0 + c)
                    if k_ready is not None:
                        k_ready(c)

                def multiply(c, x, order):
                    w = [r[(si0 + c) % NR][:, :].rearrange("p (k n) -> p k n", k=kt) for r in (whi, wlo)]
                    xh, xl, t = stats[x]
                    for k, b in order:
                        kk = c * kt + k
                        if kk == 0:
                            bank_free(i0 + x * nb + b)
                        mm = product(accb(i0 + x * nb + b), xh[:, kk, t * P:(t + 1) * P],
                                     xl[:, kk, t * P:(t + 1) * P], w[0][:, k, b * 512:(b + 1) * 512],
                                     w[1][:, k, b * 512:(b + 1) * 512], True, kk == 0, kk == total - 1)
                        if kk == total - 1:
                            mm.then_inc(s["acc_ready"], 1)
                    return mm

                by_row = [(k, b) for k in range(kt) for b in range(nb)]
                by_bank = [(k, b) for b in range(nb) for k in range(kt)]
                for c in range(chunks - 2):
                    ready(c)
                    for x in range(len(stats)):
                        mm = multiply(c, x, by_row)
                    mm.then_inc(s["chunk_used"], 1)
                ready(chunks - 2)
                for x in range(len(stats)):
                    mm = multiply(chunks - 2, x, by_row)
                    if x == len(stats) - 1:
                        mm.then_inc(s["chunk_used"], 1)
                    if x == 0:
                        ready(chunks - 1)
                    multiply(chunks - 1, x, by_bank)

            def mod_chunk(c, i):
                pe.wait_ge(landed[c % NR], 16 * (c // NR + 1))
                bank_free(i)
                w = raw[c % NR][:, :].rearrange("p (k n) -> p k n", k=8)
                for q in range(2):
                    for k in range(KD):
                        mm = pe.matmul(acc[:, i % NR, 2 * q:2 * q + 2], w[:, k, q * P:(q + 1) * P], sct[:, k, :],
                                       start=(k == 0), stop=(k == KD - 1))
                mm.then_inc(s["acc_ready"], 1)

            def mod_sum(name):
                i, j = ACC["sum_" + name], MODS.index(name)
                pe.wait_ge(s["mod_acc"], len(MOD1_DVE) + 1 + j)
                bank_free(i)
                for q in range(2):
                    mm = pe.matmul(acc[:, i % NR, 2 * q:2 * q + 2], modacc[:, j % 2, q * P:(q + 1) * P], negone[:, 0:2],
                                   start=True, stop=True)
                mm.then_inc(s["acc_ready"], 1)

            def gate2_sum(j):
                pe.wait_ge(s["mod_acc"], len(MOD1_DVE) + 1 + MODS.index(f"mod4_{j}"))
                for q in range(2):
                    mm = pe.matmul(tp[:, 0, 4 * j + 2 * q:4 * j + 2 * q + 2],
                                   modacc[:, MODS.index(f"mod4_{j}") % 2, q * P:(q + 1) * P], negone[:, 0:2],
                                   start=True, stop=True)
                mm.then_inc(s["mod4_ps"], 1)

            def transpose_tokens(n, source, ready="xn_ready", first=None):
                for t in range(TT):
                    pe.wait_ge(s[ready], (TT * n if first is None else first) + t + 1)
                    for k in range(KD):
                        mm = pe.transpose(tp[:, k // 2, (k % 2) * T + t * P:(k % 2) * T + (t + 1) * P],
                                          source[:, t, k * P:(k + 1) * P], ident)
                        if t == TT - 1 and k % 2:
                            mm.then_inc(s["xt_ps"], 1)

            def x_ready(n, b):
                pe.wait_ge(s["xlo"], 4 * n + b + 1)

            x_tiles = [(xhi, xlo, 0), (xhi, xlo, 1)]

            pe.wait_ge(s["const_in"], 16)
            pe.wait_ge(s["vec_in"], 16 * (len(VROWS) + 3))
            pe.wait_ge(s["pads"], 1)
            for r in range(3):
                mm = pe.transpose(tp[:, 3, r * P:(r + 1) * P], full2[:, r * P:(r + 1) * P], ident)
            mm.then_inc(s["vec_ps"], 1)
            pe.wait_ge(s["vec_sb"], 1)
            transpose_tokens(0, XN)
            pe.wait_ge(s["silu_c"], 1)
            for i, j in enumerate(MOD1):
                if j not in MOD1_DVE:
                    mod_chunk(CHUNK["mod1"] + j, ACC["mod1"] + i)
                    continue
                pe.wait_ge(s["mod_acc"], MOD1_DVE.index(j) + 1)
                bank_free(ACC["mod1"] + i)
                for q in range(2):
                    for v in range(2):
                        mm = pe.matmul(accb(ACC["mod1"] + i)[:, 2 * q + v:2 * q + v + 1],
                                       mod1_acc(MOD1_DVE.index(j))[:, v * 256 + q * P:v * 256 + (q + 1) * P],
                                       negone[:, 0:1],
                                       start=True, stop=True)
                mm.then_inc(s["acc_ready"], 1)
            def rope_transposes(u):
                heads = 4 if u < 4 else 2
                pe.wait_ge(s["q_rot"], u + 1)
                if u >= 4:
                    pe.wait_ge(s["q_t"], u - 3)
                for h in range(heads):
                    mm = pe.transpose(tp[:, u % 4, h * P:(h + 1) * P], half(FULL, 2 * (u % 2))[:, h * P:(h + 1) * P], ident)
                mm.then_inc(s["q_tps"], 1)

            for b in range(2):
                token_stage(SPLIT["q"] + 2 * b, ACC["q"] + 2 * b, 2, 4, 1, x_tiles, KD,
                            (lambda c: (x_ready(0, 2 * c), x_ready(0, 2 * c + 1))) if b == 0 else None)
                if b == 0:
                    transpose_tokens(1, XN)
            for j in range(4):
                rope_transposes(j)
                tiles_stage(SPLIT["u"] + j, ACC["u"] + j)
            x_ready(1, 3)
            token_stage(SPLIT["kv"], ACC["kv"], 2, 4, 1, x_tiles + [(side_hi, side_lo, 0), (side_hi, side_lo, 1)], KD)
            for j in range(2):
                tiles_stage(SPLIT[f"g{j}"], ACC[f"g{j}"])
                rope_transposes(4 + j)
            for j in range(2, 4):
                rope_transposes(4 + j)

            def scores(h):
                for t in range(TT):
                    if h == 0:
                        pe.wait_ge(s["q_t"], 8)
                    else:
                        pe.wait_ge(s["p_exp"], TT * (h - 1) + t + 1)
                    pe.matmul(tp[:, t, :], QT[:, h, t * P:(t + 1) * P], KT[:, h // 4, :], start=True, stop=True)\
                        .then_inc(s["sc_ready"], 1)

            def prob_transposes(h):
                for t in range(TT):
                    pe.wait_ge(s["p_scaled"], TT * h + t + 1)
                    if h:
                        pe.wait_ge(s["pt_done"], TT * (h - 1) + t + 1)
                    for k in range(4):
                        mm = pe.transpose(tp[:, 2 + t, k * P:(k + 1) * P], half(FULL, t)[:, k * P:(k + 1) * P], ident)
                    mm.then_inc(s["pt_ps"], 1)

            PT = FULL[:, 4:8, :]

            def values(h):
                i = ACC[f"pv{h}"]
                bank_free(i)
                pe.wait_ge(s["pt_done"], TT * (h + 1))
                if h == 0:
                    pe.wait_ge(s["v_done"], 4)
                for k in range(4):
                    mm = pe.matmul(acc[:, i % NR, 0:T], V[:, k, (h // 4) * HD:(h // 4 + 1) * HD], PT[:, k, :],
                                   start=(k == 0), stop=(k == 3))
                mm.then_inc(s["acc_ready"], 1)

            conv = XN[:, 1, :].rearrange("p (k n) -> p k n", k=KC)
            for h in range(NH):
                scores(h)
                if h:
                    values(h - 1)
                    mod_sum(f"mod2_{h - 1}")
                if h + 2 < NH:
                    tiles_stage(SPLIT[f"g{h + 2}"], ACC[f"g{h + 2}"])
                prob_transposes(h)
            values(NH - 1)
            mod_sum("mod2_7")
            sq = QT[:, 0:4, :]

            def ln_mean():
                pe.wait_ge(s["conv_out"], 1)
                pe.wait_ge(s["conv_dve"], TAPS * (KC - KP))
                pe.wait_ge(s["p_exp"], TT * NH)
                for k in range(KC):
                    mm = pe.matmul(tp[:, 0, 0:T], avg, conv[:, k, :], start=(k == 0), stop=(k == KC - 1))
                mm.then_inc(s["ln_mean"], 1)

            def ln_var():
                pe.wait_ge(s["ln_sq"], 1)
                for t in range(TT):
                    for k in range(KC):
                        mm = pe.matmul(tp[:, 1, t:t + 1], sq[:, k, t * P:(t + 1) * P], avg[:, 0:1], start=(k == 0),
                                       stop=(k == KC - 1))
                mm.then_inc(s["ln_var"], 1)

            def ln_broadcast():
                pe.wait_ge(s["ln_diag"], 1)
                for t in range(TT):
                    mm = pe.matmul(tp[:, 2, t * P:(t + 1) * P], negone, half(XN, 0)[:, t * P:(t + 1) * P], start=True,
                                   stop=True)
                mm.then_inc(s["ln_bc"], 1)

            ln_mean()
            pe.wait_ge(s["a_lo"], NH)
            for j in range(4):
                if j:
                    mod_sum(f"mod3_{j - 1}")
                tiles_stage(SPLIT[f"attnout{j}"], ACC[f"attnout{j}"], side_hi, side_lo)
                if j == 0:
                    ln_var()
                elif j == 1:
                    ln_broadcast()
            mod_sum("mod3_3")
            pe.wait_ge(s["ln_lo"], 1)
            for j in range(2):
                tiles_stage(SPLIT["convout"] + j, ACC["convout"] + 2 * j, cvt_hi, cvt_lo, KC, 2)
            pe.wait_ge(s["diag"], 1)
            for b in range(2):
                bank_free(ACC["g1b"] + b)
                pe.matmul(accb(ACC["g1b"] + b), negone, half(XN, 2 + b), start=True, stop=True)\
                    .then_inc(s["acc_ready"], 1)
            token_stage(SPLIT["wout"], ACC["wout"], 4, 2, 2, x_tiles, KD,
                        lambda c: pe.wait_ge(s["mg_lo"], c + 1))

            def ffn_up(n):
                si, i = SPLIT[f"up{n}"], ACC[f"up{n}"]

                def chunk(m, q, norm=None):
                    pe.wait_ge(s["lo_done"], si + 4 * m + q + 1)
                    if isinstance(m, int) and m == 0:
                        bank_free(i + q)
                    else:
                        pe.wait_ge(s["h_full"], NPAIR * n + 2 * m + q // 2 - 1)
                    w = [r[(si + q) % NR][:, :].rearrange("p (k n) -> p k n", k=KD) for r in (whi, wlo)]
                    for o in range(2):
                        for k in range(KD):
                            if norm is not None and o == 0 and k % 2 == 0:
                                x_ready(norm, k // 2)
                            mm = product(acc[:, (i + q) % NR, o * T:(o + 1) * T], xhi[:, k, :], xlo[:, k, :],
                                         w[0][:, k, o * P:(o + 1) * P], w[1][:, k, o * P:(o + 1) * P], False,
                                         k == 0, k == KD - 1)
                    mm.then_inc(s["acc_ready"], 1)

                for q in range(4):
                    chunk(0, q, (2, 3, 6)[n] if q == 0 else None)
                with pe.Fori(1, 5) as m:
                    for q in range(4):
                        chunk(m, q)
                for q in range(2):
                    chunk(5, q)

            def ffn_down(n):
                token_stage(SPLIT[f"down{n}"], ACC[f"down{n}"], 11, 2, 2, [(hhi, hlo, 0), (hhi, hlo, 1)], KF,
                            lambda c: before_chunk(n, c))

            def before_chunk(n, c):
                pe.wait_ge(s["h_lo"], NPAIR * n + c + 1)
                if n == 0 and 5 <= c < 9:
                    gate2_sum(c - 5)
                if n == 0 and c == 9:
                    pe.wait_ge(s["diag"], 2)
                    for b in range(2):
                        pe.matmul(tp[:, 1 + b, :], negone, half(FULL, b), start=True, stop=True)\
                            .then_inc(s["g2b_ps"], 1)

            transpose_tokens(2, XN)
            ffn_up(0)
            ffn_down(0)
            transpose_tokens(3, XN)
            ffn_up(1)
            ffn_down(1)
            transpose_tokens(4, XN)

            def project2(name, n=None):
                for j in range(2):
                    tiles_stage(SPLIT[name] + j, ACC[name] + j, n=n if j == 0 else None)

            sp4 = full2[:, 0:GH * SC].rearrange("p (h n) -> p h n", h=GH)

            def head2(which, h):
                return qk2t[which][HD2 * (h % 2):HD2 * (h % 2) + HD2, h // 2, :]

            def stick_scores(g):
                pe.wait_ge(s["qk2"], 4)
                if g:
                    pe.wait_ge(s["a_raw"], GH)
                for h in range(GH):
                    q_, k_ = head2(0, g * GH + h), head2(1, g * GH + h)
                    pe.matmul(tp[:, h, 0:T], k_[:, 0:P], q_[:, :], start=True, stop=True, skip_group_check=True)
                    pe.matmul(tp[:, h, T:SC], k_[:, P:T], q_[:, P:T], start=False, stop=True,
                              skip_group_check=True).then_inc(s["z_ps"], 1)

            def stick_sums(g):
                pe.wait_ge(s["sp_ready"], g + 1)
                for h in range(GH):
                    pe.matmul(tp[:, h, 0:SC], negtri, sp4[:, h, :], start=False, stop=True, skip_group_check=True)
                    pe.matmul(tp[:, h, P:T], negone, sp4[:, h, T:SC], start=False, stop=True,
                              skip_group_check=True).then_inc(s["arg_ready"], 1)

            def weigh_values(i, at, vv, h0):
                bank_free(i)
                for h in range(GH):
                    w, v = at(h), vv[:, :, (h0 + h) * HD2:(h0 + h + 1) * HD2]
                    o = acc[:, i % NR, :]
                    pe.matmul(o[:, h * HD2:(h + 1) * HD2], w[:, 0:P], v[:, 0, :], start=True, stop=True)
                    pe.matmul(o[:, T + h * HD2:T + (h + 1) * HD2], w[:, P:T], v[:, 0, :], start=True, stop=False)
                    mm = pe.matmul(o[:, T + h * HD2:T + (h + 1) * HD2], w[:, T:SC], v[:, 1, :], start=False,
                                   stop=True)
                return mm

            project2("qa", 4)
            pe.wait_ge(s["p_in"], 16)
            for t in range(TT):
                for k in range(2):
                    mm = pe.transpose(tp[:, 0, k * T + t * P:k * T + (t + 1) * P],
                                      bc[:, 0, t * T + k * P:t * T + (k + 1) * P], ident)
            mm.then_inc(s["p_ps"], 1)
            project2("ka")
            pe.wait_ge(s["pt_lo"], 1)
            stick_scores(0)
            token_stage(SPLIT["va"], ACC["va"], 2, 4, 1, x_tiles, KD)
            stick_sums(0)
            project2("qb")
            pe.wait_ge(s["v2"], TT)
            pe.wait_ge(s["a_ready"], 1)
            weigh_values(ACC["stick0"], lambda h: sp4[:, h, :], v2t[0], 0).then_inc(s["acc_ready"], 1)
            stick_scores(1)
            project2("kb")
            stick_sums(1)
            token_stage(SPLIT["vb"], ACC["vb"], 2, 4, 1, x_tiles, KD)
            pe.wait_ge(s["a_ready"], 2)
            weigh_values(ACC["stick1"], lambda h: sp4[:, h, :], v2t[0], GH).then_inc(s["acc_ready"], 1)

            bpt = xn2[:, 0:2 * SC].rearrange("p (b n) -> p b n", b=2)
            bt = xn2[:, 1024:1024 + 2 * SC].rearrange("p (b n) -> p b n", b=2)

            def band_scores(h):
                if h >= 2:
                    pe.wait_ge(s["b_z"], 2 * (h - 1))
                q_, k_ = head2(2, h), head2(3, h)
                pe.matmul(tp[:, h % 2, 0:P], q_[:, 0:P], k_[:, 0:P], start=True, stop=True)
                pe.matmul(tp[:, h % 2, P:SC], q_[:, P:T], k_[:, :], start=True, stop=True).then_inc(s["b_ps"], 1)

            def band_transposes(h):
                pe.wait_ge(s["b_exp"], h + 1)
                if h >= 2:
                    pe.wait_ge(s["b_t"], h - 1)
                for k in range(3):
                    mm = pe.transpose(tp[:, 2 + h % 2, k * P:(k + 1) * P], bpt[:, h % 2, k * P:(k + 1) * P], ident)
                mm.then_inc(s["b_tps"], 1)

            def band_values(h):
                i = ACC[f"band{h // GH}"]
                if h % GH == 0:
                    bank_free(i)
                pe.wait_ge(s["b_t"], h + 1)
                w, v = bt[:, h % 2, :], v2t[1][:, :, h * HD2:(h + 1) * HD2]
                o, at = acc[:, i % NR, :], (h % GH) * HD2
                pe.matmul(o[:, at:at + HD2], w[:, 0:P], v[:, 0, :], start=True, stop=True)
                pe.matmul(o[:, T + at:T + at + HD2], w[:, P:T], v[:, 0, :], start=True, stop=False)
                mm = pe.matmul(o[:, T + at:T + at + HD2], w[:, T:SC], v[:, 1, :], start=False, stop=True)
                if h % GH == GH - 1:
                    mm.then_inc(s["acc_ready"], 1)

            pe.wait_ge(s["qk2"], 8)
            pe.wait_ge(s["a_raw"], 2 * GH)
            band_scores(0)
            pe.wait_ge(s["v2"], 2 * TT)
            for h in range(H2):
                if h + 1 < H2:
                    band_scores(h + 1)
                if h:
                    band_values(h - 1)
                band_transposes(h)
            band_values(H2 - 1)

            transpose_tokens(5, MX)
            token_stage(SPLIT["wout2"], ACC["wout2"], 4, 2, 2, x_tiles, KD, lambda c: x_ready(5, c))
            transpose_tokens(6, XN)
            ffn_up(2)
            si = SPLIT["proj"]
            chunk_ready(si)
            w = [r[si % NR][:, :].rearrange("p (k n) -> p k n", k=2) for r in (whi, wlo)]
            for k in range(2):
                for t in range(TT):
                    for b in range(2):
                        mm = product(tp[:, 2 * t + b, :], phi[:, k, t * P:(t + 1) * P], plo[:, k, t * P:(t + 1) * P],
                                     w[0][:, k, b * 512:(b + 1) * 512], w[1][:, k, b * 512:(b + 1) * 512], True,
                                     k == 0, k == 1)
            mm.then_inc(s["chunk_used"], 1)
            ffn_down(2)
            pe.wait_ge(s["pw_done"], 4)
            transpose_tokens(7, X, "f_x", 4)
            token_stage(SPLIT["gate"], ACC["gate"], 4, 2, 2, x_tiles, KD, lambda c: x_ready(7, c))

        @block.scalar
        def _(act):
            n_split = [0]

            def split(si_slot, raw_slot, landed_at, used):
                act.wait_ge(landed[raw_slot], landed_at)
                if used is not None:
                    act.wait_ge(s[used[0]], used[1])
                act.copy(whi[si_slot][:, :], raw[raw_slot][:, :]).then_inc(s["hi_done"], 1)

            chunk_of = [c for c, (what, _) in enumerate(kind) if what == "lo_done"]

            def splits_to(n):
                while n_split[0] < min(n, N_SPLIT):
                    si = n_split[0]
                    c = chunk_of[si]
                    split(si % NR, c % NR, 16 * (c // NR + 1), USED[si - NR] if si >= NR else None)
                    n_split[0] += 1

            def bank_ready(i):
                act.wait_ge(s["acc_ready"], i + 1)

            def x_hi(n, gain, shift, dst):
                for b in range(4):
                    act.wait_ge(s["xt_ps"], 4 * n + b + 1)
                    if gain is None:
                        ins = act.copy(dst[:, 2 * b:2 * b + 2, :], tp[:, b, :].rearrange("p (k n) -> p k n", k=2))
                    else:
                        for k in (2 * b, 2 * b + 1):
                            ins = act.activation(dst[:, k, :], tp[:, b, (k % 2) * T:(k % 2 + 1) * T], ACT.Identity,
                                                 scale=gain[:, k:k + 1], bias=0.0 if shift is None else shift(k))
                    ins.then_inc(s["xhi"], 1)

            act.dma_start(consts[:, :], a["consts"]).then_inc(s["const_in"], 16)
            act.dma_start(X[:, :, :], a["x"].rearrange("(t p) d -> p t d", p=P)).then_inc(s["x_in"], 16)
            act.wait_ge(s["pads"], 1)
            act.dma_start(full2[0:TAPS * KC, P:2 * P], a["conv_dw_w"].rearrange("i (k p) -> (i k) p", p=P))\
                .then_inc(s["vec_in"], 16)
            act.dma_start(full2[0:3 * KF, 2 * P:3 * P], a["ffn_dw_w"].rearrange("i (k p) -> (i k) p", p=P))\
                .then_inc(s["vec_in"], 16)
            act.dma_start(full2[3 * KF:4 * KF, 2 * P:3 * P], a["ffn_dw_b"].rearrange("(k p) -> k p", p=P))\
                .then_inc(s["vec_in"], 16)
            CTX = G[:, 0:8, :].rearrange("p (t k) n -> p t (k n)", t=TT)
            act.dma_start(CTX, a["ctx"].rearrange("(t p) d -> p t d", p=P)).then_inc(s["ctx_in"], 16)
            act.wait_ge(s["vec_sb"], 1)
            act.activation(sct[:, :, 0], vec("c", 8), ACT.Silu)
            act.activation(sct[:, :, 1], vec("c_ctx", 8), ACT.Silu).then_inc(s["silu_c"], 1)
            splits_to(2)
            act.wait_ge(s["affine1"], 1)
            x_hi(0, gainA[:, 0, :], lambda k: modv[:, k, 0:1], xhi)
            splits_to(4)
            act.wait_ge(s["affine1c"], 1)
            x_hi(1, gainA[:, 1, :], lambda k: modv[:, k, 1:2], side_hi)

            def unit_squares(u, i, heads, v_tile):
                bank_ready(i)
                if u:
                    act.wait_ge(s["q_ss"], u)
                if v_tile is not None:
                    act.copy(V[:, v_tile, :], accb(i)[:, NKV * HD:2 * NKV * HD]).then_inc(s["v_done"], 1)
                for h in range(heads):
                    ins = act.activation(half(XN, 3)[:, h * HD:(h + 1) * HD], accb(i)[:, h * HD:(h + 1) * HD],
                                         ACT.Square, accum_out=qss[:, 4 * u + h:4 * u + h + 1])
                ins.then_inc(s["q_ss"], 1)

            def unit_out(u):
                act.wait_ge(s["q_tps"], u + 1)
                if u < 4:
                    b, t = u // 2, u % 2
                    dst = QT[:, 4 * b:4 * b + 4, t * P:(t + 1) * P]
                    ps = tp[:, u % 4, :].rearrange("p (h n) -> p h n", h=4)
                else:
                    t = (u - 4 + 2) % 4
                    dst = KT[:, :, t * P:(t + 1) * P]
                    ps = tp[:, u % 4, 0:NKV * P].rearrange("p (h n) -> p h n", h=NKV)
                act.copy(dst, ps).then_inc(s["q_t"], 1)

            splits_to(SPLIT["q"] + 4)
            act.wait_ge(s["xt_ps"], 8)
            for u in range(4):
                unit_squares(u, ACC["q"] + u, 4, None)
                splits_to(SPLIT["u"] + u + 1)
            for j in range(2):
                unit_out(2 * j)
                unit_out(2 * j + 1)
                bank_ready(ACC["u"] + 2 * j + 1)
                act.activation(half(XN, j), accb(ACC["u"] + 2 * j + 1), ACT.Sigmoid)\
                    .then_inc(s["glu_sig"], 1)
                splits_to(SPLIT["kv"] + j + 1)
            splits_to(SPLIT["g0"] + 2)
            for u in range(4, 8):
                unit_squares(u, ACC["kv"] + u - 4, NKV, (u - 4 + 2) % 4)
            splits_to(SPLIT["g2"] + 1)
            for u in range(4, 8):
                unit_out(u)
            splits_to(SPLIT["g2"] + 2)

            def pv_hi(h):
                bank_ready(ACC[f"pv{h}"])
                act.copy(side_hi[:, h, :], acc[:, ACC[f"pv{h}"] % NR, 0:T]).then_inc(s["a_hi"], 1)

            def g_out(h):
                bank_ready(ACC[f"g{h}"])
                act.copy(G[:, 2 * h:2 * h + 2, :], acc[:, ACC[f"g{h}"] % NR, :].rearrange("p (q n) -> p q n", q=2))\
                    .then_inc(s["g_raw"], 1)

            PT = FULL[:, 4:8, :]
            for h in range(NH):
                for t in range(TT):
                    act.wait_ge(s["nm_ready"], TT * h + t + 1)
                    if h:
                        act.wait_ge(s["pt_ps"], TT * (h - 1) + t + 1)
                    act.activation(half(FULL, t), tp[:, t, :], ACT.Exp, bias=nmax[:, t:t + 1],
                                   accum_out=psum_[:, t:t + 1]).then_inc(s["p_exp"], 1)
                if h == 0:
                    g_out(0)
                    g_out(1)
                else:
                    pv_hi(h - 1)
                slot_split(splits_to, h)
                if h + 2 < NH:
                    g_out(h + 2)
                for t in range(TT):
                    act.wait_ge(s["pt_ps"], TT * h + t + 1)
                    act.copy(PT[:, :, t * P:(t + 1) * P], tp[:, 2 + t, :].rearrange("p (k n) -> p k n", k=4))\
                        .then_inc(s["pt_done"], 1)
            pv_hi(NH - 1)
            sq = QT[:, 0:4, :]
            act.wait_ge(s["ln_c"], 1)
            act.activation(sq, QT[:, 4:8, :], ACT.Square).then_inc(s["ln_sq"], 1)
            splits_to(SPLIT["attnout1"] + 1)
            act.wait_ge(s["g_raw"], NH)
            for q in range(2):
                act.activation(G[:, 8 * q:8 * q + 8, :], G[:, 8 * q:8 * q + 8, :], ACT.Sigmoid)\
                    .then_inc(s["g_sig"], 1)
                splits_to(SPLIT["attnout2"] + q + 1)
            act.wait_ge(s["ln_n"], 1)
            for k in range(KC):
                ins = act.activation(QT[:, k, :], QT[:, 4 + k, :], ACT.Silu, scale=vec("conv_ln_g", 1, k),
                                     bias=vec("conv_ln_b", 1, k))
            ins.then_inc(s["ln_y"], 1)
            act.wait_ge(s["ln_y"], 1)
            act.copy(cvt_hi[:, :, :], QT[:, 0:4, :]).then_inc(s["ln_hi"], 1)
            splits_to(SPLIT["wout"] + 2)
            for j in range(4):
                act.wait_ge(s["mg_full"], j + 1)
                act.copy(xhi[:, 2 * j:2 * j + 2, :], FULL[:, 2 * j:2 * j + 2, :]).then_inc(s["mg_hi"], 1)
            for b in range(2):
                bank_ready(ACC["g1b"] + b)
                act.copy(bc[:, 0, b * 512:(b + 1) * 512], accb(ACC["g1b"] + b)).then_inc(s["g1b_done"], 1)
            splits_to(SPLIT["wout"] + 4)
            splits_to(SPLIT["up0"] + 2)
            x_hi(2, gainA[:, 2, :], lambda k: mod2[:, 8 + k:9 + k], xhi)
            splits_to(SPLIT["up0"] + 4)

            def ffn_up(n):
                si, i, c = SPLIT[f"up{n}"], ACC[f"up{n}"], CHUNK[f"up{n}"]
                assert n_split[0] == si + 4
                pairs = NPAIR * n

                def ahead(m, o):
                    split((si + o) % NR, (c + o) % NR, 16 * ((c + o) // NR + 2 + m), ("acc_ready", i + o + 1 + 4 * m))

                def pair(m, q, more):
                    j = 2 * m + q
                    g = i + 2 * q
                    act.wait_ge(s["acc_ready"], g + 4 * m + 1)
                    if n == 0:
                        for o in range(2):
                            w = 2 * j + o
                            act.activation(half(XN, q)[:, o * T:(o + 1) * T], acc[:, g % NR, o * T:(o + 1) * T],
                                           ACT.Identity, scale=vt[:, 2, bass.ds(KF + w, 1)],
                                           bias=vt[:, 2, bass.ds(3 * KF + w, 1)]).then_inc(s["cv_act"], 1)
                        if more:
                            ahead(m, 2 * q)
                        act.wait_ge(s["cv_dve"], 4 * j + 4)
                        act.activation(half(XN, 2 + q), half(XN, q), ACT.Gelu_apprx_tanh).then_inc(s["glu_act"], 1)
                    else:
                        act.activation(half(XN, 2 + q), accb(g), ACT.Silu).then_inc(s["glu_act"], 1)
                        if more:
                            ahead(m, 2 * q)
                    if more:
                        ahead(m, 2 * q + 1)
                    act.wait_ge(s["h_full"], pairs + j + 1)
                    act.copy(hhi[:, bass.ds(2 * j, 2), :],
                             half(FULL, q).rearrange("p (o n) -> p o n", o=2)).then_inc(s["h_hi"], 1)

                with act.Fori(0, 5) as m:
                    for q in range(2):
                        pair(m, q, True)
                n_split[0] = si + 24
                pair(5, 0, False)

            ffn_up(0)
            splits_to(SPLIT["up1"] + 1)
            for b in range(2):
                act.wait_ge(s["g2b_ps"], b + 1)
                act.copy(bc[:, 1, b * 512:(b + 1) * 512], tp[:, 1 + b, :]).then_inc(s["g2b_done"], 1)
            splits_to(SPLIT["up1"] + 2)
            x_hi(3, vec("g_ffn1_pre_2", 8), None, xhi)
            splits_to(SPLIT["up1"] + 4)
            ffn_up(1)

            def post(m, name):
                for j in range(2 * TT):
                    i = ACC[name] + j
                    bank_ready(i)
                    act.activation(half(XN, j), accb(i), ACT.Square, scale=float(D) ** -0.5,
                                   accum_out=fss2[:, j:j + 1]).then_inc(s["f_ss"], 1)

            splits_to(SPLIT["qa"] + 2)
            post(0, "down1")
            x_hi(4, vec("g_mix_pre_2", 8), None, xhi)
            splits_to(SPLIT["qa"] + 4)

            def qk_out(w, name):
                for j in range(2):
                    bank_ready(ACC[name] + j)
                    act.activation(qk2t[w][:, 2 * j:2 * j + 2, :],
                                   acc[:, (ACC[name] + j) % NR, :].rearrange("p (q n) -> p q n", q=2),
                                   ACT.Copy, scale=HD2 ** -0.5 if w % 2 == 0 else 1.0).then_inc(s["qk2"], 1)

            ez = xn2[:, 0:GH * SC].rearrange("p (h n) -> p h n", h=GH)
            sp4 = full2[:, 0:GH * SC].rearrange("p (h n) -> p h n", h=GH)

            def stick_ln(g):
                for h in range(GH):
                    act.wait_ge(s["z_ps"], GH * g + h + 1)
                    act.activation(ez[:, h, :], tp[:, h, 0:SC], ACT.Abs).then_inc(s["z_abs"], 1)
                act.wait_ge(s["z_abs"], GH * (g + 1))
                for h in range(GH):
                    act.activation(ez[:, h, :], ez[:, h, :], ACT.Exp, scale=-1.0).then_inc(s["z_exp"], 1)
                act.wait_ge(s["z_exp"], GH * (g + 1))
                for h in range(GH):
                    act.activation(ez[:, h, :], ez[:, h, :], ACT.Ln, bias=1.0).then_inc(s["z_ln"], 1)

            def stick_exp(g):
                for h in range(GH):
                    act.wait_ge(s["arg_ready"], GH * g + h + 1)
                    act.activation(sp4[:, h, :], tp[:, h, 0:SC], ACT.Exp).then_inc(s["a_raw"], 1)

            def v_out(n, name):
                for t in range(TT):
                    bank_ready(ACC[name] + t)
                    act.copy(v2t[n][:, t, :], accb(ACC[name] + t)).then_inc(s["v2"], 1)

            qk_out(0, "qa")
            splits_to(SPLIT["va"] + 1)
            act.wait_ge(s["p_ps"], 1)
            act.copy(phi[:, :, :], tp[:, 0, :].rearrange("p (k n) -> p k n", k=2)).then_inc(s["pt_hi"], 1)
            splits_to(SPLIT["va"] + 2)
            qk_out(1, "ka")
            stick_ln(0)
            splits_to(SPLIT["qb"] + 2)
            v_out(0, "va")
            stick_exp(0)
            splits_to(SPLIT["kb"] + 2)
            qk_out(2, "qb")
            stick_ln(1)
            splits_to(SPLIT["vb"] + 2)
            qk_out(3, "kb")
            stick_exp(1)
            splits_to(SPLIT["wout2"] + 2)
            v_out(1, "vb")
            bz = full2[:, 0:2 * SC].rearrange("p (b n) -> p b n", b=2)
            bpt = xn2[:, 0:2 * SC].rearrange("p (b n) -> p b n", b=2)
            bt = xn2[:, 1024:1024 + 2 * SC].rearrange("p (b n) -> p b n", b=2)

            def band_exp(h):
                act.wait_ge(s["b_z"], 2 * (h + 1))
                if h >= 2:
                    act.wait_ge(s["b_tps"], h - 1)
                for t, (lo, hi) in enumerate(((0, P), (P, SC))):
                    ins = act.activation(bpt[:, h % 2, lo:hi], bz[:, h % 2, lo:hi], ACT.Exp,
                                         bias=bmax[:, 2 * h + t:2 * h + t + 1],
                                         accum_out=bsum[:, 8 * t + h:8 * t + h + 1])
                ins.then_inc(s["b_exp"], 1)

            band_exp(0)
            for h in range(H2):
                if h + 1 < H2:
                    band_exp(h + 1)
                act.wait_ge(s["b_tps"], h + 1)
                act.copy(bt[:, h % 2, :], tp[:, 2 + h % 2, 0:SC]).then_inc(s["b_t"], 1)
            x_hi(5, vec("g_out_sb_2", 8), None, xhi)
            splits_to(SPLIT["wout2"] + 4)
            splits_to(SPLIT["up2"] + 2)
            post(1, "wout2")
            x_hi(6, vec("g_ffn2_pre_2", 8), None, xhi)
            splits_to(SPLIT["up2"] + 4)
            ffn_up(2)
            splits_to(SPLIT["gate"] + 2)
            post(2, "down2")
            x_hi(7, None, None, xhi)
            splits_to(SPLIT["gate"] + 4)
            for t in range(TT):
                for b in range(2):
                    i = ACC["gate"] + 2 * t + b
                    bank_ready(i)
                    act.activation(half(XN, 2 * t + b), accb(i), ACT.Sigmoid).then_inc(s["gate_s"], 1)
            for j in range(2 * TT):
                act.wait_ge(s["e_y"], j + 1)
                act.activation(MX[:, j // 2, (j % 2) * 512:(j % 2 + 1) * 512], half(XN, j), ACT.Square, scale=float(D) ** -0.5,
                               accum_out=fss2[:, j:j + 1]).then_inc(s["f_ss"], 1)
            for t in range(TT):
                act.wait_ge(s["out_x"], t + 1)
                act.dma_start(a["out"][t * P:(t + 1) * P, :], X[:, t, :]).then_inc(s["out_done"], 16)
            act.wait_ge(s["out_done"], 16 * TT)

        @block.vector
        def _(dve):
            n_split, n_chain, n_shift = [0], [0], [0]

            def chain(ins):
                n_chain[0] += 1
                ins.then_inc(s["dve_chain"], 1)
                dve.wait_ge(s["dve_chain"], n_chain[0])

            chunk_of = [c for c, (what, _) in enumerate(kind) if what == "lo_done"]

            def split(slot, raw_slot, n):
                dve.wait_ge(s["hi_done"], n)
                dve.tensor_tensor(wlo[slot][:, :], raw[raw_slot][:, :], whi[slot][:, :], ALU.subtract)\
                    .then_inc(s["lo_done"], 1)

            def splits_to(n):
                while n_split[0] < min(n, N_SPLIT):
                    si = n_split[0]
                    split(si % NR, chunk_of[si] % NR, si + 1)
                    n_split[0] += 1

            def bank_ready(i):
                dve.wait_ge(s["acc_ready"], i + 1)

            def mean_square(t, source, out, sem):
                dve.tensor_tensor_reduce(XN[:, t, :], source[:, t, :], source[:, t, :], 1.0 / D, EPS, ALU.mult, ALU.add,
                                         out[:, t:t + 1]).then_inc(s[sem], 1)

            def scale_tokens(n, t, source):
                dve.wait_ge(s["ri_ready"], TT * n + t + 1)
                dve.tensor_scalar(XN[:, t, :], source[:, t, :], ri[:, t:t + 1], None, ALU.mult)\
                    .then_inc(s["xn_ready"], 1)

            def norm(n, source):
                for t in range(TT):
                    mean_square(t, source, ss, "ss_ready")
                for t in range(TT):
                    scale_tokens(n, t, source)

            def norm_tile(n, t, sem, value):
                dve.wait_ge(s[sem], value)
                mean_square(t, X, ss, "ss_ready")
                scale_tokens(n, t, X)

            def x_lo(n, gain, shift, dh, dl):
                for b in range(4):
                    dve.wait_ge(s["xhi"], 4 * n + b + 1)
                    if gain is None:
                        dve.tensor_tensor(dl[:, 2 * b:2 * b + 2, :], tp[:, b, :].rearrange("p (k n) -> p k n", k=2),
                                          dh[:, 2 * b:2 * b + 2, :], ALU.subtract).then_inc(s["xlo"], 1)
                        continue
                    dst = dl if shift is None else FULL
                    for k in (2 * b, 2 * b + 1):
                        ins = dve.scalar_tensor_tensor(dst[:, k, :], tp[:, b, (k % 2) * T:(k % 2 + 1) * T],
                                                       gain[:, k:k + 1], dh[:, k, :], ALU.mult, ALU.subtract)
                    if shift is not None:
                        ins.then_inc(s["shift_dve"], 1)
                        dve.wait_ge(s["shift_dve"], n_shift[0] + 1)
                        n_shift[0] += 1
                        for k in (2 * b, 2 * b + 1):
                            ins = dve.tensor_scalar(dl[:, k, :], FULL[:, k, :], shift(k), None, ALU.add)
                    ins.then_inc(s["xlo"], 1)

            dve.memset(full2[:, 0:3 * P], 0.0).then_inc(s["pads"], 1)
            dve.wait_ge(s["vec_ps"], 1)
            dve.tensor_copy(vt[:, :, :], tp[:, 3, 0:3 * P].rearrange("p (r n) -> p r n", r=3))\
                .then_inc(s["vec_sb"], 1)
            dve.wait_ge(s["x_in"], 16)
            norm(0, X)

            def weigh(c, out, column, k, sem=None, beside=0):
                w = raw[c % NR][:, k * 256:(k + 1) * 256]
                if k == 0:
                    ins = dve.tensor_scalar(out, w, sct[:, k, column:column + 1], None, ALU.mult)
                else:
                    dve.wait_ge(s["weigh"], n_weigh[0] - beside)
                    ins = dve.scalar_tensor_tensor(out, w, sct[:, k, column:column + 1], out, ALU.mult, ALU.add)
                if k == KD - 1 and sem is not None:
                    ins.then_inc(s[sem], 1)
                else:
                    n_weigh[0] += 1
                    ins.then_inc(s["weigh"], 1)

            n_weigh = [0]
            dve.wait_ge(s["silu_c"], 1)
            for step, j in enumerate(MOD1_DVE):
                c = CHUNK["mod1"] + j
                dve.wait_ge(landed[c % NR], 16 * (c // NR + 1))
                for k in range(KD):
                    for v in range(2):
                        weigh(c, mod1_acc(step)[:, v * 256:(v + 1) * 256], v, k, "mod_acc" if v == 1 else None, 1)
                for i in ((), (0, 1), (2, 3), (4,), (5, 6, 7))[step]:
                    j = MOD1[i]
                    bank_ready(ACC["mod1"] + i)
                    b = vec("b_mod", 2, 2 * j)
                    dve.tensor_tensor(modv[:, 2 * j:2 * j + 2, :],
                                      b.rearrange("p (q c) -> p q c", c=1).broadcast_to([P, 2, 2]),
                                      accb(ACC["mod1"] + i)[:, 0:4].rearrange("p (q c) -> p q c", q=2),
                                      ALU.subtract if j in MOD1_DVE else ALU.add).then_inc(s["mod_out"], 1)
            dve.wait_ge(s["mod_out"], 8)
            for w, sem in ((0, "affine1"), (1, "affine1c")):
                dve.scalar_tensor_tensor(gainA[:, w, :], modv[:, 8:16, w], 1.0, vec("norm1_g", 8), ALU.add, ALU.mult)\
                    .then_inc(s[sem], 1)
            dve.wait_ge(s["affine1"], 1)
            splits_to(1)
            x_lo(0, gainA[:, 0, :], lambda k: modv[:, k, 0:1], xhi, xlo)
            splits_to(2)
            CTX = G[:, 0:8, :].rearrange("p (t k) n -> p t (k n)", t=TT)
            dve.wait_ge(s["ctx_in"], 16)
            norm(1, CTX)
            splits_to(4)
            x_lo(1, gainA[:, 1, :], lambda k: modv[:, k, 1:2], side_hi, side_lo)

            def unit(u, i, heads, t, kind_):
                w = heads * HD
                qn, t1, t2 = (half(FULL, x)[:, 0:w] for x in (1, 2 * (u % 2), 3))

                def by_head(v):
                    return v.rearrange("p (h d) -> p h d", h=heads)

                def table(r):
                    return rope[:, r:r + 1, t * HD:(t + 1) * HD].broadcast_to([P, heads, HD])

                def swapped(v):
                    return v.rearrange("p (h i two) -> p h i two", h=heads, two=2)[:, :, :, ::-1]

                dve.wait_ge(s["q_ri"], u + 1)
                if u:
                    dve.wait_ge(s["q_rot"], u)
                r = qri[:, 4 * u:4 * u + heads].rearrange("p (h d) -> p h d", d=1).broadcast_to([P, heads, HD])
                dve.tensor_tensor(by_head(qn), by_head(accb(i)[:, 0:w]), r, ALU.mult).then_inc(s["q_norm"], 1)
                dve.wait_ge(s["q_norm"], u + 1)
                if u >= 2:
                    dve.wait_ge(s["q_tps"], u - 1)
                if kind_ is None:
                    g_ = rope[:, 4:5, 0:HD].broadcast_to([P, heads, HD])
                    dve.tensor_tensor(by_head(t1), by_head(qn), g_, ALU.mult).then_inc(s["q_rot"], 1)
                    return
                dve.tensor_tensor(by_head(t1), by_head(qn), table(kind_), ALU.mult)
                for h in range(heads):
                    ins = dve.tensor_tensor(
                        t2[:, h * HD:(h + 1) * HD].rearrange("p (i two) -> p i two", two=2),
                        qn[:, h * HD:(h + 1) * HD].rearrange("p (i two) -> p i two", two=2)[:, :, ::-1],
                        rope[:, kind_ + 1, t * HD:(t + 1) * HD].rearrange("p (i two) -> p i two", two=2), ALU.mult)
                chain(ins)
                dve.tensor_tensor(t1, t1, t2, ALU.add).then_inc(s["q_rot"], 1)

            dve.wait_ge(s["tables"], 1)
            splits_to(SPLIT["q"] + 4)
            for u in range(4):
                unit(u, ACC["q"] + u, 4, u % 2, 0)
                splits_to(SPLIT["u"] + u + 1)
            for j in range(2):
                dve.wait_ge(s["glu_sig"], j + 1)
                dve.tensor_tensor(conv_x[:, 2 * j:2 * j + 2, PAD:PAD + T],
                                  accb(ACC["u"] + 2 * j).rearrange("p (q n) -> p q n", q=2),
                                  half(XN, j).rearrange("p (q n) -> p q n", q=2), ALU.mult)\
                    .then_inc(s["conv_in"], 1)
                splits_to(SPLIT["kv"] + j + 1)
            splits_to(SPLIT["g0"] + 2)
            for u in range(4, 8):
                unit(u, ACC["kv"] + u - 4, NKV, u % 2, 2 if u < 6 else None)
            splits_to(SPLIT["g2"] + 2)

            def pv_lo(h):
                i = ACC[f"pv{h}"]
                dve.wait_ge(s["a_hi"], h + 1)
                dve.tensor_tensor(side_lo[:, h, :], acc[:, i % NR, 0:T], side_hi[:, h, :], ALU.subtract)\
                    .then_inc(s["a_lo"], 1)

            def mod_out(name):
                i, j = ACC["sum_" + name], MODS.index(name)
                bank_ready(i)
                ps = accb(i)[:, 0:4].rearrange("p (q c) -> p q c", q=2)[:, :, 0]
                dve.tensor_tensor(mod2[:, 2 * j:2 * j + 2], vec("b_mod", 2, 16 + 2 * j), ps, ALU.subtract)\
                    .then_inc(s["mod_out"], 1)

            def mod_weigh(name, between=None):
                j, c = MODS.index(name), CHUNK[name]
                dve.wait_ge(landed[c % NR], 16 * (c // NR + 1))
                if j >= 14:
                    dve.wait_ge(s["mod4_ps"], j - 13)
                elif j >= 2:
                    dve.wait_ge(s["acc_ready"], ACC["sum_" + MODS[j - 2]] + 1)
                for k in range(KD):
                    weigh(c, modacc[:, j % 2, :], 0, k, "mod_acc")
                    if between is not None:
                        between(k)

            KV_ = KC - KP

            def conv_tap(i, k):
                if i >= TAPS:
                    return
                at = XN[:, 1, k * T:(k + 1) * T]
                w = vt[:, 1, KC * i + k:KC * i + k + 1]
                if i == 0:
                    dve.tensor_scalar(at, conv_x[:, k, 0:T], w, vec("conv_dw_b", 1, k), ALU.mult, ALU.add)\
                        .then_inc(s["conv_dve"], 1)
                else:
                    dve.wait_ge(s["conv_dve"], KV_ * (i - 1) + k + 1)
                    dve.scalar_tensor_tensor(at, conv_x[:, k, i:i + T], w, at, ALU.mult, ALU.add)\
                        .then_inc(s["conv_dve"], 1)

            per_slot = (TAPS + NH - 1) // NH
            assert per_slot * KV_ == KD
            for h in range(NH):
                for t in range(TT):
                    dve.wait_ge(s["sc_ready"], TT * h + t + 1)
                    dve.tensor_reduce(nmax[:, t:t + 1], tp[:, t, :], AX, ALU.max, negate=True)\
                        .then_inc(s["nm_ready"], 1)
                for t in range(TT):
                    dve.wait_ge(s["p_exp"], TT * h + t + 1)
                    chain(dve.reciprocal(prec[:, t:t + 1], psum_[:, t:t + 1]))
                    dve.tensor_scalar(half(FULL, t), half(FULL, t), prec[:, t:t + 1], None, ALU.mult)\
                        .then_inc(s["p_scaled"], 1)
                if h:
                    pv_lo(h - 1)
                mod_weigh(f"mod2_{h}", lambda k: conv_tap(per_slot * h + k // KV_, k % KV_))
                slot_split(splits_to, h)
                if h:
                    mod_out(f"mod2_{h - 1}")
            mod_out(f"mod2_{NH - 1}")
            pv_lo(NH - 1)
            conv = XN[:, 1, :].rearrange("p (k n) -> p k n", k=KC)
            cent = QT[:, 4:8, :]

            def diagonal(out, at):
                for k in range(KD):
                    ins = dve.tensor_scalar(out[:, k * P:(k + 1) * P], ident, mod2[:, at + k:at + k + 1], -1.0,
                                            ALU.mult, ALU.mult)
                ins.then_inc(s["diag"], 1)

            def over_tiles(v):
                return v.rearrange("p (k n) -> p k n", k=1).broadcast_to([P, KC, T])

            dve.wait_ge(s["ln_mean"], 1)
            dve.tensor_tensor(cent, conv, over_tiles(tp[:, 0, 0:T]), ALU.subtract).then_inc(s["ln_c"], 1)
            for j in range(4):
                splits_to(min(SPLIT[f"attnout{j}"] + 2, SPLIT["convout"]))
                mod_weigh(f"mod3_{j}")
                if j:
                    mod_out(f"mod3_{j - 1}")
                if j == 3:
                    splits_to(SPLIT["convout"] + 1)
                    dve.wait_ge(s["ln_hi"], 1)
                    dve.tensor_tensor(cvt_lo[:, :, :], QT[:, 0:4, :], cvt_hi[:, :, :], ALU.subtract)\
                        .then_inc(s["ln_lo"], 1)
                b = ACC[f"attnout{j}"]
                bank_ready(b)
                dve.wait_ge(s["g_sig"], 1)
                v = G[:, 2 * j:2 * j + 2, :]
                dve.tensor_tensor(v, accb(b).rearrange("p (q n) -> p q n", q=2), v, ALU.mult)\
                    .then_inc(s["ya_done"], 1)
                if j == 0:
                    dve.wait_ge(s["ln_var"], 1)
                    dve.tensor_copy(lnv, tp[:, 1, 0:TT]).then_inc(s["ln_ve"], 1)
                    dve.wait_ge(s["ln_c"], 1)
                    diagonal(xn2[:, D:2 * D], 0)
                    dve.wait_ge(s["ln_r"], 1)
                    for t in range(TT):
                        ins = dve.tensor_scalar(half(XN, 0)[:, t * P:(t + 1) * P], ident, lnv[:, t:t + 1], -1.0,
                                                ALU.mult, ALU.mult)
                    ins.then_inc(s["ln_diag"], 1)
                elif j == 1:
                    dve.wait_ge(s["ln_bc"], 1)
                    dve.tensor_tensor(cent, cent, over_tiles(tp[:, 2, 0:T]), ALU.mult).then_inc(s["ln_n"], 1)
            splits_to(SPLIT["convout"] + 2)
            mod_out("mod3_3")
            splits_to(SPLIT["wout"] + 2)
            dve.wait_ge(s["g_sig"], 2)
            dve.wait_ge(s["ya_done"], 4)
            for j in range(4):
                b = ACC["convout"] + j
                bank_ready(b)
                v = G[:, 8 + 2 * j:10 + 2 * j, :]
                dve.tensor_tensor(v, accb(b).rearrange("p (q n) -> p q n", q=2), v, ALU.mult)\
                    .then_inc(s["yb_done"], 1)
                dve.wait_ge(s["yb_done"], j + 1)
                dve.tensor_tensor(FULL[:, 2 * j:2 * j + 2, :], v, G[:, 2 * j:2 * j + 2, :], ALU.add)\
                    .then_inc(s["mg_full"], 1)
                dve.wait_ge(s["mg_hi"], j + 1)
                dve.tensor_tensor(xlo[:, 2 * j:2 * j + 2, :], FULL[:, 2 * j:2 * j + 2, :], xhi[:, 2 * j:2 * j + 2, :],
                                  ALU.subtract).then_inc(s["mg_lo"], 1)

            dve.wait_ge(s["mod_out"], 20)
            chain(dve.scalar_tensor_tensor(gainA[:, 2, :], mod2[:, 16:24], 1.0, vec("norm2_g", 8), ALU.add, ALU.mult))
            splits_to(SPLIT["wout"] + 4)

            def residual(name, t, gate, first, sem):
                for b in range(2):
                    i = ACC[name] + 2 * t + b
                    bank_ready(i)
                    dve.tensor_tensor(XN[:, t, b * 512:(b + 1) * 512], accb(i), bc[:, gate, b * 512:(b + 1) * 512],
                                      ALU.mult).then_inc(s["res_y"], 1)
                dve.wait_ge(s["res_y"], first + 2 * t + 2)
                dve.tensor_tensor(X[:, t, :], X[:, t, :], XN[:, t, :], ALU.add).then_inc(s[sem], 1)

            dve.wait_ge(s["g1b_done"], 2)
            splits_to(SPLIT["up0"] + 2)
            for t in range(TT):
                residual("wout", t, 0, 0, "res1")
                norm_tile(2, t, "res1", t + 1)
            x_lo(2, gainA[:, 2, :], lambda k: mod2[:, 8 + k:9 + k], xhi, xlo)
            splits_to(SPLIT["up0"] + 4)

            def ffn_up(n):
                si, i, c = SPLIT[f"up{n}"], ACC[f"up{n}"], CHUNK[f"up{n}"]
                assert n_split[0] == si + 4
                pairs = NPAIR * n

                def ahead(m, o):
                    split((si + o) % NR, (c + o) % NR, si + o + 5 + 4 * m)

                def pair(m, q, more):
                    j = 2 * m + q
                    g, u = i + 2 * q, i + 2 * q + 1
                    if n == 0:
                        for tap, (dst, sr) in enumerate((((1, T), (0, T - 1)), ((0, T - 1), (1, T)))):
                            for o in range(2):
                                if tap == 0:
                                    dve.wait_ge(s["cv_act"], 2 * j + 2)
                                else:
                                    dve.wait_ge(s["cv_dve"], 4 * j + o + 1)
                                at = half(XN, q)[:, o * T + dst[0]:o * T + dst[1]]
                                ins = dve.scalar_tensor_tensor(
                                    at, acc[:, g % NR, o * T + sr[0]:o * T + sr[1]],
                                    vt[:, 2, bass.ds(2 * tap * KF + 2 * j + o, 1)], at, ALU.mult, ALU.add)
                                ins.then_inc(s["cv_dve"], 1)
                    if more:
                        ahead(m, 2 * q)
                    dve.wait_ge(s["glu_act"], pairs + j + 1)
                    dve.wait_ge(s["acc_ready"], u + 4 * m + 1)
                    dve.tensor_tensor(half(FULL, q), accb(u), half(XN, 2 + q), ALU.mult).then_inc(s["h_full"], 1)
                    if more:
                        ahead(m, 2 * q + 1)
                    dve.wait_ge(s["h_hi"], pairs + j + 1)
                    dve.tensor_tensor(hlo[:, bass.ds(2 * j, 2), :], half(FULL, q).rearrange("p (o n) -> p o n", o=2),
                                      hhi[:, bass.ds(2 * j, 2), :], ALU.subtract).then_inc(s["h_lo"], 1)

                with dve.Fori(0, 5) as m:
                    for q in range(2):
                        pair(m, q, True)
                n_split[0] = si + 24
                pair(5, 0, False)

            ffn_up(0)
            for j in range(4):
                splits_to(SPLIT["down0"] + 4 + j)
                mod_weigh(f"mod4_{j}")
            splits_to(SPLIT["down0"] + 9)
            dve.wait_ge(s["mod4_ps"], 4)
            dve.tensor_tensor(mod2[:, 24:32], vec("b_mod", 8, 40),
                              tp[:, 0, 0:16].rearrange("p (k c) -> p k c", c=2)[:, :, 0], ALU.subtract)\
                .then_inc(s["mod_out"], 1)
            dve.wait_ge(s["mod_out"], 21)
            diagonal(full2[:, 0:D], 24)
            splits_to(SPLIT["up1"] + 2)
            dve.wait_ge(s["g2b_done"], 2)
            dve.wait_ge(s["fgain"], 16)
            for t in range(TT):
                residual("down0", t, 1, 4, "res2")
                dve.wait_ge(s["res2"], t + 1)
                mean_square(t, X, fss, "fin_ss")
                dve.wait_ge(s["fin_ri"], t + 1)
                dve.scalar_tensor_tensor(X[:, t, :], X[:, t, :], fri[:, t:t + 1], bc[:, 2, :], ALU.mult, ALU.mult)\
                    .then_inc(s["fin_x"], 1)
                norm_tile(3, t, "fin_x", t + 1)
            x_lo(3, vec("g_ffn1_pre_2", 8), None, xhi, xlo)
            splits_to(SPLIT["up1"] + 4)
            ffn_up(1)

            def post(m, name, t, gain, factor):
                dve.wait_ge(s["fgain"], 16 * (m + 2))
                dve.wait_ge(s["f_ri"], TT * m + t + 1)
                for b in range(2):
                    i = ACC[name] + 2 * t + b
                    dve.scalar_tensor_tensor(XN[:, t, b * 512:(b + 1) * 512], accb(i), fri[:, t:t + 1],
                                             bc[:, gain, b * 512:(b + 1) * 512], ALU.mult, ALU.mult)\
                        .then_inc(s["f_y"], 1)
                dve.wait_ge(s["f_y"], 4 * m + 2 * t + 2)
                dve.scalar_tensor_tensor(X[:, t, :], XN[:, t, :], factor, X[:, t, :], ALU.mult, ALU.add)\
                    .then_inc(s["f_x"], 1)

            splits_to(SPLIT["qa"] + 2)
            for t in range(TT):
                post(0, "down1", t, 0, 0.5)
                norm_tile(4, t, "f_x", t + 1)
            x_lo(4, vec("g_mix_pre_2", 8), None, xhi, xlo)
            splits_to(SPLIT["qa"] + 4)

            dve.wait_ge(s["table_in"], 16)
            tin = MX[:, :, :].rearrange("p a b -> p (a b)").rearrange("p (h n) -> p h n", h=H2)
            chain(dve.memset(tin[0:64, :, 0:64], -1e30))
            for h in range(H2):
                dve.tensor_copy(toe[:, h, 0:P], tin[:, h, P - 1::-1])
                ins = dve.tensor_copy(toe[:, h, P:SC], tin[:, h, ::-1])
            chain(ins)

            ez = xn2[:, 0:GH * SC].rearrange("p (h n) -> p h n", h=GH)
            sp4 = full2[:, 0:GH * SC].rearrange("p (h n) -> p h n", h=GH)

            def stick_softplus(g):
                for h in range(GH):
                    dve.wait_ge(s["z_ln"], GH * g + h + 1)
                    dve.scalar_tensor_tensor(sp4[:, h, :], tp[:, h, 0:SC], 0.0, ez[:, h, :], ALU.max, ALU.add)\
                        .then_inc(s["sp_raw"], 1)

            def heads_out(i, g, base, recips, sem):
                bank_ready(i)
                for t in range(TT):
                    dst = MX[:, t, base + g * T:base + (g + 1) * T]
                    ps = acc[:, i % NR, t * T:(t + 1) * T]
                    if recips is None:
                        ins = dve.tensor_copy(dst, ps)
                    else:
                        r = recips[:, 8 * t + g * GH:8 * t + g * GH + GH].rearrange("p (h d) -> p h d", d=1)
                        ins = dve.tensor_tensor(dst.rearrange("p (h d) -> p h d", h=GH),
                                                ps.rearrange("p (h d) -> p h d", h=GH),
                                                r.broadcast_to([P, GH, HD2]), ALU.mult)
                ins.then_inc(s[sem], 1)
                dve.wait_ge(s[sem], g + 1)

            splits_to(SPLIT["va"] + 1)
            dve.wait_ge(s["pt_hi"], 1)
            dve.tensor_tensor(plo[:, :, :], tp[:, 0, :].rearrange("p (k n) -> p k n", k=2), phi[:, :, :], ALU.subtract)\
                .then_inc(s["pt_lo"], 1)
            splits_to(SPLIT["va"] + 2)
            stick_softplus(0)
            splits_to(SPLIT["kb"] + 2)
            heads_out(ACC["stick0"], 0, 0, None, "stick_o")
            stick_softplus(1)
            splits_to(SPLIT["wout2"] + 2)
            heads_out(ACC["stick1"], 1, 0, None, "stick_o")
            bz = full2[:, 0:2 * SC].rearrange("p (b n) -> p b n", b=2)

            def band_bias(h):
                dve.wait_ge(s["b_ps"], h + 1)
                if h >= 2:
                    dve.wait_ge(s["b_exp"], h - 1)
                chain(dve.tensor_tensor(bz[:, h % 2, :], tp[:, h % 2, 0:SC], toe[:, h, :], ALU.add))
                for t, (lo, hi) in enumerate(((0, P), (P, SC))):
                    dve.tensor_reduce(bmax[:, 2 * h + t:2 * h + t + 1], bz[:, h % 2, lo:hi], AX, ALU.max,
                                      negate=True).then_inc(s["b_z"], 1)

            def group_norm(i):
                for t in range(TT):
                    at = MX[:, t, i * W2:(i + 1) * W2]
                    dve.tensor_tensor_reduce(full2[:, 1024:1024 + W2], at, at, 1.0, 0.0, ALU.mult, ALU.add,
                                             mss[:, 2 * i + t:2 * i + t + 1]).then_inc(s["mx_ss"], 1)
                    dve.wait_ge(s["mx_ss"], 2 * i + t + 1)

            def group_scale(i, sem):
                for t in range(TT):
                    dve.wait_ge(s["mx_ri"], 2 * i + t + 1)
                    at = MX[:, t, i * W2:(i + 1) * W2]
                    dve.tensor_scalar(at, at, mri[:, 2 * i + t:2 * i + t + 1], None, ALU.mult).then_inc(s[sem], 1)

            for h in range(H2):
                band_bias(h)
                if h % GH == GH - 1:
                    g = h // GH
                    dve.wait_ge(s["b_exp"], h + 1)
                    for t in range(TT):
                        r = slice(8 * t + g * GH, 8 * t + g * GH + GH)
                        ins = dve.reciprocal(brec[:, r], bsum[:, r])
                    chain(ins)
                if h == GH - 1:
                    group_norm(0)
                if h == GH + 1:
                    heads_out(ACC["band0"], 0, W2, brec, "band_o")
                if h == GH + 2:
                    group_scale(0, "mx_scaled")
            heads_out(ACC["band1"], 1, W2, brec, "band_o")
            group_norm(1)
            group_scale(1, "xn_ready")
            x_lo(5, vec("g_out_sb_2", 8), None, xhi, xlo)
            splits_to(SPLIT["wout2"] + 4)
            splits_to(SPLIT["up2"] + 2)
            for t in range(TT):
                post(1, "wout2", t, 1, 1.0)
                norm_tile(5, t, "f_x", TT + t + 1)
            x_lo(6, vec("g_ffn2_pre_2", 8), None, xhi, xlo)
            splits_to(SPLIT["up2"] + 4)
            ffn_up(2)
            splits_to(SPLIT["down2"] + 4)
            dve.wait_ge(s["chunk_used"], USED[SPLIT["proj"]][1])
            dve.wait_ge(s["h_lo"], 3 * NPAIR)
            for q in range(4):
                dve.tensor_copy(half(FULL, q), tp[:, q, :]).then_inc(s["pw_done"], 1)
            splits_to(SPLIT["gate"] + 2)
            for t in range(TT):
                post(2, "down2", t, 2, 0.5)
            dve.wait_ge(s["f_x"], 6)
            x_lo(7, None, None, xhi, xlo)
            splits_to(SPLIT["gate"] + 4)
            for j in range(2 * TT):
                dve.wait_ge(s["gate_s"], j + 1)
                dve.tensor_tensor(half(XN, j), half(XN, j), half(FULL, j), ALU.mult)\
                    .then_inc(s["e_y"], 1)
            dve.wait_ge(s["fgain"], 16 * 5)
            for t in range(TT):
                dve.wait_ge(s["f_ri"], TT * 3 + t + 1)
                chain(dve.scalar_tensor_tensor(XN[:, t, :], XN[:, t, :], fri[:, t:t + 1], bc[:, 1, :], ALU.mult,
                                               ALU.mult))
                dve.tensor_tensor(X[:, t, :], XN[:, t, :], X[:, t, :], ALU.add)\
                    .then_inc(s["out_x"], 1)


def constants():
    k = np.zeros((P, C_END), np.float32)
    k[:, C_ID:C_ID + P] = np.eye(P)
    k[:, C_TRI:C_TRI + P] = -np.tril(np.ones((P, P)))
    k[:, C_NEG:C_NEG + P] = -1.0
    k[:, C_AVG:C_AVG + P] = 1.0 / CD
    half_, grid = HD // 2, 64
    inv = (np.float32(10000.0) ** (-np.arange(0, half_, 2, dtype=np.float32) / np.float32(half_))).astype(np.float32)
    pos = np.arange(T)
    ang = np.concatenate([(pos // grid).astype(np.float32)[:, None] * inv,
                          (pos % grid).astype(np.float32)[:, None] * inv], axis=-1)
    for t in range(TT):
        at = ang[t * P:(t + 1) * P]
        k[:, C_COS + t * HD:C_COS + (t + 1) * HD] = np.repeat(np.cos(at), 2, axis=1)
        sin = np.repeat(np.sin(at), 2, axis=1)
        sin[:, 0::2] *= -1.0
        k[:, C_SIN + t * HD:C_SIN + (t + 1) * HD] = sin
    return k


SHAPES = {"x": (T, D), "ctx": (T, D), "c": (D,), "c_ctx": (D,), "w_mod": (D, 6 * D), "b_mod": (6 * D,),
          "norm1_g": (D,), "w_in": (D, 4608), "q_norm_g": (HD,), "k_norm_g": (HD,), "w_attn_out": (D, D),
          "conv_dw_w": (TAPS, CD), "conv_dw_b": (CD,), "conv_ln_g": (CD,), "conv_ln_b": (CD,),
          "w_conv_out": (CD, D), "w_out": (D, D), "norm2_g": (D,), "w_up": (D, 2 * F), "ffn_dw_w": (3, F),
          "ffn_dw_b": (F,), "w_down": (F, D), "final_g": (D,), "p_2": (T, 256), "g_ffn1_pre_2": (D,),
          "g_ffn1_post_2": (D,), "w_ffn1_gate_2": (D, F), "w_ffn1_up_2": (D, F), "w_ffn1_down_2": (F, D),
          "g_mix_pre_2": (D,), "g_mix_post_2": (D,), "w_in_2": (D, 6 * W2), "g_out_sb_2": (W2,),
          "g_out_ch_2": (W2,), "w_out_2": (D, D), "g_ffn2_pre_2": (D,), "g_ffn2_post_2": (D,),
          "w_ffn2_gate_2": (D, F), "w_ffn2_up_2": (D, F), "w_ffn2_down_2": (F, D), "w_ple_proj_2": (256, D),
          "w_ple_gate_2": (D, D), "g_ple_post_2": (D,)}


def kernel(**inputs):
    import concourse.bacc as bacc
    from concourse.bass_utils import run_bass_kernel_spmd

    nc = bacc.Bacc("TRN2", target_bir_lowering=False, num_devices=1)
    arrays = {name: np.ascontiguousarray(inputs[name]).reshape(shape) for name, shape in SHAPES.items()}
    rel = np.ascontiguousarray(inputs["rel_bias_2"])[0]
    arrays["bias"] = np.pad(rel[:, 1:], ((0, 0), (0, 2 * T - 2 * P + P - 1)), mode="edge")
    arrays["consts"] = constants()
    aps = {name: nc.dram_tensor(f"in_{name}", v.shape, mybir.dt.from_np(v.dtype), kind="ExternalInput").ap()
           for name, v in arrays.items()}
    aps["out"] = nc.dram_tensor("out_0", (T, D), F32, kind="ExternalOutput").ap()
    build(nc, aps)
    r = run_bass_kernel_spmd(nc, [{f"in_{name}": v for name, v in arrays.items()}], core_ids=[0])
    return r.results[0]["out_0"].reshape(1, T, D)
```
